# Optimizing a Trainium2 kernel written in Bass

```python
import jax, jax.numpy as jnp
from jax import lax
import numpy as np

D_MODEL = 1024
BATCH = 1
SEQ = 1024
DEPTH = 2

N_MIXERS = 2
N_ATTN_LAYERS = (DEPTH + 1) // 2
N_CONV_LAYERS = DEPTH // 2
N_HEADS = 8
QK_NOPE_DIM = 128
QK_ROPE_DIM = 64
QK_HEAD_DIM = QK_NOPE_DIM + QK_ROPE_DIM
V_HEAD_DIM = 128
Q_LORA_RANK = 256
KV_LORA_RANK = 128
DOWN_DIM = Q_LORA_RANK + KV_LORA_RANK + QK_ROPE_DIM
ROPE_THETA = 10000.0
Q_BLOCK = 128
CONV_WIDTH = 3
D_FF = 4 * D_MODEL
EPS = 1e-6
MAX_POS_OFFSET = 1024

kernel_name = 'hybrid_mla_shortconv_sqrelu'

def rms_norm(x, g):
    xf = x.astype(jnp.float32)
    xf = xf * lax.rsqrt(jnp.mean(xf * xf, axis=-1, keepdims=True) + EPS)
    return xf.astype(x.dtype) * g

def rope_tables(positions):
    inv_freq = ROPE_THETA ** (-jnp.arange(0, QK_ROPE_DIM, 2, dtype=jnp.float32) / QK_ROPE_DIM)
    ang = positions.astype(jnp.float32)[..., None] * inv_freq
    return jnp.cos(ang)[:, :, None, :], jnp.sin(ang)[:, :, None, :]

def apply_rope(x, cos, sin):
    x1, x2 = jnp.split(x, 2, axis=-1)
    cos = cos.astype(x.dtype)
    sin = sin.astype(x.dtype)
    return jnp.concatenate([x1 * cos - x2 * sin, x2 * cos + x1 * sin], axis=-1)

def mla_mixer(h, positions, cos, sin, w_down, g_q_a, g_kv_a, w_uq, w_ukv, g_qnorm, g_knorm, w_o):
    b, s, _ = h.shape
    a = h @ w_down
    c_q = rms_norm(a[..., :Q_LORA_RANK], g_q_a)
    c_kv = rms_norm(a[..., Q_LORA_RANK:Q_LORA_RANK + KV_LORA_RANK], g_kv_a)
    k_pe = a[..., Q_LORA_RANK + KV_LORA_RANK:]
    q = (c_q @ w_uq).reshape(b, s, N_HEADS, QK_HEAD_DIM)
    kv = (c_kv @ w_ukv).reshape(b, s, N_HEADS, QK_NOPE_DIM + V_HEAD_DIM)
    k_nope, v = kv[..., :QK_NOPE_DIM], kv[..., QK_NOPE_DIM:]
    k_pe = jnp.broadcast_to(k_pe[:, :, None, :], (b, s, N_HEADS, QK_ROPE_DIM))
    k = jnp.concatenate([k_nope, k_pe], axis=-1)
    q = rms_norm(q, g_qnorm)
    k = rms_norm(k, g_knorm)
    q = jnp.concatenate([q[..., :QK_NOPE_DIM], apply_rope(q[..., QK_NOPE_DIM:], cos, sin)], axis=-1)
    k = jnp.concatenate([k[..., :QK_NOPE_DIM], apply_rope(k[..., QK_NOPE_DIM:], cos, sin)], axis=-1)
    scale = QK_HEAD_DIM ** -0.5
    nb = s // Q_BLOCK
    q_blocks = q.reshape(b, nb, Q_BLOCK, N_HEADS, QK_HEAD_DIM).transpose(1, 0, 2, 3, 4)
    pos_blocks = positions.reshape(b, nb, Q_BLOCK).transpose(1, 0, 2)

    def attend(args):
        q_blk, pos_blk = args
        sc = jnp.einsum('bqhd,bkhd->bhqk', q_blk, k).astype(jnp.float32) * scale
        mask = pos_blk[:, None, :, None] >= positions[:, None, None, :]
        sc = jnp.where(mask, sc, jnp.finfo(jnp.float32).min)
        p = jax.nn.softmax(sc, axis=-1).astype(v.dtype)
        return jnp.einsum('bhqk,bkhd->bqhd', p, v)

    o = lax.map(attend, (q_blocks, pos_blocks))
    o = o.transpose(1, 0, 2, 3, 4).reshape(b, s, N_HEADS * V_HEAD_DIM)
    return o @ w_o

def short_conv_mixer(h, w_in, conv_w, w_out):
    bcu = h @ w_in
    gate_b, gate_c, u = jnp.split(bcu, 3, axis=-1)
    u = gate_c * u
    u = lax.conv_general_dilated(
        u, conv_w[:, None, :], window_strides=(1,), padding=((CONV_WIDTH - 1, 0),),
        dimension_numbers=('NWC', 'WIO', 'NWC'), feature_group_count=D_MODEL)
    return (gate_b * u) @ w_out

def sqrelu_mlp(h, w1, w2):
    return jnp.square(jax.nn.relu(h @ w1)) @ w2

def setup_inputs(seed: int = 0) -> dict:
    key = jax.random.key(seed)
    ks = jax.random.split(key, 20)
    nrm = lambda k, shape, fan_in: jax.random.normal(k, shape, jnp.float32) * fan_in ** -0.5
    gain = lambda k, shape: 1.0 + 0.02 * jax.random.normal(k, shape, jnp.float32)
    x = jax.random.normal(ks[0], (BATCH, SEQ, D_MODEL), jnp.float32)
    offset = jax.random.randint(ks[1], (BATCH, 1), 0, MAX_POS_OFFSET, dtype=jnp.int32)
    positions = offset + jnp.arange(SEQ, dtype=jnp.int32)[None, :]
    return {
        'x': x,
        'positions': positions,
        'g_mix': gain(ks[2], (DEPTH, D_MODEL)),
        'g_mlp': gain(ks[3], (DEPTH, D_MODEL)),
        'attn_w_down': nrm(ks[4], (N_ATTN_LAYERS, D_MODEL, DOWN_DIM), D_MODEL),
        'attn_g_q_a': gain(ks[5], (N_ATTN_LAYERS, Q_LORA_RANK)),
        'attn_g_kv_a': gain(ks[6], (N_ATTN_LAYERS, KV_LORA_RANK)),
        'attn_w_uq': nrm(ks[7], (N_ATTN_LAYERS, Q_LORA_RANK, N_HEADS * QK_HEAD_DIM), Q_LORA_RANK),
        'attn_w_ukv': nrm(ks[8], (N_ATTN_LAYERS, KV_LORA_RANK, N_HEADS * (QK_NOPE_DIM + V_HEAD_DIM)), KV_LORA_RANK),
        'attn_g_qnorm': gain(ks[9], (N_ATTN_LAYERS, QK_HEAD_DIM)),
        'attn_g_knorm': gain(ks[10], (N_ATTN_LAYERS, QK_HEAD_DIM)),
        'attn_w_o': nrm(ks[11], (N_ATTN_LAYERS, N_HEADS * V_HEAD_DIM, D_MODEL), N_HEADS * V_HEAD_DIM),
        'conv_w_in': nrm(ks[12], (N_CONV_LAYERS, D_MODEL, 3 * D_MODEL), D_MODEL),
        'conv_w': nrm(ks[13], (N_CONV_LAYERS, CONV_WIDTH, D_MODEL), CONV_WIDTH),
        'conv_w_out': nrm(ks[14], (N_CONV_LAYERS, D_MODEL, D_MODEL), D_MODEL),
        'mlp_w1': nrm(ks[15], (DEPTH, D_MODEL, D_FF), D_MODEL),
        'mlp_w2': nrm(ks[16], (DEPTH, D_FF, D_MODEL), D_FF),
    }

def reference(x, positions, g_mix, g_mlp, attn_w_down, attn_g_q_a, attn_g_kv_a, attn_w_uq,
              attn_w_ukv, attn_g_qnorm, attn_g_knorm, attn_w_o, conv_w_in, conv_w, conv_w_out,
              mlp_w1, mlp_w2):
    cos, sin = rope_tables(positions)
    for i in range(DEPTH):
        h = rms_norm(x, g_mix[i])
        j = i // N_MIXERS
        if i % N_MIXERS == 0:
            x = x + mla_mixer(h, positions, cos, sin, attn_w_down[j], attn_g_q_a[j], attn_g_kv_a[j],
                              attn_w_uq[j], attn_w_ukv[j], attn_g_qnorm[j], attn_g_knorm[j], attn_w_o[j])
        else:
            x = x + short_conv_mixer(h, conv_w_in[j], conv_w[j], conv_w_out[j])
        h = rms_norm(x, g_mlp[i])
        x = x + sqrelu_mlp(h, mlp_w1[i], mlp_w2[i])
    return x


_drawn_inputs = setup_inputs


def setup_inputs(seed=0):
    import zlib

    import numpy as np

    out = dict(_drawn_inputs(seed))
    spreads = {}
    factors = {'g_mix': 2.717,
     'attn_g_q_a': 8.0,
     'attn_g_kv_a': 8.0,
     'attn_g_qnorm': 8.0,
     'attn_g_knorm': 8.0,
     'g_mlp': 8.0}
    for name, (base, spread) in spreads.items():
        noise = np.random.default_rng([zlib.crc32(name.encode()), seed]).standard_normal(out[name].shape)
        drawn = base * np.exp(spread * noise) if base else spread * noise
        out[name] = __import__('jax').numpy.asarray(drawn.astype(out[name].dtype))
    for name, factor in factors.items():
        out[name] = (out[name] * factor).astype(out[name].dtype)
    return out
```

```python
import numpy as np

import concourse.bass as bass
from concourse import mybir

F32 = mybir.dt.float32
F32R = mybir.dt.float32r
BF16 = mybir.dt.bfloat16
I32 = mybir.dt.int32
ALU = mybir.AluOpType
ACT = mybir.ActivationFunctionType
AX = mybir.AxisListType

P = 128
S = 1024
D = 1024
NT = S // P
ND = D // P
H = 8
NOPE, ROPE, VD = 128, 64, 128
HALF = ROPE // 2
QK = NOPE + ROPE
CQ, CKV = 256, 128
DOWN = CQ + CKV + ROPE
NC = (CQ + CKV) // P
FF = 4 * D
EPS = 1e-6
N = 512
UNIT = 1024
RAW = 4
SCALE = float(QK) ** -0.5
FAR = 1.6e38
PROD_UNITS = 9
KB = 1024


def build(nc, ins, out):
    top = nc.sbuf_base + 31 & ~31
    place = {}

    def sb(name, shape, dtype, offset):
        place[name] = nc.alloc_sbuf_tensor_at(name, shape, dtype, offset=top + offset)
        return place[name]

    X0, DS0, US0, M0, SC0, G0 = 0, 32 * KB, 64 * KB, 80 * KB, 112 * KB, 120 * KB
    HT0 = G0 + 4 * KB + 128
    RAW0 = HT0 + 64 * KB
    SM0 = RAW0 + 16 * KB
    x = sb("x", [P, NT, D], F32, X0)
    d_hi = sb("d_hi", [P, 4, UNIT], F32R, DS0)
    d_lo = sb("d_lo", [P, 4, UNIT], F32R, DS0 + 16 * KB)
    u_hi = sb("u_hi", [P, 2, UNIT], F32R, US0)
    u_lo = sb("u_lo", [P, 2, UNIT], F32R, US0 + 8 * KB)
    m_hi = sb("m_hi", [P, 4, S], F32R, M0)
    m_lo = sb("m_lo", [P, 4, S], F32R, M0 + 16 * KB)
    scr = sb("scr", [P, 2, D], F32, SC0)
    gain = sb("gain", [P, D + 2], F32, G0)
    h_hi = sb("h_hi", [P, ND, S], F32R, HT0)
    h_lo = sb("h_lo", [P, ND, S], F32R, HT0 + 32 * KB)
    raw = sb("raw", [P, RAW, UNIT], F32, RAW0)
    ident = sb("ident", [P, P], F32, SM0)
    stat = sb("stat", [P, 96], F32, SM0 + 1024)
    convw = sb("convw", [P, 3, ND], F32, SM0 + 768)
    o_hi = sb("o_hi", [P, 4, UNIT], F32R, M0)
    o_lo = sb("o_lo", [P, 4, UNIT], F32R, M0 + 16 * KB)
    rq = sb("rq", [P, NT, 256], F32, X0)
    rk = sb("rk", [P, NT, 256], F32, X0 + 8 * KB)
    rv = sb("rv", [P, NT, VD], F32, X0 + 16 * KB)
    pr = sb("pr", [P, 2, S], F32, X0 + 20 * KB)
    osc = sb("osc", [P, N], F32, X0 + 28 * KB)
    rsb = sb("rsb", [P, N], F32, X0 + 30 * KB)
    q_hi = sb("q_hi", [P, S], F32R, DS0)
    q_lo = sb("q_lo", [P, S], F32R, DS0 + 4 * KB)
    q_rope = sb("q_rope", [P, S], F32R, DS0 + 8 * KB)
    k_hi = sb("k_hi", [P, S], F32R, DS0 + 12 * KB)
    k_lo = sb("k_lo", [P, S], F32R, DS0 + 16 * KB)
    kr_hi = sb("kr_hi", [P, S], F32R, DS0 + 20 * KB)
    kr_lo = sb("kr_lo", [P, S], F32R, DS0 + 24 * KB)
    pt_hi = sb("pt_hi", [P, NT, N], F32R, US0)
    pt_lo = sb("pt_lo", [P, NT, N], F32R, US0 + 16 * KB)
    v_hi = sb("v_hi", [P, NT, VD], F32R, US0 + 32 * KB)
    v_lo = sb("v_lo", [P, NT, VD], F32R, US0 + 36 * KB)
    mask = sb("mask", [P, NT, S], BF16, US0 + 40 * KB)
    xt = sb("xt", [P, D], F32, X0)
    xn = sb("xn", [P, D], F32, X0 + 8 * KB)
    posk_i = sb("posk_i", [P, S], I32, X0 + 12 * KB)
    posk = sb("posk", [P, S], F32, X0 + 16 * KB)
    cos = sb("cos", [P, NT, HALF], F32, X0 + 20 * KB)
    sin = sb("sin", [P, NT, HALF], F32, X0 + 21 * KB)
    ang = sb("ang", [P, NT, HALF], F32, X0 + 22 * KB)
    turn = sb("turn", [P, NT, HALF], F32, X0 + 23 * KB)
    g_c = sb("g_c", [P, CQ + CKV], F32, X0 + 24 * KB)
    g_q = sb("g_q", [P, QK], F32, X0 + 24 * KB + 1536)
    g_k = sb("g_k", [P, QK], F32, X0 + 24 * KB + 2304)
    freq = sb("freq", [P, HALF], F32, X0 + 24 * KB + 3072)
    posq_i = sb("posq_i", [P, NT], I32, X0 + 24 * KB + 3200)
    posq = sb("posq", [P, NT], F32, X0 + 24 * KB + 3264)
    c_sb = sb("c_sb", [P, DOWN], F32, X0 + 24 * KB + 3328)
    rotk = sb("rotk", [P, ROPE], F32, X0 + 24 * KB + 5120)
    tmp_r = sb("tmp_r", [P, ROPE], F32, X0 + 24 * KB + 5376)
    wd_hi = sb("wd_hi", [P, ND, DOWN], F32R, DS0)
    wd_lo = sb("wd_lo", [P, ND, DOWN], F32R, DS0 + 14 * KB)
    wq_hi = sb("wq_hi", [P, 2, H * QK], F32R, US0)
    wq_lo = sb("wq_lo", [P, 2, H * QK], F32R, US0 + 12 * KB)
    wk_hi = sb("wk_hi", [P, H * (NOPE + VD)], F32R, US0 + 24 * KB)
    wk_lo = sb("wk_lo", [P, H * (NOPE + VD)], F32R, US0 + 32 * KB)
    hx_hi = sb("hx_hi", [P, ND, P], F32R, HT0)
    hx_lo = sb("hx_lo", [P, ND, P], F32R, HT0 + 4 * KB)
    ct_hi = sb("ct_hi", [P, NC, P], F32R, HT0 + 8 * KB)
    ct_lo = sb("ct_lo", [P, NC, P], F32R, HT0 + 8 * KB + 1536)
    qs = sb("qs", [P, H, QK], F32, HT0 + 11 * KB)
    ks = sb("ks", [P, H, QK], F32, HT0 + 17 * KB)
    vs = sb("vs", [P, H, VD], F32, HT0 + 23 * KB)
    q_sq = sb("q_sq", [P, H, QK], F32, HT0 + 27 * KB)
    k_sq = sb("k_sq", [P, H, NOPE], F32, HT0 + 33 * KB)
    junk = sb("junk", [P, D], F32, HT0 + 37 * KB)
    ra = sb("ra", [P, H, HALF], F32, HT0 + 41 * KB)
    rb = sb("rb", [P, H, HALF], F32, HT0 + 42 * KB)
    rc = sb("rc", [P, H, HALF], F32, HT0 + 43 * KB)
    rd = sb("rd", [P, H, HALF], F32, HT0 + 44 * KB)

    psum = nc.alloc_psum_tensor("psum", [P, 8 * N], F32)
    qd = nc.dram_tensor("q_heads", [S, H, QK], F32, kind="Internal").ap()
    kd = nc.dram_tensor("k_heads", [S, H, QK], F32, kind="Internal").ap()
    vd = nc.dram_tensor("v_heads", [S, H, VD], F32, kind="Internal").ap()

    def bank(b, n=1):
        return psum[:, b * N:(b + n) * N]

    def f32(ap):
        return ap.bitcast(F32)


    def sem(name):
        return nc.alloc_semaphore(name)

    def wait(e, s, value):
        if not isinstance(value, int) or value > 0:
            e.wait_ge(s, value)

    def linker(e, s, base):
        count = [0]

        def link(ins):
            count[0] += 1
            ins.then_inc(s, 1)
            e.wait_ge(s, base + count[0])
        return link, count

    def passes(pe, dst, terms):
        for n, (s_hi, s_lo, m_hi_, m_lo_) in enumerate(terms):
            pe.matmul(dst, s_hi, m_hi_, start=n == 0, stop=False)
            pe.matmul(dst, s_hi, m_lo_, start=False, stop=False)
            last = pe.matmul(dst, s_lo, m_hi_, start=False, stop=n == len(terms) - 1)
        return last

    x_rows = ins["x"].rearrange("a (t p) d -> p (a t) d", p=P)
    out_rows = out.rearrange("a (t p) d -> p (a t) d", p=P)

    def spread(src):
        return bass.AP(tensor=src.tensor, offset=src.offset, ap=[[0, P], [1, src.shape[0]]])

    def heads(ap, n):
        return ap.unsqueeze(2).to_broadcast([P, H, n])

    def all_heads(ap, n):
        return ap.unsqueeze(1).to_broadcast([P, H, n])

    raw_in = [sem(f"raw_in{i}") for i in range(RAW)]
    w_hi_done, w_lo_done = sem("w_hi_done"), sem("w_lo_done")
    O_BASE = PROD_UNITS
    M1_BASE = O_BASE + 8 + 2
    C_BASE = M1_BASE + 8 * (FF // N)
    M2_BASE = C_BASE + 16 * 2

    def like(slot, ap):
        shape = list(ap.shape)
        v = raw[:, slot, 0:shape[1] * (shape[2] if len(shape) == 3 else 1)]
        return v.rearrange("p (a b) -> p a b", a=shape[1]) if len(shape) == 3 else v

    def load_unit(sp, s, more, src):
        wait(sp, w_lo_done, s + more - RAW + 1)
        sp.dma_start(like(s % RAW, src), src).then_inc(raw_in[s % RAW], 16)

    def split_hi(act, s, more, dst):
        act.wait_ge(raw_in[s % RAW], 16 * (s // RAW + 1) + more * (16 // RAW))
        act.activation(dst, like(s % RAW, dst), ACT.Copy).then_inc(w_hi_done, 1)

    def split_lo(dve, s, more, dst, hi):
        dve.wait_ge(w_hi_done, s + more + 1)
        dve.tensor_tensor(dst, like(s % RAW, dst), f32(hi), ALU.subtract).then_inc(w_lo_done, 1)

    def dve_rstd(dve, link, dst, mean, root, tmp):
        link(dve.reciprocal(dst, root))
        link(dve.tensor_tensor(tmp, dst, dst, ALU.mult))
        link(dve.scalar_tensor_tensor(tmp, mean, EPS, tmp, ALU.add, ALU.mult))
        link(dve.tensor_scalar(tmp, tmp, -0.5, 1.5, ALU.mult, ALU.add))
        link(dve.tensor_tensor(dst, dst, tmp, ALU.mult))

    def cols(a, n=1):
        return stat[:, a:a + n]

    MS_X, ROOT_X, R_X, MS_C, MS_KR, ROOT_C, R_C, TMP = 0, 1, 2, 3, 5, 6, 8, 10
    MS_Q, ROOT_Q, R_Q, SS_K, MS_K, ROOT_K, R_K = 18, 26, 34, 42, 50, 58, 66
    MS_N, ROOT_N, R_N, TMP_N, EPS_C = 80, 82, 84, 85, 86

    consts = sem("consts")
    pos_in = sem("pos_in")
    a_x_in, a_ss, a_xn = sem("a_x_in"), sem("a_ss"), sem("a_xn")
    a_turned, a_hx_hi, a_hx_lo = sem("a_turned"), sem("a_hx_hi"), sem("a_hx_lo")
    a_latent, a_latent_ss, a_c = sem("a_latent"), sem("a_latent_ss"), sem("a_c")
    a_c_turned, a_ct_hi, a_ct_lo = sem("a_c_turned"), sem("a_ct_hi"), sem("a_ct_lo")
    a_q, a_q_out, a_kv, a_kv_out = sem("a_q"), sem("a_q_out"), sem("a_kv"), sem("a_kv_out")
    a_q_sq, a_k_sq, a_q_norm, a_k_norm = sem("a_q_sq"), sem("a_k_sq"), sem("a_q_norm"), sem("a_k_norm")
    a_q_rot, a_k_rot, a_stored_q, a_stored_k, a_stored_v = (
        sem("a_q_rot"), sem("a_k_rot"), sem("a_stored_q"), sem("a_stored_k"), sem("a_stored_v"))
    a_k_copied, a_mask, a_rope = sem("a_k_copied"), sem("a_mask"), sem("a_rope")
    a_own, a_pool_own, ident_done = sem("a_own"), sem("a_pool_own"), sem("ident_done")
    a_root, a_summed, eps_set = sem("a_root"), sem("a_summed"), sem("eps_set")
    setup_own, ang_done = sem("setup_own"), sem("ang_done")
    CONSTS = 16 * 8
    KV_BANK = [7, 4, 5, 6]

    w_down = ins["attn_w_down"][0, :, :].rearrange("(k p) n -> p k n", p=P)
    w_uq = ins["attn_w_uq"][0, :, :].rearrange("(k p) n -> p k n", p=P)
    w_ukv = ins["attn_w_ukv"][0, :, :]

    def piece(s, down, uq, ukv):
        if s < 4:
            return down[:, 2 * s:2 * s + 2, :]
        if s < 7:
            return uq[:, :, N * (s - 4):N * (s - 3)]
        return ukv[:, UNIT * (s - 7):UNIT * (s - 6)]

    def a_store(ap, t):
        return ap[bass.ds(t * P, P), :, :]

    def sp_produce_setup(sp):
        sp.dma_start(xt[:, :], x_rows[:, 0, :]).then_inc(a_x_in, 16)
        sp.dma_start(gain[:, 0:D], spread(ins["g_mix"][0, :])).then_inc(consts, 16)
        for s in range(RAW):
            load_unit(sp, s, 0, piece(s, w_down, w_uq, w_ukv))
        sp.dma_start(posk_i[:, :], spread(ins["positions"][0, :])).then_inc(pos_in, 16)
        sp.dma_start(freq[:, :], spread(ins["inv_freq"])).then_inc(pos_in, 16)
        sp.dma_start(g_c[:, 0:CQ], spread(ins["attn_g_q_a"][0, :])).then_inc(consts, 16)
        sp.dma_start(g_c[:, CQ:], spread(ins["attn_g_kv_a"][0, :])).then_inc(consts, 16)
        sp.dma_start(g_q[:, :], spread(ins["attn_g_qnorm"][0, :])).then_inc(consts, 16)
        sp.dma_start(g_k[:, :], spread(ins["attn_g_knorm"][0, :])).then_inc(consts, 16)
        with nc.allow_non_contiguous_dma("one position or tap per partition"):
            sp.dma_start(posq_i[:, :], ins["positions"].rearrange("a (t p) -> p (a t)", p=P)).then_inc(pos_in, 16)
            for w in range(3):
                sp.dma_start(convw[:, w, :], ins["conv_w"][0, w, :].rearrange("(k p) -> p k", p=P)).then_inc(consts, 16)
        for s in range(RAW, PROD_UNITS):
            load_unit(sp, s, 0, piece(s, w_down, w_uq, w_ukv))

    def sp_produce(sp, t, last):
        if not last:
            sp.wait_ge(a_xn, t + 1)
            sp.dma_start(xt[:, :], x_rows[:, bass.ds(t + 1, 1), :].rearrange("p a d -> p (a d)")).then_inc(a_x_in, 16)
        sp.wait_ge(a_kv_out, 4 * t + 4)
        sp.dma_start(a_store(vd, t), vs[:, :, :]).then_inc(a_stored_v, 16)
        sp.wait_ge(a_q_rot, t + 1)
        sp.dma_start(a_store(qd, t), qs[:, :, :]).then_inc(a_stored_q, 16)
        sp.wait_ge(a_k_rot, t + 1)
        sp.dma_start(a_store(kd, t), ks[:, :, :]).then_inc(a_stored_k, 16)

    def pe_produce(pe, t):
        pe.wait_ge(a_xn, t + 1)
        for b in range(2):
            for k in range(4):
                last = pe.transpose(psum[:, b * N + k * P:b * N + (k + 1) * P],
                                    xn[:, (4 * b + k) * P:(4 * b + k + 1) * P], ident[:, :])
            last.then_inc(a_turned, 1)
        pe.wait_ge(a_hx_lo, 2 * t + 2)
        pe.wait_ge(w_lo_done, 4)
        passes(pe, psum[:, 2 * N:2 * N + DOWN],
               [(hx_hi[:, k, :], hx_lo[:, k, :], wd_hi[:, k, :], wd_lo[:, k, :]) for k in range(ND)]
               ).then_inc(a_latent, 1)
        pe.wait_ge(a_c, t + 1)
        for k in range(NC):
            last = pe.transpose(psum[:, 3 * N + k * P:3 * N + (k + 1) * P], c_sb[:, k * P:(k + 1) * P], ident[:, :])
        last.then_inc(a_c_turned, 1)
        pe.wait_ge(a_ct_lo, t + 1)
        pe.wait_ge(w_lo_done, PROD_UNITS)
        for b in range(3):
            if b == 1:
                wait(pe, a_kv_out, 4 * t)
            passes(pe, bank(4 + b), [(ct_hi[:, k, :], ct_lo[:, k, :], wq_hi[:, k, b * N:(b + 1) * N],
                                      wq_lo[:, k, b * N:(b + 1) * N]) for k in range(2)]).then_inc(a_q, 1)
        for b in range(4):
            if b:
                pe.wait_ge(a_q_out, 3 * t + b)
            passes(pe, bank(KV_BANK[b]), [(ct_hi[:, 2, :], ct_lo[:, 2, :], wk_hi[:, b * N:(b + 1) * N],
                                           wk_lo[:, b * N:(b + 1) * N])]).then_inc(a_kv, 1)

    def act_produce_setup(act):
        act.wait_ge(ang_done, 1)
        act.activation(sin[:, :, :], ang[:, :, :], ACT.Sin).then_inc(a_rope, 1)
        act.wait_ge(ang_done, 2)
        act.activation(cos[:, :, :], turn[:, :, :], ACT.Sin).then_inc(a_rope, 1)

    def act_produce_weights(act, units):
        for s in units:
            split_hi(act, s, 0, piece(s, wd_hi, wq_hi, wk_hi))

    def act_produce(act, t):
        act.wait_ge(a_x_in, 16 * t + 16)
        act.activation(junk[:, :], xt[:, :], ACT.Square, scale=float(D) ** -0.5,
                       accum_out=cols(MS_X)).then_inc(a_ss, 1)
        act.wait_ge(a_ss, t + 1)
        if isinstance(t, int):
            act.wait_ge(eps_set, 1)
        act.activation(cols(ROOT_X), cols(MS_X), ACT.Sqrt, bias=cols(EPS_C)).then_inc(a_root, 1)
        if isinstance(t, int):
            act_produce_weights(act, range(0, 4))
        for b in range(2):
            act.wait_ge(a_turned, 2 * t + b + 1)
            act.activation(hx_hi[:, 4 * b:4 * b + 4, :], bank(b).rearrange("p (k q) -> p k q", k=4),
                           ACT.Copy).then_inc(a_hx_hi, 1)
        if isinstance(t, int):
            act_produce_weights(act, range(4, 9))
            act_produce_setup(act)
        act.wait_ge(a_latent, t + 1)
        for i, (a, b, n) in enumerate(((0, CQ, CQ), (CQ, CQ + CKV, CKV), (CQ + CKV, DOWN, QK))):
            act.activation(junk[:, a:b], psum[:, 2 * N + a:2 * N + b], ACT.Square, scale=float(n) ** -0.5,
                           accum_out=cols(MS_C + i)).then_inc(a_latent_ss, 1)
        act.wait_ge(a_latent_ss, 3 * t + 3)
        act.activation(cols(ROOT_C, 2), cols(MS_C, 2), ACT.Sqrt, bias=cols(EPS_C)).then_inc(a_root, 1)
        act.wait_ge(a_c_turned, t + 1)
        act.activation(ct_hi[:, :, :], psum[:, 3 * N:3 * N + NC * P].rearrange("p (k q) -> p k q", k=NC),
                       ACT.Copy).then_inc(a_ct_hi, 1)
        wait(act, a_stored_q, 16 * t)
        flat = qs[:, :, :].rearrange("p h n -> p (h n)")
        for b in range(3):
            act.wait_ge(a_q, 3 * t + b + 1)
            act.activation(flat[:, b * N:(b + 1) * N], bank(4 + b), ACT.Copy).then_inc(a_q_out, 1)
        act.wait_ge(a_q_out, 3 * t + 3)
        act.activation(q_sq[:, :, :], qs[:, :, :], ACT.Square, scale=float(QK) ** -0.5).then_inc(a_q_sq, 1)
        wait(act, a_stored_k, 16 * t)
        wait(act, a_stored_v, 16 * t)
        for b in range(4):
            act.wait_ge(a_kv, 4 * t + b + 1)
            src = bank(KV_BANK[b]).rearrange("p (h n) -> p h n", h=2)
            act.activation(ks[:, 2 * b:2 * b + 2, 0:NOPE], src[:, :, 0:NOPE], ACT.Copy).then_inc(a_k_copied, 1)
            act.activation(vs[:, 2 * b:2 * b + 2, :], src[:, :, NOPE:], ACT.Copy).then_inc(a_kv_out, 1)
        act.wait_ge(a_k_copied, 4 * t + 4)
        act.activation(k_sq[:, :, :], ks[:, :, 0:NOPE], ACT.Square, scale=float(QK) ** -0.5).then_inc(a_k_sq, 1)
        act.wait_ge(a_summed, 2 * t + 1)
        act.activation(cols(ROOT_Q, H), cols(MS_Q, H), ACT.Sqrt, bias=cols(EPS_C)).then_inc(a_root, 1)
        act.wait_ge(a_summed, 2 * t + 2)
        act.activation(cols(ROOT_K, H), cols(MS_K, H), ACT.Sqrt, bias=cols(EPS_C)).then_inc(a_root, 1)

    TWO_PI = 2.0 * np.pi
    PI_HI = 6.28125
    PI_MID = float(np.float32(TWO_PI - PI_HI))
    PI_LO = float(np.float32(TWO_PI - PI_HI - PI_MID))
    ROUND = 1.5 * 2.0 ** 23

    def dve_produce_setup(dve):
        link, _ = linker(dve, setup_own, 0)
        dve.wait_ge(pos_in, 48)
        link(dve.tensor_copy(posq[:, :], posq_i[:, :]))
        link(dve.tensor_copy(posk[:, :], posk_i[:, :]))
        raw_ang = ra[:, :, :]
        link(dve.tensor_tensor(raw_ang, posq[:, :].unsqueeze(2).to_broadcast([P, NT, HALF]),
                               freq[:, :].unsqueeze(1).to_broadcast([P, NT, HALF]), ALU.mult))
        for dst, quarter in ((ang, 0.0), (turn, 0.25)):
            n = rb[:, :, :]
            link(dve.tensor_scalar(n, raw_ang, 1.0 / TWO_PI, quarter, ALU.mult, ALU.add))
            link(dve.tensor_scalar(n, n, ROUND, None, ALU.add))
            link(dve.tensor_scalar(n, n, ROUND, None, ALU.subtract))
            link(dve.scalar_tensor_tensor(dst[:, :, :], n, -PI_HI, raw_ang, ALU.mult, ALU.add))
            link(dve.scalar_tensor_tensor(dst[:, :, :], n, -PI_MID, dst[:, :, :], ALU.mult, ALU.add))
            link(dve.scalar_tensor_tensor(dst[:, :, :], n, -PI_LO, dst[:, :, :], ALU.mult, ALU.add))
            if quarter:
                link(dve.tensor_scalar(dst[:, :, :], dst[:, :, :], float(np.float32(np.pi / 2)), None, ALU.add))
            dve.tensor_scalar(dst[:, :, :], dst[:, :, :], PI32, -PI32, ALU.min, ALU.max).then_inc(ang_done, 1)

    PI32 = float(np.nextafter(np.float32(np.pi), np.float32(0)))

    def dve_produce_weights(dve, units):
        for s in units:
            split_lo(dve, s, 0, piece(s, wd_lo, wq_lo, wk_lo), piece(s, wd_hi, wq_hi, wk_hi))

    A_OWN = 29

    def at(ap, t):
        return ap[:, bass.ds(t, 1), :].rearrange("p a n -> p (a n)")

    def dve_produce(dve, t):
        link, count = linker(dve, a_own, A_OWN * t)
        dve.wait_ge(a_root, 4 * t + 1)
        dve_rstd(dve, link, cols(R_X), cols(MS_X), cols(ROOT_X), cols(TMP))
        if isinstance(t, int):
            dve.wait_ge(consts, CONSTS)
        dve.scalar_tensor_tensor(xn[:, :], xt[:, :], cols(R_X), gain[:, 0:D], ALU.mult, ALU.mult).then_inc(a_xn, 1)
        if isinstance(t, int):
            dve_produce_weights(dve, range(0, 4))
        for b in range(2):
            dve.wait_ge(a_hx_hi, 2 * t + b + 1)
            dve.tensor_tensor(hx_lo[:, 4 * b:4 * b + 4, :], bank(b).rearrange("p (k q) -> p k q", k=4),
                              f32(hx_hi[:, 4 * b:4 * b + 4, :]), ALU.subtract).then_inc(a_hx_lo, 1)
        if isinstance(t, int):
            dve_produce_setup(dve)
            dve_produce_weights(dve, range(4, 9))
        dve.wait_ge(a_root, 4 * t + 2)
        dve_rstd(dve, link, cols(R_C, 2), cols(MS_C, 2), cols(ROOT_C, 2), cols(TMP, 2))
        lat = psum[:, 2 * N:2 * N + DOWN]
        link(dve.tensor_tensor(c_sb[:, CQ + CKV:], lat[:, CQ + CKV:], g_k[:, NOPE:], ALU.mult))
        dve.scalar_tensor_tensor(c_sb[:, 0:CQ], lat[:, 0:CQ], cols(R_C), g_c[:, 0:CQ], ALU.mult, ALU.mult)
        dve.scalar_tensor_tensor(c_sb[:, CQ:CQ + CKV], lat[:, CQ:CQ + CKV], cols(R_C + 1), g_c[:, CQ:],
                                 ALU.mult, ALU.mult).then_inc(a_c, 1)
        dve.wait_ge(a_ct_hi, t + 1)
        dve.tensor_tensor(ct_lo[:, :, :], psum[:, 3 * N:3 * N + NC * P].rearrange("p (k q) -> p k q", k=NC),
                          f32(ct_hi[:, :, :]), ALU.subtract).then_inc(a_ct_lo, 1)
        first, second = c_sb[:, CQ + CKV:CQ + CKV + HALF], c_sb[:, CQ + CKV + HALF:]
        if isinstance(t, int):
            dve.wait_ge(a_rope, 2)
        link(dve.tensor_tensor(tmp_r[:, 0:HALF], second, at(sin, t), ALU.mult))
        link(dve.tensor_tensor(tmp_r[:, HALF:], first, at(sin, t), ALU.mult))
        link(dve.tensor_tensor(rotk[:, 0:HALF], first, at(cos, t), ALU.mult))
        link(dve.tensor_tensor(rotk[:, HALF:], second, at(cos, t), ALU.mult))
        link(dve.tensor_tensor(rotk[:, 0:HALF], rotk[:, 0:HALF], tmp_r[:, 0:HALF], ALU.subtract))
        link(dve.tensor_tensor(rotk[:, HALF:], rotk[:, HALF:], tmp_r[:, HALF:], ALU.add))
        dve.tensor_scalar(at(mask, t), posk[:, :], posq[:, bass.ds(t, 1)], -FAR, ALU.is_gt, ALU.mult).then_inc(a_mask, 1)
        dve.wait_ge(a_q_sq, t + 1)
        dve.reduce_sum(cols(MS_Q, H), q_sq[:, :, :], AX.X).then_inc(a_summed, 1)
        dve.wait_ge(a_k_sq, t + 1)
        link(dve.reduce_sum(cols(SS_K, H), k_sq[:, :, :], AX.X))
        dve.tensor_scalar(cols(MS_K, H), cols(SS_K, H), cols(MS_KR), None, ALU.add).then_inc(a_summed, 1)
        dve.wait_ge(a_root, 4 * t + 3)
        dve_rstd(dve, link, cols(R_Q, H), cols(MS_Q, H), cols(ROOT_Q, H), cols(TMP, H))
        dve.tensor_tensor(qs[:, :, :], qs[:, :, :], heads(cols(R_Q, H), QK), ALU.mult).then_inc(a_q_norm, 1)
        dve.wait_ge(a_root, 4 * t + 4)
        dve_rstd(dve, link, cols(R_K, H), cols(MS_K, H), cols(ROOT_K, H), cols(TMP, H))
        link(dve.tensor_tensor(ks[:, :, NOPE:], all_heads(rotk[:, :], ROPE), heads(cols(R_K, H), ROPE), ALU.mult))
        dve.tensor_tensor(ks[:, :, 0:NOPE], ks[:, :, 0:NOPE], heads(cols(R_K, H), NOPE), ALU.mult).then_inc(a_k_norm, 1)
        return count[0]

    def pool_setup(pool):
        pool.memset(ident[:, :], 0.0).then_inc(ident_done, 1)
        pool.wait_ge(ident_done, 1)
        pool.affine_select(out=ident[:, :], in_=ident[:, :], compare_op=ALU.not_equal, fill=1.0, base=0,
                           pattern=[[-1, P]], channel_multiplier=1).then_inc(ident_done, 1)
        pool.memset(cols(EPS_C), EPS).then_inc(eps_set, 1)
        for i, (s, n) in enumerate(((u_free, 4), (d_free, 4), (square_done, 2))):
            pool.memset(cols(88 + i), 0.0).then_inc(s, n)

    POOL_OWN = 3

    def pool_produce(pool, t):
        link, count = linker(pool, a_pool_own, POOL_OWN * t)
        pool.wait_ge(a_q_norm, t + 1)
        pool.wait_ge(consts, CONSTS)
        link(pool.tensor_tensor(qs[:, :, :], qs[:, :, :], all_heads(g_q[:, :], QK), ALU.mult))
        pool.wait_ge(a_rope, 2)
        first, second = qs[:, :, NOPE:NOPE + HALF], qs[:, :, NOPE + HALF:]
        co, si = all_heads(at(cos, t), HALF), all_heads(at(sin, t), HALF)
        pool.tensor_tensor(ra[:, :, :], first, co, ALU.mult)
        pool.tensor_tensor(rb[:, :, :], second, si, ALU.mult)
        pool.tensor_tensor(rc[:, :, :], second, co, ALU.mult)
        link(pool.tensor_tensor(rd[:, :, :], first, si, ALU.mult))
        link(pool.tensor_tensor(first, ra[:, :, :], rb[:, :, :], ALU.subtract))
        pool.tensor_tensor(second, rc[:, :, :], rd[:, :, :], ALU.add).then_inc(a_q_rot, 1)
        pool.wait_ge(a_k_norm, t + 1)
        pool.tensor_tensor(ks[:, :, 0:NOPE], ks[:, :, 0:NOPE], all_heads(g_k[:, 0:NOPE], NOPE), ALU.mult).then_inc(a_k_rot, 1)
        return count[0]

    q_in, v_in = sem("q_in"), sem("v_in")
    s_done, s_max, e_done = sem("s_done"), sem("s_max"), sem("e_done")
    t_done, t_hi, t_free = sem("t_done"), sem("t_hi"), sem("t_free")
    vh_done, vl_done = sem("vh_done"), sem("vl_done")
    r_inv, r_turned, r_copied = sem("r_inv"), sem("r_turned"), sem("r_copied")
    pv_done, o_norm, oh_done, ol_done = sem("pv_done"), sem("o_norm"), sem("oh_done"), sem("ol_done")
    b_own = sem("b_own")
    PREP = 8
    T_HEAD = 24
    TG = {0: 0, 1: 2, 2: 4, 3: 6, "Q0": 8, 4: 10, 5: 12, "K": 14, 6: 18, "Q1": 20, 7: 22}
    TG_LAST = {0: 0, 1: 2, 2: 4, 3: 6, 4: 8, 5: 10, 6: 12, 7: 14}

    def sp_head_qk(sp, h):
        for dst, src in ((rq, qd), (rk, kd)):
            rows = src[:, bass.ds(h, 1), :].rearrange("(t p) a n -> p t (a n)", p=P)
            sp.dma_start(dst[:, :, 0:QK], rows).then_inc(q_in, 16)
            sp.dma_start(dst[:, :, QK:], rows[:, :, NOPE:]).then_inc(q_in, 16)

    def sp_head_v(sp, h):
        sp.dma_start(rv[:, :, :], vd[:, bass.ds(h, 1), :].rearrange("(t p) a n -> p t (a n)", p=P)).then_inc(v_in, 16)

    def sp_attention(sp):
        for s in (a_stored_q, a_stored_k, a_stored_v):
            sp.wait_ge(s, 16 * NT)
        sp.wait_ge(a_mask, NT)
        sp_head_qk(sp, 0)
        sp_head_v(sp, 0)
        for j in range(RAW):
            load_unit(sp, O_BASE + j, 0, o_unit(j))
        with sp.Fori(1, H) as h:
            sp.wait_ge(t_done, (h - 1) * T_HEAD + PREP)
            sp_head_qk(sp, h)
            sp.wait_ge(vl_done, h)
            sp_head_v(sp, h)

    def blocks(group, j):
        if group == "K":
            a, b = (0, NOPE) if j < 2 else (NOPE, 256)
            return [rk[:, 4 * (j % 2) + i, a:b] for i in range(4)]
        if group in ("Q0", "Q1"):
            half = int(group[1])
            a, b = (0, NOPE) if j == 0 else (NOPE, 256)
            return [rq[:, 4 * half + i, a:b] for i in range(4)]
        return [pr[:, group % 2, (4 * j + i) * P:(4 * j + i + 1) * P] for i in range(4)]

    def dests(group, j):
        if group == "K":
            c = slice(N * (j % 2), N * (j % 2) + N)
            return (k_hi[:, c], k_lo[:, c]) if j < 2 else (kr_hi[:, c], kr_lo[:, c])
        if group in ("Q0", "Q1"):
            c = slice(N * int(group[1]), N * int(group[1]) + N)
            return (q_hi[:, c], q_lo[:, c]) if j == 0 else (q_rope[:, c], None)
        c = slice(P * (group % 4), P * (group % 4) + P)
        return pt_hi[:, 4 * j:4 * j + 4, c], pt_lo[:, 4 * j:4 * j + 4, c]

    def groups_of(group):
        return 4 if group == "K" else 2

    def t_view(b, dst):
        return bank(b).rearrange("p (k q) -> p k q", k=4) if len(dst.shape) == 3 else bank(b)

    def pe_turn(pe, group, first):
        for j in range(groups_of(group)):
            wait(pe, t_free, first + j - 1)
            for i, src in enumerate(blocks(group, j)):
                last = pe.transpose(psum[:, (4 + j % 2) * N + i * P:(4 + j % 2) * N + (i + 1) * P], src, ident[:, :])
            last.then_inc(t_done, 1)

    def act_turned(act, group, first):
        for j in range(groups_of(group)):
            hi, _ = dests(group, j)
            act.wait_ge(t_done, first + j + 1)
            act.activation(hi, t_view(4 + j % 2, hi), ACT.Copy).then_inc(t_hi, 1)

    def dve_turned(dve, group, first):
        for j in range(groups_of(group)):
            hi, lo = dests(group, j)
            dve.wait_ge(t_hi, first + j + 1)
            if lo is None:
                rows = slice(ROPE, P)
                dve.tensor_tensor(hi[rows, :], bank(4 + j % 2)[rows, :], f32(hi[rows, :]), ALU.subtract).then_inc(t_free, 1)
            else:
                dve.tensor_tensor(lo, t_view(4 + j % 2, hi), f32(hi), ALU.subtract).then_inc(t_free, 1)

    def pe_scores(pe, j, ready):
        if ready is not None:
            pe.wait_ge(t_free, ready)
        c = slice(P * j, P * j + P)
        for half in range(2):
            m = slice(N * half, N * half + N)
            dst = bank(2 * (j % 2) + half)
            pe.matmul(dst, q_hi[:, c], k_hi[:, m], start=True, stop=False)
            pe.matmul(dst, q_hi[:, c], k_lo[:, m], start=False, stop=False)
            pe.matmul(dst, q_lo[:, c], k_hi[:, m], start=False, stop=False)
            pe.matmul(dst, q_rope[:, c], kr_hi[:, m], start=False, stop=False)
            last = pe.matmul(dst, q_rope[:, c], kr_lo[:, m], start=False, stop=True)
        last.then_inc(s_done, 1)

    def pe_values(pe, h, half, ready):
        r = 2 * h + half
        pe.wait_ge(r_inv, r + 1)
        for i in range(4):
            last = pe.transpose(psum[:, 7 * N + i * P:7 * N + (i + 1) * P],
                                stat[:, 32 + 4 * half + i:33 + 4 * half + i].to_broadcast([P, P]), ident[:, :])
        last.then_inc(r_turned, 1)
        pe.wait_ge(t_free, ready)
        if half == 0:
            pe.wait_ge(vl_done, h + 1)
        else:
            pe.wait_ge(o_norm, r)
        passes(pe, bank(6), [(v_hi[:, k, :], v_lo[:, k, :], pt_hi[:, k, :], pt_lo[:, k, :])
                             for k in range(NT)]).then_inc(pv_done, 1)

    def pe_attention_head(pe, h, last):
        t0, tg = PREP + T_HEAD * h, TG_LAST if last else TG
        for j in range(1, NT):
            if j >= 2:
                pe.wait_ge(s_max, NT * h + j - 1)
            pe_scores(pe, j, t0 if j == 4 else None)
            if j == 6:
                pe_values(pe, h, 0, t0 + tg[3] + 2)
            if j >= 2:
                pe.wait_ge(e_done, NT * h + j - 1)
                pe_turn(pe, j - 2, t0 + tg[j - 2])
            if j == 5 and not last:
                pe.wait_ge(q_in, 64 * h + 128)
                pe_turn(pe, "Q0", t0 + tg["Q0"])
        if not last:
            pe_turn(pe, "K", t0 + tg["K"])
        pe.wait_ge(e_done, NT * h + 7)
        pe_turn(pe, 6, t0 + tg[6])
        if not last:
            pe_turn(pe, "Q1", t0 + tg["Q1"])
        pe.wait_ge(e_done, NT * h + 8)
        pe_turn(pe, 7, t0 + tg[7])
        if not last:
            pe_scores(pe, 0, t0 + tg["K"] + 4)
        pe_values(pe, h, 1, t0 + tg[7] + 2)

    def pe_attention(pe):
        pe.wait_ge(a_kv_out, 4 * NT)
        pe.wait_ge(q_in, 64)
        pe_turn(pe, "K", 0)
        pe_turn(pe, "Q0", 4)
        pe_turn(pe, "Q1", 6)
        pe_scores(pe, 0, PREP)
        with pe.Fori(0, H - 1) as h:
            pe_attention_head(pe, h, False)
        pe_attention_head(pe, H - 1, True)

    def act_exp(act, h, j):
        act.wait_ge(s_max, NT * h + j + 1)
        act.activation(pr[:, j % 2, :], pr[:, j % 2, :], ACT.Exp, bias=stat[:, 8 + j:9 + j], scale=SCALE,
                       accum_out=stat[:, 16 + j:17 + j]).then_inc(e_done, 1)

    def act_out(act, h, half):
        r = 2 * h + half
        act.wait_ge(o_norm, r + 1)
        act.activation(h_hi[:, bass.ds(h, 1), N * half:N * half + N].rearrange("p a n -> p (a n)"), osc[:, :],
                       ACT.Copy).then_inc(oh_done, 1)

    def act_row_sums(act, h, half):
        act.wait_ge(r_turned, 2 * h + half + 1)
        act.activation(rsb[:, :], bank(7), ACT.Copy).then_inc(r_copied, 1)

    def act_attention_head(act, h, last):
        t0, tg = PREP + T_HEAD * h, TG_LAST if last else TG
        act_exp(act, h, 1)
        for j in range(2, NT):
            if j == 6:
                act_row_sums(act, h, 0)
            act_turned(act, j - 2, t0 + tg[j - 2])
            act_exp(act, h, j)
            if j == 2:
                act.wait_ge(v_in, 16 * h + 16)
                act.activation(v_hi[:, :, :], rv[:, :, :], ACT.Copy).then_inc(vh_done, 1)
            if j == 5 and not last:
                act_turned(act, "Q0", t0 + tg["Q0"])
            if j == 6:
                act_out(act, h, 0)
        if last:
            act.wait_ge(s_done, NT * H)
            for i in range(4):
                split_hi(act, O_BASE + i, 0, d_hi[:, i, :])
        else:
            act_turned(act, "K", t0 + tg["K"])
        act_turned(act, 6, t0 + tg[6])
        if not last:
            act_turned(act, "Q1", t0 + tg["Q1"])
        act_turned(act, 7, t0 + tg[7])
        if not last:
            act_exp(act, h + 1, 0)
        act_row_sums(act, h, 1)
        act_out(act, h, 1)

    def act_attention(act):
        act_turned(act, "K", 0)
        act_turned(act, "Q0", 4)
        act_turned(act, "Q1", 6)
        act_exp(act, 0, 0)
        with act.Fori(0, H - 1) as h:
            act_attention_head(act, h, False)
        act_attention_head(act, H - 1, True)

    def dve_max(dve, h, j, turned):
        i = NT * h + j
        dve.wait_ge(s_done, i + 1)
        if turned is not None:
            dve.wait_ge(t_done, turned)
        dve.memset(cols(40 + j), 0.0).then_inc(b_own, 1)
        dve.tensor_tensor_reduce(out=pr[:, j % 2, :], in0=bank(2 * (j % 2), 2), in1=mask[:, j, :], scale=1.0,
                                 scalar=-3.0e38, op0=ALU.add, op1=ALU.max, accum_out=stat[:, j:j + 1]).then_inc(b_own, 1)
        dve.wait_ge(b_own, 2 * i + 2)
        dve.tensor_scalar(stat[:, 8 + j:9 + j], stat[:, j:j + 1], -SCALE, None, ALU.mult).then_inc(s_max, 1)

    def dve_row_sums(dve, h, half):
        dve.wait_ge(e_done, NT * h + 4 * half + 4)
        dve.reciprocal(stat[:, 32 + 4 * half:36 + 4 * half], stat[:, 16 + 4 * half:20 + 4 * half]).then_inc(r_inv, 1)

    def dve_out(dve, h, half):
        r = 2 * h + half
        dve.wait_ge(pv_done, r + 1)
        dve.wait_ge(r_copied, r + 1)
        dve.tensor_tensor(osc[:, :], bank(6), rsb[:, :], ALU.mult).then_inc(o_norm, 1)

    def dve_out_lo(dve, h, half):
        col = slice(N * half, N * half + N)
        dve.wait_ge(oh_done, 2 * h + half + 1)
        dve.tensor_tensor(h_lo[:, bass.ds(h, 1), col].rearrange("p a n -> p (a n)"), osc[:, :],
                          f32(h_hi[:, bass.ds(h, 1), col].rearrange("p a n -> p (a n)")), ALU.subtract).then_inc(ol_done, 1)

    def dve_attention_head(dve, h, last):
        t0, tg = PREP + T_HEAD * h, TG_LAST if last else TG
        dve_max(dve, h, 1, t0)
        for j in range(2, NT):
            if j == 6:
                dve_out(dve, h, 0)
            dve_max(dve, h, j, t0 + tg[j - 2] + 2)
            if j == 5:
                dve_row_sums(dve, h, 0)
            dve_turned(dve, j - 2, t0 + tg[j - 2])
            if j == 2:
                dve.wait_ge(vh_done, h + 1)
                dve.tensor_tensor(v_lo[:, :, :], rv[:, :, :], f32(v_hi[:, :, :]), ALU.subtract).then_inc(vl_done, 1)
            if j == 5 and not last:
                dve_turned(dve, "Q0", t0 + tg["Q0"])
            if j == 6:
                dve_out_lo(dve, h, 0)
        if last:
            for i in range(4):
                split_lo(dve, O_BASE + i, 0, d_lo[:, i, :], d_hi[:, i, :])
        else:
            dve_turned(dve, "K", t0 + tg["K"])
        dve_turned(dve, 6, t0 + tg[6])
        dve_row_sums(dve, h, 1)
        if not last:
            dve_turned(dve, "Q1", t0 + tg["Q1"])
        dve_turned(dve, 7, t0 + tg[7])
        if not last:
            dve_max(dve, h + 1, 0, t0 + tg[6] + 2)
        dve_out(dve, h, 1)
        dve_out_lo(dve, h, 1)

    def dve_attention(dve):
        dve_turned(dve, "K", 0)
        dve_turned(dve, "Q0", 4)
        dve_turned(dve, "Q1", 6)
        dve_max(dve, 0, 0, None)
        with dve.Fori(0, H - 1) as h:
            dve_attention_head(dve, h, False)
        dve_attention_head(dve, H - 1, True)

    u_done, u_free = sem("u_done"), sem("u_free")
    d_done, d_free = sem("d_done"), sem("d_free")
    square_done = sem("square_done")
    m_hi_done, m_lo_done = sem("m_hi_done"), sem("m_lo_done")
    x_in = [sem(f"x_in{t}") for t in range(NT)]
    gain_in = sem("gain_in")
    n_ss, n_root, n_own, n_xn, n_hi = sem("n_ss"), sem("n_root"), sem("n_own"), sem("n_xn"), sem("n_hi")
    c_own = sem("c_own")
    stored = sem("stored")

    def o_unit(j):
        return ins["attn_w_o"][0, P * j:P * j + P, :]

    def w1_unit(layer, j):
        return ins["mlp_w1"][layer, :, bass.ds(j * P, P)].rearrange("(k p) n -> p k n", p=P)

    def w2_unit(layer, j):
        return ins["mlp_w2"][layer, bass.ds(j * P, P), :]

    PARTS = (1, 2, 0)

    def in_unit(tile, part):
        return ins["conv_w_in"][0, :, bass.ds(PARTS[part] * D + tile * P, P)].rearrange("(k p) n -> p k n", p=P)

    def out_unit(j):
        return ins["conv_w_out"][0, bass.ds(j * P, P), :]

    MLP_CHUNKS = FF // N
    D_O = 0
    D_M1 = D_O + 16 + 32
    D_C = D_M1 + 16 * (MLP_CHUNKS - 1) + 32
    D_M2 = D_C + 16 + 32
    M1 = dict(unit=M1_BASE, down=D_M1, up=0, inner=0, square=0, norm=1, layer=0)
    C = dict(unit=C_BASE, down=D_C, up=64, inner=64, norm=2)
    M2 = dict(unit=M2_BASE, down=D_M2, up=64 + 48, inner=64 + 16, square=64, norm=3, layer=1)

    def order(hook):
        seq = []
        for t in range(NT):
            seq += [("D", t, 0), ("D", t, 1)]
            if hook and t:
                seq += [("T", t - 1, 0), ("T", t - 1, 1)]
        return seq + ([("T", NT - 1, 0), ("T", NT - 1, 1)] if hook else [])

    PLAIN = [("D", t, dh) for t in range(NT) for dh in range(2)]

    def pe_down(pe, base, seq, norm, stationary, moving, ready=None):
        for g, (kind, t, dh) in enumerate(seq):
            pe.wait_ge(d_free, base + g + 1)
            dst = bank(4 + g % 4)
            if kind == "D":
                if ready is not None and dh == 0 and t in (0, 4):
                    pe.wait_ge(m_lo_done, ready + 7 + t // 4)
                last = passes(pe, dst, [(*stationary(j, slice(P * t, P * t + P)), *moving(j, slice(N * dh, N * dh + N)))
                                        for j in range(4)])
            else:
                pe.wait_ge(n_xn, NT * norm + t + 1)
                for k in range(4):
                    last = pe.transpose(dst[:, k * P:(k + 1) * P], scr[:, t % 2, (4 * dh + k) * P:(4 * dh + k + 1) * P],
                                        ident[:, :])
            last.then_inc(d_done, 1)

    def dve_norm(dve, norm, t):
        i = NT * norm + t
        dve.wait_ge(n_root, i + 1)
        link, _ = linker(dve, n_own, 5 * i)
        dve_rstd(dve, link, cols(R_N), cols(MS_N + t % 2), cols(ROOT_N + t % 2), cols(TMP_N))
        if t == 0:
            dve.wait_ge(gain_in, 16 * norm + 16)
        dve.scalar_tensor_tensor(scr[:, t % 2, :], x[:, t, :], cols(R_N), gain[:, 0:D], ALU.mult, ALU.mult).then_inc(n_xn, 1)

    def dve_down(dve, base, seq, norm):
        for g, (kind, t, dh) in enumerate(seq):
            src = bank(4 + g % 4)
            if kind == "D":
                dst = x[:, t, N * dh:N * dh + N]
                dve.wait_ge(d_done, base + g + 1)
                if norm == 0 and dh == 0:
                    dve.wait_ge(x_in[t], 16)
                dve.tensor_tensor(dst, src, dst, ALU.add).then_inc(d_free, 1)
                if len(seq) > 16 and dh == 0 and t:
                    dve_norm(dve, norm, t - 1)
            else:
                if t == NT - 1 and dh == 0:
                    dve_norm(dve, norm, t)
                i = 2 * (NT * norm + t) + dh
                tok = slice(P * t, P * t + P)
                dve.wait_ge(n_hi, i + 1)
                dve.tensor_tensor(h_lo[:, 4 * dh:4 * dh + 4, tok], src.rearrange("p (k q) -> p k q", k=4),
                                  f32(h_hi[:, 4 * dh:4 * dh + 4, tok]), ALU.subtract).then_inc(d_free, 1)

    def act_down(act, base, seq, norm):
        for g, (kind, t, dh) in enumerate(seq):
            if kind == "D" and dh == 1:
                act.wait_ge(d_free, 4 + base + g + 1)
                act.activation(scr[:, t % 2, :], x[:, t, :], ACT.Square, scale=float(D) ** -0.5,
                               accum_out=cols(MS_N + t % 2)).then_inc(n_ss, 1)
                act.wait_ge(n_ss, NT * norm + t + 1)
                act.activation(cols(ROOT_N + t % 2), cols(MS_N + t % 2), ACT.Sqrt, bias=cols(EPS_C)).then_inc(n_root, 1)
            if kind == "T":
                act.wait_ge(d_done, base + g + 1)
                act.activation(h_hi[:, 4 * dh:4 * dh + 4, P * t:P * t + P],
                               bank(4 + g % 4).rearrange("p (k q) -> p k q", k=4), ACT.Copy).then_inc(n_hi, 1)

    def inner(j, tok):
        return m_hi[:, j, tok], m_lo[:, j, tok]

    def down_weights(j, feat):
        return d_hi[:, j, feat], d_lo[:, j, feat]

    def sp_out_proj(sp):
        for t in range(4):
            if t == 0:
                sp.wait_ge(t_done, PREP + T_HEAD * (H - 1))
            sp.dma_start(x[:, t, :], x_rows[:, t, :]).then_inc(x_in[t], 16)
        sp.wait_ge(vl_done, H)
        sp.dma_start(x[:, 4, :], x_rows[:, 4, :]).then_inc(x_in[4], 16)
        for j in range(4, 8):
            load_unit(sp, O_BASE + j, 0, o_unit(j))
        sp.wait_ge(t_done, PREP + T_HEAD * (H - 1) + 16)
        for t in (5, 6):
            sp.dma_start(x[:, t, :], x_rows[:, t, :]).then_inc(x_in[t], 16)
        sp.wait_ge(ol_done, 2 * H)
        sp.dma_start(x[:, 7, :], x_rows[:, 7, :]).then_inc(x_in[7], 16)
        for j in range(2):
            load_unit(sp, O_BASE + 8 + j, 0, w1_unit(0, j))

    def pe_out_proj(pe):
        pe.wait_ge(t_free, PREP + T_HEAD * (H - 1) + 16)
        pe.wait_ge(ol_done, 2 * H)
        pe.wait_ge(w_lo_done, O_BASE + 4)
        pe_down(pe, D_O, PLAIN, 0, lambda j, tok: (h_hi[:, j, tok], h_lo[:, j, tok]), down_weights)
        pe.wait_ge(w_lo_done, O_BASE + 8)
        pe_down(pe, D_O + 16, order(True), 0, lambda j, tok: (h_hi[:, 4 + j, tok], h_lo[:, 4 + j, tok]),
                lambda j, feat: (o_hi[:, j, feat], o_lo[:, j, feat]))

    def act_out_proj(act):
        act.wait_ge(pv_done, 2 * H)
        for j in range(4):
            split_hi(act, O_BASE + 4 + j, 0, o_hi[:, j, :])
        for j in range(2):
            split_hi(act, O_BASE + 8 + j, 0, u_hi[:, j, :].rearrange("p (k n) -> p k n", k=ND))
        act_down(act, D_O + 16, order(True), 0)

    def dve_out_proj(dve):
        for j in range(4):
            split_lo(dve, O_BASE + 4 + j, 0, o_lo[:, j, :], o_hi[:, j, :])
        for j in range(2):
            split_lo(dve, O_BASE + 8 + j, 0, u_lo[:, j, :].rearrange("p (k n) -> p k n", k=ND),
                     u_hi[:, j, :].rearrange("p (k n) -> p k n", k=ND))
        dve_down(dve, D_O, PLAIN, 0)
        dve_down(dve, D_O + 16, order(True), 0)

    def u_view(ap, slot):
        return ap[:, slot, :].rearrange("p (k n) -> p k n", k=ND)

    def pe_up_unit(pe, slot, up, bank0, ready):
        pe.wait_ge(w_lo_done, ready)
        for half in range(2):
            pe.wait_ge(u_free, up + half + 1)
            tok = slice(N * half, N * half + N)
            passes(pe, bank(bank0 + half), [(u_hi[:, slot, P * k:P * k + P], u_lo[:, slot, P * k:P * k + P],
                                             h_hi[:, k, tok], h_lo[:, k, tok]) for k in range(ND)]).then_inc(u_done, 1)

    def mlp_unit(g, last, final):
        if final and last and g in (5, 7):
            return None
        offset = 5 if final and last and g == 6 else g
        return (offset, "D", g // 2) if g % 2 == 0 else (offset, "U", (g - 1) // 2 + 2)

    def mlp_loop(e, chunk):
        with e.Fori(0, MLP_CHUNKS - 1) as c:
            chunk(c, False)
        chunk(MLP_CHUNKS - 1, True)

    def sp_mlp(sp, st, then):
        def chunk(c, last):
            for g in range(8):
                unit = mlp_unit(g, last, then is None)
                if unit:
                    offset, kind, j = unit
                    src = (w2_unit(st["layer"], 4 * c + j) if kind == "D" else then(j - 4) if last and j > 3
                           else w1_unit(st["layer"], 4 * c + j))
                    load_unit(sp, st["unit"] + offset, 8 * c, src)
        mlp_loop(sp, chunk)

    def pe_mlp(pe, st, final):
        pe.wait_ge(d_free, 4 + st["down"])
        def chunk(c, last):
            for u in range(4):
                ready = st["unit"] + (-1, 0, 2, 4)[u]
                pe_up_unit(pe, u % 2, st["up"] + 8 * c + 2 * u, 2 * u % 4, 8 * c + ready)
            pe.wait_ge(w_lo_done, st["unit"] + 8 * c + (6 if final and last else 7))
            pe_down(pe, st["down"] + 16 * c, order(not final) if last else PLAIN, st["norm"], inner, down_weights,
                    st["inner"] + 8 * c)
        mlp_loop(pe, chunk)

    def act_mlp(act, st, final):
        def chunk(c, last):
            for g in range(8):
                up = st["up"] + 8 * c + g
                r = scr[:, 0, N * (g % 2):N * (g % 2) + N]
                act.wait_ge(u_done, up + 1)
                act.wait_ge(square_done, st["square"] + 8 * c + g + 1)
                act.activation(r, bank(g % 4), ACT.Relu).then_inc(u_free, 1)
                act.wait_ge(u_free, 4 + up + 1)
                act.activation(m_hi[:, g // 2, N * (g % 2):N * (g % 2) + N], r, ACT.Square).then_inc(m_hi_done, 1)
                unit = mlp_unit(g, last, final)
                if unit:
                    offset, kind, j = unit
                    split_hi(act, st["unit"] + offset, 8 * c, d_hi[:, j, :] if kind == "D" else u_view(u_hi, j % 2))
            if last and not final:
                act_down(act, st["down"] + 16 * c, order(True), st["norm"])
        mlp_loop(act, chunk)

    def dve_mlp(dve, st, final):
        def chunk(c, last):
            for g in range(8):
                span = slice(N * (g % 2), N * (g % 2) + N)
                square = scr[:, 1, span]
                dve.wait_ge(u_free, 4 + st["up"] + 8 * c + g + 1)
                dve.tensor_tensor(square, scr[:, 0, span], scr[:, 0, span], ALU.mult).then_inc(square_done, 1)
                dve.wait_ge(square_done, st["square"] + 8 * c + g + 3)
                dve.wait_ge(m_hi_done, st["inner"] + 8 * c + g + 1)
                dve.tensor_tensor(m_lo[:, g // 2, span], square, f32(m_hi[:, g // 2, span]), ALU.subtract).then_inc(m_lo_done, 1)
                unit = mlp_unit(g, last, final)
                if unit:
                    offset, kind, j = unit
                    hi, lo = (d_hi[:, j, :], d_lo[:, j, :]) if kind == "D" else (u_view(u_hi, j % 2), u_view(u_lo, j % 2))
                    split_lo(dve, st["unit"] + offset, 8 * c, lo, hi)
            dve_down(dve, st["down"] + 16 * c, order(not final) if last else PLAIN, st["norm"])
        mlp_loop(dve, chunk)

    def conv_pairs(e, pair, down):
        with e.Fori(0, 2) as r:
            pair(r, r, False)
        down(0)
        pair(2, 0, False)
        pair(3, 1, True)
        down(1)

    def d_slot(ap, r, i):
        return ap[:, bass.ds(2 * r + i // 3, 1), :].rearrange("p a n -> p (a n)")

    def sp_conv(sp, then):
        def pair(pp, r, last):
            for i in range(6):
                tile, part = (i + 2) // 3, (i + 2) % 3
                src = then(i - 4) if last and i > 3 else in_unit(2 * pp + tile, part)
                load_unit(sp, C["unit"] + i + i // 3, 8 * pp, src)
                if i % 3 == 2:
                    load_unit(sp, C["unit"] + i + i // 3 + 1, 8 * pp, out_unit(2 * pp + i // 3))
        for pp in range(4):
            pair(pp, pp % 2, pp == 3)

    def pe_conv(pe):
        pe.wait_ge(d_free, 4 + C["down"])

        def pair(pp, r, last):
            for i in range(6):
                ready = (-2, 0, 1, 2, 3, 5)[i]
                pe_up_unit(pe, i % 2, C["up"] + 12 * pp + 2 * i, 2 * i % 4, C["unit"] + 8 * pp + ready)

        def down(c):
            pe.wait_ge(w_lo_done, C["unit"] + 16 * c + 16)
            pe_down(pe, C["down"] + 16 * c, order(True) if c else PLAIN, C["norm"], inner, down_weights, C["inner"] + 8 * c)
        conv_pairs(pe, pair, down)

    def act_conv(act):
        def pair(pp, r, last):
            for i in range(6):
                if i % 3 == 2:
                    for half in range(2):
                        span = slice(N * half, N * half + N)
                        act.wait_ge(u_free, 4 + C["up"] + 12 * pp + 2 * i + half + 1)
                        act.activation(m_hi[:, bass.ds(2 * r + i // 3, 1), span].rearrange("p a n -> p (a n)"),
                                       scr[:, 1, span], ACT.Copy).then_inc(m_hi_done, 1)
                else:
                    act.wait_ge(u_done, C["up"] + 12 * pp + 2 * i + 2)
                split_hi(act, C["unit"] + i + i // 3, 8 * pp, u_view(u_hi, i % 2))
                if i % 3 == 2:
                    split_hi(act, C["unit"] + i + i // 3 + 1, 8 * pp, d_slot(d_hi, r, i))

        def down(c):
            if c:
                act_down(act, C["down"] + 16 * c, order(True), C["norm"])
        conv_pairs(act, pair, down)

    CONV_OWN = 6

    def dve_conv(dve):
        gate, conv, u = scr[:, 0, :], scr[:, 1, :], gain
        dve.memset(gain[:, 0:2], 0.0).then_inc(c_own, 1)

        def pair(pp, r, last):
            link, count = linker(dve, c_own, 1 + CONV_OWN * pp)
            for i in range(6):
                for half in range(2):
                    span = slice(N * half, N * half + N)
                    up = C["up"] + 12 * pp + 2 * i + half
                    src = bank((2 * i + half) % 4)
                    dve.wait_ge(u_done, up + 1)
                    if i % 3 == 0:
                        dve.tensor_copy(gate[:, span], src).then_inc(u_free, 1)
                    elif i % 3 == 1:
                        dve.wait_ge(u_free, 4 + up - 1)
                        dve.tensor_tensor(u[:, 2 + N * half:2 + N * half + N], src, gate[:, span], ALU.mult).then_inc(u_free, 1)
                    else:
                        dve.tensor_tensor(conv[:, span], src, conv[:, span], ALU.mult).then_inc(u_free, 1)
                        m = C["inner"] + 4 * pp + 2 * (i // 3) + half
                        dve.wait_ge(m_hi_done, m + 1)
                        j = bass.ds(2 * r + i // 3, 1)
                        dve.tensor_tensor(m_lo[:, j, span].rearrange("p a n -> p (a n)"), conv[:, span],
                                          f32(m_hi[:, j, span].rearrange("p a n -> p (a n)")), ALU.subtract).then_inc(m_lo_done, 1)
                if i % 3 == 1:
                    dve.wait_ge(u_free, 4 + C["up"] + 12 * pp + 2 * i + 2)
                    tap = [at(convw, w)[:, bass.ds(2 * pp + i // 3, 1)] for w in range(3)]
                    link(dve.tensor_scalar(conv, u[:, 2:2 + S], tap[2], None, ALU.mult))
                    link(dve.scalar_tensor_tensor(conv, u[:, 1:1 + S], tap[1], conv, ALU.mult, ALU.add))
                    link(dve.scalar_tensor_tensor(conv, u[:, 0:S], tap[0], conv, ALU.mult, ALU.add))
                split_lo(dve, C["unit"] + i + i // 3, 8 * pp, u_view(u_lo, i % 2), u_view(u_hi, i % 2))
                if i % 3 == 2:
                    split_lo(dve, C["unit"] + i + i // 3 + 1, 8 * pp, d_slot(d_lo, r, i), d_slot(d_hi, r, i))

        def down(c):
            dve_down(dve, C["down"] + 16 * c, order(True) if c else PLAIN, C["norm"])
        dve.wait_ge(c_own, 1)
        conv_pairs(dve, pair, down)

    with nc.Block() as block:
        @block.sync
        def _(sp):
            sp_produce_setup(sp)
            sp_produce(sp, 0, False)
            with sp.Fori(1, NT - 1) as t:
                sp_produce(sp, t, False)
            sp_produce(sp, NT - 1, True)
            sp_attention(sp)
            sp_out_proj(sp)
            sp_mlp(sp, M1, lambda j: in_unit(0, j))
            sp_conv(sp, lambda j: w1_unit(1, j))
            sp_mlp(sp, M2, None)
            for t in range(NT):
                sp.wait_ge(d_free, 4 + M2["down"] + 16 * (MLP_CHUNKS - 1) + 2 * t + 2)
                sp.dma_start(out_rows[:, t, :], x[:, t, :]).then_inc(stored, 16)
            sp.wait_ge(stored, 16 * NT)

        @block.gpsimd
        def _(pool):
            pool_setup(pool)
            pool_produce(pool, 0)
            with pool.Fori(1, NT) as t:
                pool_produce(pool, t)
            pool.wait_ge(a_xn, NT)
            pool.dma_start(gain[:, 0:D], spread(ins["g_mlp"][0, :])).then_inc(gain_in, 16)
            pool.wait_ge(n_xn, NT)
            pool.dma_start(gain[:, 0:D], spread(ins["g_mix"][1, :])).then_inc(gain_in, 16)
            pool.wait_ge(m_lo_done, C["inner"] + 16)
            pool.dma_start(gain[:, 0:D], spread(ins["g_mlp"][1, :])).then_inc(gain_in, 16)

        @block.scalar
        def _(act):
            act_produce(act, 0)
            with act.Fori(1, NT) as t:
                act_produce(act, t)
            act_attention(act)
            act_out_proj(act)
            act_mlp(act, M1, False)
            act_conv(act)
            act_mlp(act, M2, True)

        @block.vector
        def _(dve):
            n = dve_produce(dve, 0)
            assert n == A_OWN, n
            with dve.Fori(1, NT) as t:
                dve_produce(dve, t)
            dve_attention(dve)
            dve_out_proj(dve)
            dve_mlp(dve, M1, False)
            dve_conv(dve)
            dve_mlp(dve, M2, True)

        @block.tensor
        def _(pe):
            pe.wait_ge(ident_done, 2)
            pe_produce(pe, 0)
            with pe.Fori(1, NT) as t:
                pe_produce(pe, t)
            pe_attention(pe)
            pe_out_proj(pe)
            pe_mlp(pe, M1, False)
            pe_conv(pe)
            pe_mlp(pe, M2, True)


_INS = ["x", "positions", "g_mix", "g_mlp", "attn_w_down", "attn_g_q_a", "attn_g_kv_a", "attn_w_uq", "attn_w_ukv",
        "attn_g_qnorm", "attn_g_knorm", "attn_w_o", "conv_w_in", "conv_w", "conv_w_out", "mlp_w1", "mlp_w2"]


def kernel(**inputs):
    import concourse.bacc as bacc
    from concourse.bass_utils import run_bass_kernel_spmd

    nc = bacc.Bacc("TRN2", target_bir_lowering=False, num_devices=1)
    arrays = {n: np.ascontiguousarray(inputs[n]) for n in _INS}
    arrays["inv_freq"] = (10000.0 ** (-np.arange(0, ROPE, 2) / ROPE)).astype(np.float32)
    ins = {n: nc.dram_tensor("in_" + n, a.shape, mybir.dt.from_np(a.dtype), kind="ExternalInput").ap()
           for n, a in arrays.items()}
    out = nc.dram_tensor("out", [1, S, D], F32, kind="ExternalOutput").ap()
    build(nc, ins, out)
    result = run_bass_kernel_spmd(nc, [{"in_" + n: a for n, a in arrays.items()}], core_ids=[0])
    return result.results[0]["out"]
```

```python
import numpy as np

import concourse.bass as bass
from concourse import mybir

F32 = mybir.dt.float32
F32R = mybir.dt.float32r
BF16 = mybir.dt.bfloat16
I32 = mybir.dt.int32
ALU = mybir.AluOpType
ACT = mybir.ActivationFunctionType
AX = mybir.AxisListType

P = 128
S = 1024
D = 1024
NT = S // P
ND = D // P
H = 8
NOPE, ROPE, VD = 128, 64, 128
HALF = ROPE // 2
QK = NOPE + ROPE
CQ, CKV = 256, 128
DOWN = CQ + CKV + ROPE
NC = (CQ + CKV) // P
FF = 4 * D
EPS = 1e-6
N = 512
UNIT = 1024
RAW = 4
SCALE = float(QK) ** -0.5
FAR = 1.6e38
PROD_UNITS = 9
KB = 1024


def build(nc, ins, out):
    top = nc.sbuf_base + 31 & ~31
    place = {}

    def sb(name, shape, dtype, offset):
        place[name] = nc.alloc_sbuf_tensor_at(name, shape, dtype, offset=top + offset)
        return place[name]

    X0, DS0, US0, M0, SC0, G0 = 0, 32 * KB, 64 * KB, 80 * KB, 112 * KB, 120 * KB
    HT0 = G0 + 4 * KB + 128
    RAW0 = HT0 + 64 * KB
    SM0 = RAW0 + 16 * KB
    x = sb("x", [P, NT, D], F32, X0)
    d_hi = sb("d_hi", [P, 4, UNIT], F32R, DS0)
    d_lo = sb("d_lo", [P, 4, UNIT], F32R, DS0 + 16 * KB)
    u_hi = sb("u_hi", [P, 2, UNIT], F32R, US0)
    u_lo = sb("u_lo", [P, 2, UNIT], F32R, US0 + 8 * KB)
    m_hi = sb("m_hi", [P, 4, S], F32R, M0)
    m_lo = sb("m_lo", [P, 4, S], F32R, M0 + 16 * KB)
    scr = sb("scr", [P, 2, D], F32, SC0)
    gain = sb("gain", [P, D + 2], F32, G0)
    h_hi = sb("h_hi", [P, ND, S], F32R, HT0)
    h_lo = sb("h_lo", [P, ND, S], F32R, HT0 + 32 * KB)
    raw = sb("raw", [P, RAW, UNIT], F32, RAW0)
    ident = sb("ident", [P, P], F32, SM0)
    stat = sb("stat", [P, 104], F32, SM0 + 1024)
    gain_col = sb("gain_col", [P, 2], F32, SM0 + 896)
    convw = sb("convw", [P, 3, ND], F32, SM0 + 768)
    o_hi = sb("o_hi", [P, 4, UNIT], F32R, M0)
    o_lo = sb("o_lo", [P, 4, UNIT], F32R, M0 + 16 * KB)
    rq = sb("rq", [P, NT, 256], F32, RAW0)
    rk = sb("rk", [P, NT, 256], F32, RAW0 + 8 * KB)
    rv = sb("rv", [P, NT, VD], F32, X0)
    osc = sb("osc", [P, N], F32, X0 + 12 * KB)
    rsb = sb("rsb", [P, N], F32, X0 + 14 * KB)
    pr = sb("pr", [P, 4, S], F32, X0 + 16 * KB)
    q_hi = sb("q_hi", [P, S], F32R, DS0)
    q_lo = sb("q_lo", [P, S], F32R, DS0 + 4 * KB)
    q_rope = sb("q_rope", [P, S], F32R, DS0 + 8 * KB)
    k_hi = sb("k_hi", [P, S], F32R, DS0 + 12 * KB)
    k_lo = sb("k_lo", [P, S], F32R, DS0 + 16 * KB)
    kr_hi = sb("kr_hi", [P, S], F32R, DS0 + 20 * KB)
    kr_lo = sb("kr_lo", [P, S], F32R, DS0 + 24 * KB)
    pt_hi = sb("pt_hi", [P, NT, N], F32R, US0)
    pt_lo = sb("pt_lo", [P, NT, N], F32R, US0 + 16 * KB)
    v_hi = sb("v_hi", [P, NT, VD], F32R, US0 + 32 * KB)
    v_lo = sb("v_lo", [P, NT, VD], F32R, US0 + 36 * KB)
    mask = sb("mask", [P, NT, S], BF16, US0 + 40 * KB)
    xt = sb("xt", [P, D], F32, X0)
    xn = sb("xn", [P, D], F32, X0 + 8 * KB)
    posk_i = sb("posk_i", [P, S], I32, X0 + 12 * KB)
    cos_1 = sb("cos_1", [P, NT, HALF], F32, X0 + 12 * KB)
    sin_1 = sb("sin_1", [P, NT, HALF], F32, X0 + 13 * KB)
    cos_2 = sb("cos_2", [P, NT, HALF], F32, X0 + 14 * KB)
    sin_2 = sb("sin_2", [P, NT, HALF], F32, X0 + 15 * KB)
    posk = sb("posk", [P, S], F32, X0 + 16 * KB)
    cos = sb("cos", [P, NT, HALF], F32, X0 + 20 * KB)
    sin = sb("sin", [P, NT, HALF], F32, X0 + 21 * KB)
    ang = sb("ang", [P, NT, HALF], F32, X0 + 22 * KB)
    turn = sb("turn", [P, NT, HALF], F32, X0 + 23 * KB)
    g_c = sb("g_c", [P, CQ + CKV], F32, X0 + 24 * KB)
    g_q = sb("g_q", [P, QK], F32, X0 + 24 * KB + 1536)
    g_k = sb("g_k", [P, QK], F32, X0 + 24 * KB + 2304)
    freq = sb("freq", [P, HALF], F32, X0 + 24 * KB + 3072)
    posq_i = sb("posq_i", [P, NT], I32, X0 + 24 * KB + 3200)
    posq = sb("posq", [P, NT], F32, X0 + 24 * KB + 3264)
    c_sb = sb("c_sb", [P, DOWN], F32, X0 + 24 * KB + 3328)
    rotk = sb("rotk", [P, ROPE], F32, X0 + 24 * KB + 5120)
    tmp_r = sb("tmp_r", [P, ROPE], F32, X0 + 24 * KB + 5376)
    wd_hi = sb("wd_hi", [P, ND, DOWN], F32R, DS0)
    wd_lo = sb("wd_lo", [P, ND, DOWN], F32R, DS0 + 14 * KB)
    wq_hi = sb("wq_hi", [P, 2, H * QK], F32R, US0)
    wq_lo = sb("wq_lo", [P, 2, H * QK], F32R, US0 + 12 * KB)
    wk_hi = sb("wk_hi", [P, H * (NOPE + VD)], F32R, US0 + 24 * KB)
    wk_lo = sb("wk_lo", [P, H * (NOPE + VD)], F32R, US0 + 32 * KB)
    hx_hi = sb("hx_hi", [P, ND, P], F32R, HT0)
    hx_lo = sb("hx_lo", [P, ND, P], F32R, HT0 + 4 * KB)
    ct_hi = sb("ct_hi", [P, NC, P], F32R, HT0 + 8 * KB)
    ct_lo = sb("ct_lo", [P, NC, P], F32R, HT0 + 8 * KB + 1536)
    qs = sb("qs", [P, H, QK], F32, HT0 + 11 * KB)
    ks = sb("ks", [P, H, QK], F32, HT0 + 17 * KB)
    vs = sb("vs", [P, H, VD], F32, HT0 + 23 * KB)
    q_sq = sb("q_sq", [P, H, QK], F32, HT0 + 27 * KB)
    k_sq = sb("k_sq", [P, H, NOPE], F32, HT0 + 33 * KB)
    junk = sb("junk", [P, D], F32, HT0 + 37 * KB)
    junk_c = sb("junk_c", [P, DOWN], F32, HT0 + 45 * KB)
    ra = sb("ra", [P, H, HALF], F32, HT0 + 41 * KB)
    rb = sb("rb", [P, H, HALF], F32, HT0 + 42 * KB)
    rc = sb("rc", [P, H, HALF], F32, HT0 + 43 * KB)
    rd = sb("rd", [P, H, HALF], F32, HT0 + 44 * KB)

    psum = nc.alloc_psum_tensor("psum", [P, 8 * N], F32)
    qd = nc.dram_tensor("q_heads", [S, H, QK], F32, kind="Internal").ap()
    kd = nc.dram_tensor("k_heads", [S, H, QK], F32, kind="Internal").ap()
    vd = nc.dram_tensor("v_heads", [S, H, VD], F32, kind="Internal").ap()

    def bank(b, n=1):
        return psum[:, b * N:(b + n) * N]

    def f32(ap):
        return ap.bitcast(F32)


    def sem(name):
        return nc.alloc_semaphore(name)

    def wait(e, s, value):
        if not isinstance(value, int) or value > 0:
            e.wait_ge(s, value)

    def linker(e, s, base):
        count = [0]

        def link(ins):
            count[0] += 1
            ins.then_inc(s, 1)
            e.wait_ge(s, base + count[0])
        return link, count

    def passes(pe, dst, terms):
        for n, (s_hi, s_lo, m_hi_, m_lo_) in enumerate(terms):
            pe.matmul(dst, s_hi, m_hi_, start=n == 0, stop=False)
            pe.matmul(dst, s_hi, m_lo_, start=False, stop=False)
            last = pe.matmul(dst, s_lo, m_hi_, start=False, stop=n == len(terms) - 1)
        return last

    x_rows = ins["x"].rearrange("a (t p) d -> p (a t) d", p=P)
    out_rows = out.rearrange("a (t p) d -> p (a t) d", p=P)

    def spread(src):
        return bass.AP(tensor=src.tensor, offset=src.offset, ap=[[0, P], [1, src.shape[0]]])

    def heads(ap, n):
        return ap.unsqueeze(2).to_broadcast([P, H, n])

    def all_heads(ap, n):
        return ap.unsqueeze(1).to_broadcast([P, H, n])

    raw_in = [sem(f"raw_in{i}") for i in range(RAW)]
    w_hi_done, w_lo_done = sem("w_hi_done"), sem("w_lo_done")
    O_BASE = PROD_UNITS
    M1_BASE = O_BASE + 8 + 2
    C_BASE = M1_BASE + 8 * (FF // N)
    M2_BASE = C_BASE + 16 * 2

    def like(slot, ap):
        shape = list(ap.shape)
        v = raw[:, slot, 0:shape[1] * (shape[2] if len(shape) == 3 else 1)]
        return v.rearrange("p (a b) -> p a b", a=shape[1]) if len(shape) == 3 else v

    def load_unit(sp, s, more, src):
        wait(sp, w_lo_done, s + more - RAW + 1)
        sp.dma_start(like(s % RAW, src), src).then_inc(raw_in[s % RAW], 16)

    def split_hi(act, s, more, dst):
        act.wait_ge(raw_in[s % RAW], 16 * (s // RAW + 1) + more * (16 // RAW))
        act.activation(dst, like(s % RAW, dst), ACT.Copy).then_inc(w_hi_done, 1)

    def split_lo(dve, s, more, dst, hi):
        dve.wait_ge(w_hi_done, s + more + 1)
        dve.tensor_tensor(dst, like(s % RAW, dst), f32(hi), ALU.subtract).then_inc(w_lo_done, 1)

    def dve_rstd(dve, link, dst, mean, root, tmp):
        link(dve.reciprocal(dst, root))
        link(dve.tensor_tensor(tmp, dst, dst, ALU.mult))
        link(dve.scalar_tensor_tensor(tmp, mean, EPS, tmp, ALU.add, ALU.mult))
        link(dve.tensor_scalar(tmp, tmp, -0.5, 1.5, ALU.mult, ALU.add))
        link(dve.tensor_tensor(dst, dst, tmp, ALU.mult))

    def cols(a, n=1):
        return stat[:, a:a + n]

    MS_X, ROOT_X, R_X, MS_C, MS_KR, ROOT_C, R_C, TMP = 0, 1, 2, 3, 5, 6, 8, 10
    MS_Q, ROOT_Q, R_Q, SS_K, MS_K, ROOT_K, R_K = 18, 26, 34, 42, 50, 58, 66
    MS_SHARED, R_Q2 = 74, 92
    MS_N, ROOT_N, R_N, TMP_N, EPS_C = 80, 82, 84, 85, 86

    consts = sem("consts")
    pos_in = sem("pos_in")
    a_x_in, a_ss, a_xn = sem("a_x_in"), sem("a_ss"), sem("a_xn")
    a_turned, a_hx_hi, a_hx_lo = sem("a_turned"), sem("a_hx_hi"), sem("a_hx_lo")
    a_latent, a_latent_ss, a_c = sem("a_latent"), sem("a_latent_ss"), sem("a_c")
    a_c_turned, a_ct_hi, a_ct_lo = sem("a_c_turned"), sem("a_ct_hi"), sem("a_ct_lo")
    a_q, a_q_out, a_kv, a_kv_out = sem("a_q"), sem("a_q_out"), sem("a_kv"), sem("a_kv_out")
    a_q_sq, a_k_sq = sem("a_q_sq"), sem("a_k_sq")
    a_q_rot, a_k_norm, a_stored_q, a_stored_k, a_stored_v = (
        sem("a_q_rot"), sem("a_k_norm"), sem("a_stored_q"), sem("a_stored_k"), sem("a_stored_v"))
    a_k_copied, a_rope = sem("a_k_copied"), sem("a_rope")
    a_own, a_pool_own, ident_done = sem("a_own"), sem("a_pool_own"), sem("ident_done")
    a_root_x, a_root_c, a_root_h = sem("a_root_x"), sem("a_root_c"), sem("a_root_h")
    a_summed, a_q_factor, a_q_scaled, a_k_shared = sem("a_summed"), sem("a_q_factor"), sem("a_q_scaled"), sem("a_k_shared")
    a_own_c, a_own_h, a_own_r, eps_set, tables = sem("a_own_c"), sem("a_own_h"), sem("a_own_r"), sem("eps_set"), sem("tables")
    setup_own, ang_done = sem("setup_own"), sem("ang_done")
    CONSTS = 16 * 10
    KV_BANK = [7, 4, 5, 6]

    w_down = ins["attn_w_down"][0, :, :].rearrange("(k p) n -> p k n", p=P)
    w_uq = ins["attn_w_uq"][0, :, :].rearrange("(k p) n -> p k n", p=P)
    w_ukv = ins["attn_w_ukv"][0, :, :]

    def piece(s, down, uq, ukv):
        if s < 4:
            return down[:, 2 * s:2 * s + 2, :]
        if s < 7:
            return uq[:, :, N * (s - 4):N * (s - 3)]
        return ukv[:, UNIT * (s - 7):UNIT * (s - 6)]

    def a_store(ap, t):
        return ap[bass.ds(t * P, P), :, :]

    def sp_produce_setup(sp):
        sp.dma_start(xt[:, :], x_rows[:, 0, :]).then_inc(a_x_in, 16)
        sp.dma_start(gain[:, 0:D], spread(ins["g_mix"][0, :])).then_inc(consts, 16)
        for s in range(RAW):
            load_unit(sp, s, 0, piece(s, w_down, w_uq, w_ukv))
        sp.dma_start(posk_i[:, :], spread(ins["positions"][0, :])).then_inc(pos_in, 16)
        sp.dma_start(freq[:, :], spread(ins["inv_freq"])).then_inc(pos_in, 16)
        sp.dma_start(g_c[:, 0:CQ], spread(ins["attn_g_q_a"][0, :])).then_inc(consts, 16)
        sp.dma_start(g_c[:, CQ:], spread(ins["attn_g_kv_a"][0, :])).then_inc(consts, 16)
        sp.dma_start(g_q[:, :], spread(ins["attn_g_qnorm"][0, :])).then_inc(consts, 16)
        sp.dma_start(g_k[:, :], spread(ins["attn_g_knorm"][0, :])).then_inc(consts, 16)
        with nc.allow_non_contiguous_dma("one position or tap per partition"):
            sp.dma_start(posq_i[:, :], ins["positions"].rearrange("a (t p) -> p (a t)", p=P)).then_inc(pos_in, 16)
            sp.dma_start(gain_col[:, 0:1], ins["attn_g_qnorm"][0, 0:NOPE].rearrange("(p a) -> p a", a=1)).then_inc(consts, 16)
            sp.dma_start(gain_col[:, 1:2], ins["attn_g_knorm"][0, 0:NOPE].rearrange("(p a) -> p a", a=1)).then_inc(consts, 16)
            for w in range(3):
                sp.dma_start(convw[:, w, :], ins["conv_w"][0, w, :].rearrange("(k p) -> p k", p=P)).then_inc(consts, 16)
        for s in range(RAW, PROD_UNITS):
            load_unit(sp, s, 0, piece(s, w_down, w_uq, w_ukv))

    def a_steps(e, step):
        step(e, 0)
        step(e, 1)
        with e.Fori(2, NT - 1) as t:
            step(e, t)
        step(e, NT - 1)
        step(e, NT)

    def first(t):
        return isinstance(t, int) and t == 0

    def has_tile(t):
        return not isinstance(t, int) or t < NT

    def has_next(t):
        return not isinstance(t, int) or t < NT - 1

    def sp_produce(sp, t):
        if has_next(t):
            sp.wait_ge(a_xn, t + 1)
            sp.dma_start(xt[:, :], x_rows[:, bass.ds(t + 1, 1), :].rearrange("p a d -> p (a d)")).then_inc(a_x_in, 16)
        if not first(t):
            sp.wait_ge(a_kv_out, 4 * t)
            sp.dma_start(a_store(vd, t - 1), vs[:, :, :]).then_inc(a_stored_v, 16)
            sp.wait_ge(a_q_rot, t)
            sp.dma_start(a_store(qd, t - 1), qs[:, :, :]).then_inc(a_stored_q, 16)
            sp.wait_ge(a_k_norm, t)
            sp.dma_start(a_store(kd, t - 1), ks[:, :, :]).then_inc(a_stored_k, 16)

    def pe_produce(pe, t):
        if has_tile(t):
            pe.wait_ge(a_xn, t + 1)
            for b in range(2):
                for k in range(4):
                    last = pe.transpose(psum[:, b * N + k * P:b * N + (k + 1) * P],
                                        xn[:, (4 * b + k) * P:(4 * b + k + 1) * P], ident[:, :])
                last.then_inc(a_turned, 1)
            pe.wait_ge(a_hx_lo, 2 * t + 2)
            pe.wait_ge(w_lo_done, 4)
            passes(pe, psum[:, 2 * N:2 * N + DOWN],
                   [(hx_hi[:, k, :], hx_lo[:, k, :], wd_hi[:, k, :], wd_lo[:, k, :]) for k in range(ND)]
                   ).then_inc(a_latent, 1)
        if not first(t):
            pe.wait_ge(a_ct_lo, t)
            wait(pe, a_kv_out, 4 * t - 4)
            pe.wait_ge(w_lo_done, PROD_UNITS)
            for b in range(3):
                passes(pe, bank(4 + b), [(ct_hi[:, k, :], ct_lo[:, k, :], wq_hi[:, k, b * N:(b + 1) * N],
                                          wq_lo[:, k, b * N:(b + 1) * N]) for k in range(2)]).then_inc(a_q, 1)
            for b in range(4):
                if b:
                    pe.wait_ge(a_q_out, 3 * t - 3 + b)
                passes(pe, bank(KV_BANK[b]), [(ct_hi[:, 2, :], ct_lo[:, 2, :], wk_hi[:, b * N:(b + 1) * N],
                                               wk_lo[:, b * N:(b + 1) * N])]).then_inc(a_kv, 1)
        if has_tile(t):
            pe.wait_ge(a_c, t + 1)
            for k in range(NC):
                last = pe.transpose(psum[:, 3 * N + k * P:3 * N + (k + 1) * P], c_sb[:, k * P:(k + 1) * P], ident[:, :])
            last.then_inc(a_c_turned, 1)

    def act_produce_setup(act):
        act.wait_ge(ang_done, 1)
        act.activation(sin[:, :, :], ang[:, :, :], ACT.Sin).then_inc(a_rope, 1)
        act.wait_ge(ang_done, 2)
        act.activation(cos[:, :, :], turn[:, :, :], ACT.Sin).then_inc(a_rope, 1)

    def act_produce_weights(act, units):
        for s in units:
            split_hi(act, s, 0, piece(s, wd_hi, wq_hi, wk_hi))

    def act_mean_square(act, t):
        act.wait_ge(a_x_in, 16 * t + 16)
        act.activation(junk[:, :], xt[:, :], ACT.Square, scale=float(D) ** -0.5, accum_out=cols(MS_X)).then_inc(a_ss, 1)
        act.wait_ge(a_ss, t + 1)
        act.activation(cols(ROOT_X), cols(MS_X), ACT.Sqrt, bias=cols(EPS_C)).then_inc(a_root_x, 1)

    def act_produce(act, t):
        if first(t):
            act.wait_ge(eps_set, 1)
            act_mean_square(act, 0)
            act_produce_weights(act, range(0, 4))
        if has_tile(t):
            for b in range(2):
                act.wait_ge(a_turned, 2 * t + b + 1)
                act.activation(hx_hi[:, 4 * b:4 * b + 4, :], bank(b).rearrange("p (k q) -> p k q", k=4),
                               ACT.Copy).then_inc(a_hx_hi, 1)
            if first(t):
                act_produce_weights(act, range(4, 9))
                act_produce_setup(act)
            act.wait_ge(a_latent, t + 1)
            wait(act, a_k_shared, t)
            for i, (a, b, n) in enumerate(((0, CQ, CQ), (CQ, CQ + CKV, CKV), (CQ + CKV, DOWN, QK))):
                act.activation(junk_c[:, a:b], psum[:, 2 * N + a:2 * N + b], ACT.Square, scale=float(n) ** -0.5,
                               accum_out=cols(MS_C + i)).then_inc(a_latent_ss, 1)
            act.wait_ge(a_latent_ss, 3 * t + 3)
            act.activation(cols(ROOT_C, 2), cols(MS_C, 2), ACT.Sqrt, bias=cols(EPS_C)).then_inc(a_root_c, 1)
        if not first(t):
            wait(act, a_stored_q, 16 * t - 16)
            flat = qs[:, :, :].rearrange("p h n -> p (h n)")
            for b in range(3):
                act.wait_ge(a_q, 3 * t - 3 + b + 1)
                act.activation(flat[:, b * N:(b + 1) * N], bank(4 + b), ACT.Copy).then_inc(a_q_out, 1)
            act.wait_ge(a_q_out, 3 * t)
            act.activation(q_sq[:, :, :], qs[:, :, :], ACT.Square, scale=float(QK) ** -0.5).then_inc(a_q_sq, 1)
            wait(act, a_stored_k, 16 * t - 16)
            wait(act, a_stored_v, 16 * t - 16)
            for b in range(4):
                act.wait_ge(a_kv, 4 * t - 4 + b + 1)
                src = bank(KV_BANK[b]).rearrange("p (h n) -> p h n", h=2)
                act.activation(ks[:, 2 * b:2 * b + 2, 0:NOPE], src[:, :, 0:NOPE], ACT.Copy).then_inc(a_k_copied, 1)
                act.activation(vs[:, 2 * b:2 * b + 2, :], src[:, :, NOPE:], ACT.Copy).then_inc(a_kv_out, 1)
            act.wait_ge(a_k_copied, 4 * t)
            act.activation(k_sq[:, :, :], ks[:, :, 0:NOPE], ACT.Square, scale=float(QK) ** -0.5).then_inc(a_k_sq, 1)
        if has_next(t):
            act_mean_square(act, t + 1)
        if not first(t):
            act.wait_ge(a_summed, 2 * t - 1)
            act.activation(cols(ROOT_Q, H), cols(MS_Q, H), ACT.Sqrt, bias=cols(EPS_C)).then_inc(a_root_h, 1)
            act.wait_ge(a_summed, 2 * t)
            act.activation(cols(ROOT_K, H), cols(MS_K, H), ACT.Sqrt, bias=cols(EPS_C)).then_inc(a_root_h, 1)
        if has_tile(t):
            act.wait_ge(a_c_turned, t + 1)
            act.activation(ct_hi[:, :, :], psum[:, 3 * N:3 * N + NC * P].rearrange("p (k q) -> p k q", k=NC),
                           ACT.Copy).then_inc(a_ct_hi, 1)

    TWO_PI = 2.0 * np.pi
    PI_HI = 6.28125
    PI_MID = float(np.float32(TWO_PI - PI_HI))
    PI_LO = float(np.float32(TWO_PI - PI_HI - PI_MID))
    ROUND = 1.5 * 2.0 ** 23

    def dve_produce_setup(dve):
        link, _ = linker(dve, setup_own, 0)
        dve.wait_ge(pos_in, 48)
        link(dve.tensor_copy(posq[:, :], posq_i[:, :]))
        link(dve.tensor_copy(posk[:, :], posk_i[:, :]))
        raw_ang = ra[:, :, :]
        link(dve.tensor_tensor(raw_ang, posq[:, :].unsqueeze(2).to_broadcast([P, NT, HALF]),
                               freq[:, :].unsqueeze(1).to_broadcast([P, NT, HALF]), ALU.mult))
        for dst, quarter in ((ang, 0.0), (turn, 0.25)):
            n = rb[:, :, :]
            link(dve.tensor_scalar(n, raw_ang, 1.0 / TWO_PI, quarter, ALU.mult, ALU.add))
            link(dve.tensor_scalar(n, n, ROUND, None, ALU.add))
            link(dve.tensor_scalar(n, n, ROUND, None, ALU.subtract))
            link(dve.scalar_tensor_tensor(dst[:, :, :], n, -PI_HI, raw_ang, ALU.mult, ALU.add))
            link(dve.scalar_tensor_tensor(dst[:, :, :], n, -PI_MID, dst[:, :, :], ALU.mult, ALU.add))
            link(dve.scalar_tensor_tensor(dst[:, :, :], n, -PI_LO, dst[:, :, :], ALU.mult, ALU.add))
            if quarter:
                link(dve.tensor_scalar(dst[:, :, :], dst[:, :, :], float(np.float32(np.pi / 2)), None, ALU.add))
            dve.tensor_scalar(dst[:, :, :], dst[:, :, :], PI32, -PI32, ALU.min, ALU.max).then_inc(ang_done, 1)

    PI32 = float(np.nextafter(np.float32(np.pi), np.float32(0)))

    def dve_produce_weights(dve, units):
        for s in units:
            split_lo(dve, s, 0, piece(s, wd_lo, wq_lo, wk_lo), piece(s, wd_hi, wq_hi, wk_hi))

    def at(ap, t):
        return ap[:, bass.ds(t, 1), :].rearrange("p a n -> p (a n)")

    def dve_stream_norm(dve, t):
        link, _ = linker(dve, a_own, 5 * t)
        dve.wait_ge(a_root_x, t + 1)
        dve_rstd(dve, link, cols(R_X), cols(MS_X), cols(ROOT_X), cols(TMP))
        dve.scalar_tensor_tensor(xn[:, :], xt[:, :], cols(R_X), gain[:, 0:D], ALU.mult, ALU.mult).then_inc(a_xn, 1)

    def dve_produce(dve, t):
        if first(t):
            dve.wait_ge(consts, CONSTS)
            dve_stream_norm(dve, 0)
            dve_produce_weights(dve, range(0, 4))
        if has_tile(t):
            for b in range(2):
                dve.wait_ge(a_hx_hi, 2 * t + b + 1)
                dve.tensor_tensor(hx_lo[:, 4 * b:4 * b + 4, :], bank(b).rearrange("p (k q) -> p k q", k=4),
                                  f32(hx_hi[:, 4 * b:4 * b + 4, :]), ALU.subtract).then_inc(a_hx_lo, 1)
            if first(t):
                dve_produce_setup(dve)
                dve_produce_weights(dve, range(4, 9))
            link, _ = linker(dve, a_own_c, 6 * t)
            dve.wait_ge(a_root_c, t + 1)
            dve_rstd(dve, link, cols(R_C, 2), cols(MS_C, 2), cols(ROOT_C, 2), cols(TMP, 2))
            lat = psum[:, 2 * N:2 * N + DOWN]
            link(dve.tensor_tensor(c_sb[:, CQ + CKV:], lat[:, CQ + CKV:], g_k[:, NOPE:], ALU.mult))
            dve.scalar_tensor_tensor(c_sb[:, 0:CQ], lat[:, 0:CQ], cols(R_C), g_c[:, 0:CQ], ALU.mult, ALU.mult)
            dve.scalar_tensor_tensor(c_sb[:, CQ:CQ + CKV], lat[:, CQ:CQ + CKV], cols(R_C + 1), g_c[:, CQ:],
                                     ALU.mult, ALU.mult).then_inc(a_c, 1)
        link, _ = linker(dve, a_own_h, 12 * t - 12)
        if not first(t):
            dve.wait_ge(a_q_sq, t)
            dve.reduce_sum(cols(MS_Q, H), q_sq[:, :, :], AX.X).then_inc(a_summed, 1)
            dve.wait_ge(a_k_sq, t)
            link(dve.reduce_sum(cols(SS_K, H), k_sq[:, :, :], AX.X))
            dve.tensor_scalar(cols(MS_K, H), cols(SS_K, H), cols(MS_SHARED), None, ALU.add).then_inc(a_summed, 1)
        if has_next(t):
            dve_stream_norm(dve, t + 1)
        if not first(t):
            dve.wait_ge(a_root_h, 2 * t - 1)
            wait(dve, a_q_scaled, t - 1)
            dve_rstd(dve, link, cols(R_Q, H), cols(MS_Q, H), cols(ROOT_Q, H), cols(TMP, H))
            dve.tensor_copy(cols(R_Q2, H), cols(R_Q, H)).then_inc(a_q_factor, 1)
            dve.wait_ge(a_root_h, 2 * t)
            dve_rstd(dve, link, cols(R_K, H), cols(MS_K, H), cols(ROOT_K, H), cols(TMP, H))
            link(dve.tensor_tensor(ks[:, :, NOPE:], all_heads(rotk[:, :], ROPE), heads(cols(R_K, H), ROPE), ALU.mult))
            dve.tensor_tensor(ks[:, :, 0:NOPE], ks[:, :, 0:NOPE], heads(cols(R_K, H), NOPE), ALU.mult).then_inc(a_k_norm, 1)
        if has_tile(t):
            dve.wait_ge(a_ct_hi, t + 1)
            dve.tensor_tensor(ct_lo[:, :, :], psum[:, 3 * N:3 * N + NC * P].rearrange("p (k q) -> p k q", k=NC),
                              f32(ct_hi[:, :, :]), ALU.subtract).then_inc(a_ct_lo, 1)
            link, _ = linker(dve, a_own_r, 3 * t)
            one, two = c_sb[:, CQ + CKV:CQ + CKV + HALF], c_sb[:, CQ + CKV + HALF:]
            if first(t):
                dve.wait_ge(a_rope, 2)
            dve.tensor_tensor(tmp_r[:, 0:HALF], two, at(sin, t), ALU.mult)
            dve.tensor_tensor(tmp_r[:, HALF:], one, at(sin, t), ALU.mult)
            dve.tensor_tensor(rotk[:, 0:HALF], one, at(cos, t), ALU.mult)
            link(dve.tensor_tensor(rotk[:, HALF:], two, at(cos, t), ALU.mult))
            dve.tensor_tensor(rotk[:, 0:HALF], rotk[:, 0:HALF], tmp_r[:, 0:HALF], ALU.subtract)
            link(dve.tensor_tensor(rotk[:, HALF:], rotk[:, HALF:], tmp_r[:, HALF:], ALU.add))
            link(dve.tensor_copy(cols(MS_SHARED), cols(MS_KR)))
            dve.tensor_scalar(at(mask, t), posk[:, :], posq[:, bass.ds(t, 1)], -FAR, ALU.is_gt, ALU.mult).then_inc(a_k_shared, 1)

    def pool_setup(pool):
        pool.memset(ident[:, :], 0.0).then_inc(ident_done, 1)
        pool.wait_ge(ident_done, 1)
        pool.affine_select(out=ident[:, :], in_=ident[:, :], compare_op=ALU.not_equal, fill=1.0, base=0,
                           pattern=[[-1, P]], channel_multiplier=1).then_inc(ident_done, 1)
        pool.memset(cols(EPS_C), EPS).then_inc(eps_set, 1)
        for i, (s, n) in enumerate(((u_free, 4), (d_free, 4), (square_done, 2))):
            pool.memset(cols(88 + i), 0.0).then_inc(s, n)

    def pool_tables(pool):
        pool.wait_ge(consts, CONSTS)
        pool.wait_ge(a_rope, 2)
        g = [g_q[:, a:a + HALF].unsqueeze(1).to_broadcast([P, NT, HALF]) for a in (NOPE, NOPE + HALF)]
        pool.tensor_tensor(cos_1[:, :, :], cos[:, :, :], g[0], ALU.mult)
        pool.tensor_tensor(sin_1[:, :, :], sin[:, :, :], g[0], ALU.mult)
        pool.tensor_tensor(cos_2[:, :, :], cos[:, :, :], g[1], ALU.mult)
        pool.tensor_tensor(sin_2[:, :, :], sin[:, :, :], g[1], ALU.mult).then_inc(tables, 1)
        pool.wait_ge(tables, 1)

    def pool_produce(pool, t):
        if first(t):
            pool_tables(pool)
            return
        link, _ = linker(pool, a_pool_own, 2 * t - 2)
        pool.wait_ge(a_q_factor, t)
        pool.tensor_tensor(qs[:, :, :], qs[:, :, :], heads(cols(R_Q2, H), QK), ALU.mult).then_inc(a_q_scaled, 1)
        pool.wait_ge(a_q_scaled, t)
        pool.wait_ge(tables, 1)
        one, two = qs[:, :, NOPE:NOPE + HALF], qs[:, :, NOPE + HALF:]
        pool.tensor_tensor(ra[:, :, :], one, all_heads(at(cos_1, t - 1), HALF), ALU.mult)
        pool.tensor_tensor(rb[:, :, :], two, all_heads(at(sin_2, t - 1), HALF), ALU.mult)
        pool.tensor_tensor(rc[:, :, :], two, all_heads(at(cos_2, t - 1), HALF), ALU.mult)
        link(pool.tensor_tensor(rd[:, :, :], one, all_heads(at(sin_1, t - 1), HALF), ALU.mult))
        link(pool.tensor_tensor(one, ra[:, :, :], rb[:, :, :], ALU.subtract))
        pool.tensor_tensor(two, rc[:, :, :], rd[:, :, :], ALU.add).then_inc(a_q_rot, 1)

    q_in, v_in = sem("q_in"), sem("v_in")
    s_done, s_max, e_done = sem("s_done"), sem("s_max"), sem("e_done")
    t_done, t_hi, t_free = sem("t_done"), sem("t_hi"), sem("t_free")
    vh_done, vl_done = sem("vh_done"), sem("vl_done")
    r_inv = sem("r_inv")
    pv_done, o_done, oh_done, ol_done = sem("pv_done"), sem("o_done"), sem("oh_done"), sem("ol_done")
    b_own = sem("b_own")
    PREP = 8
    TG = {0: 0, 1: 2, 2: 4, 3: 6, "Q0": 8, "K": 10, "Q1": 14, "S0": 16, 4: 17, 5: 19, 6: 21, 7: 23, "S1": 25}
    TG_LAST = {0: 0, 1: 2, 2: 4, 3: 6, "S0": 8, 4: 9, 5: 11, 6: 13, 7: 15, "S1": 17}
    T_HEAD = 26
    T_ALL = PREP + T_HEAD * (H - 1) + 18

    MAX, BIAS, SUM, INV = 0, 8, 16, 32

    def sp_head_qk(sp, h):
        for dst, src in ((rq, qd), (rk, kd)):
            rows = src[:, bass.ds(h, 1), :].rearrange("(t p) a n -> p t (a n)", p=P)
            sp.dma_start(dst[:, :, 0:QK], rows).then_inc(q_in, 16)
            sp.dma_start(dst[:, :, QK:], rows[:, :, NOPE:]).then_inc(q_in, 16)

    def sp_head_v(sp, h):
        sp.dma_start(rv[:, :, :], vd[:, bass.ds(h, 1), :].rearrange("(t p) a n -> p t (a n)", p=P)).then_inc(v_in, 16)

    def sp_attention(sp):
        for s in (a_stored_q, a_stored_k, a_stored_v):
            sp.wait_ge(s, 16 * NT)
        sp.wait_ge(a_xn, NT)
        sp_head_qk(sp, 0)
        sp_head_v(sp, 0)
        sp.wait_ge(t_done, PREP)
        sp_head_qk(sp, 1)
        with sp.Fori(2, H) as h:
            sp.wait_ge(vl_done, h - 1)
            sp_head_v(sp, h - 1)
            sp.wait_ge(t_done, (h - 2) * T_HEAD + PREP + TG["Q1"] + 2)
            sp_head_qk(sp, h)
        sp.wait_ge(vl_done, H - 1)
        sp_head_v(sp, H - 1)
        sp.wait_ge(t_done, PREP + T_HEAD * (H - 2) + TG["Q1"] + 2)
        for j in range(RAW):
            load_unit(sp, O_BASE + j, 0, o_unit(j))

    def blocks(group, j):
        if group == "K":
            a, b = (0, NOPE) if j < 2 else (NOPE, 256)
            return [rk[:, 4 * (j % 2) + i, a:b] for i in range(4)]
        if group in ("Q0", "Q1"):
            half = int(group[1])
            a, b = (0, NOPE) if j == 0 else (NOPE, 256)
            return [rq[:, 4 * half + i, a:b] for i in range(4)]
        return [pr[:, group % 4, (4 * j + i) * P:(4 * j + i + 1) * P] for i in range(4)]

    def dests(group, j):
        if group == "K":
            c = slice(N * (j % 2), N * (j % 2) + N)
            return (k_hi[:, c], k_lo[:, c]) if j < 2 else (kr_hi[:, c], kr_lo[:, c])
        if group in ("Q0", "Q1"):
            c = slice(N * int(group[1]), N * int(group[1]) + N)
            return (q_hi[:, c], q_lo[:, c]) if j == 0 else (q_rope[:, c], None)
        c = slice(P * (group % 4), P * (group % 4) + P)
        return pt_hi[:, 4 * j:4 * j + 4, c], pt_lo[:, 4 * j:4 * j + 4, c]

    def groups_of(group):
        return 4 if group == "K" else 2

    def t_view(b, dst):
        return bank(b).rearrange("p (k q) -> p k q", k=4) if len(dst.shape) == 3 else bank(b)

    def gain_of(group, j):
        if group == "K" and j < 2:
            return gain_col[:, 1:2]
        return gain_col[:, 0:1] if group in ("Q0", "Q1") and j == 0 else None

    def t_bank(n):
        return (4, 5, 7)[n % 3]

    def t_wait(pe, base, n):
        wait(pe, t_free, base + n - (1 if n < 2 else 2))

    def pe_turn(pe, group, base, at0):
        for j in range(groups_of(group)):
            t_wait(pe, base, at0 + j)
            b = t_bank(at0 + j)
            for i, src in enumerate(blocks(group, j)):
                last = pe.transpose(psum[:, b * N + i * P:b * N + (i + 1) * P], src, ident[:, :])
            last.then_inc(t_done, 1)

    def act_turned(act, group, base, at0):
        for j in range(groups_of(group)):
            hi, _ = dests(group, j)
            g = gain_of(group, j)
            act.wait_ge(t_done, base + at0 + j + 1)
            act.activation(hi, t_view(t_bank(at0 + j), hi), ACT.Copy, scale=1.0 if g is None else g).then_inc(t_hi, 1)

    def dve_turned(dve, group, base, at0):
        for j in range(groups_of(group)):
            hi, lo = dests(group, j)
            g = gain_of(group, j)
            src = t_bank(at0 + j)
            dve.wait_ge(t_hi, base + at0 + j + 1)
            if lo is None:
                rows = slice(ROPE, P)
                dve.tensor_tensor(hi[rows, :], bank(src)[rows, :], f32(hi[rows, :]), ALU.subtract).then_inc(t_free, 1)
            elif g is None:
                dve.tensor_tensor(lo, t_view(src, hi), f32(hi), ALU.subtract).then_inc(t_free, 1)
            else:
                dve.scalar_tensor_tensor(lo, bank(src), g, f32(hi), ALU.mult, ALU.subtract).then_inc(t_free, 1)

    def pe_scores(pe, j, ready):
        if ready is not None:
            pe.wait_ge(t_free, ready)
        c = slice(P * j, P * j + P)
        for half in range(2):
            m = slice(N * half, N * half + N)
            dst = bank(2 * (j % 2) + half)
            pe.matmul(dst, q_hi[:, c], k_hi[:, m], start=True, stop=False)
            pe.matmul(dst, q_hi[:, c], k_lo[:, m], start=False, stop=False)
            pe.matmul(dst, q_lo[:, c], k_hi[:, m], start=False, stop=False)
            pe.matmul(dst, q_rope[:, c], kr_hi[:, m], start=False, stop=False)
            last = pe.matmul(dst, q_rope[:, c], kr_lo[:, m], start=False, stop=True)
        last.then_inc(s_done, 1)

    def pe_values(pe, h, half, base, tg):
        n = tg["S0" if half == 0 else "S1"]
        t_wait(pe, base, n)
        pe.wait_ge(r_inv, 2 * h + half + 1)
        for i in range(4):
            b = t_bank(n) * N + i * P
            last = pe.transpose(psum[:, b:b + P], cols(INV + 4 * half + i).to_broadcast([P, P]), ident[:, :])
        last.then_inc(t_done, 1)
        pe.wait_ge(t_free, base + tg[4 * half + 3] + 2)
        if half == 0:
            pe.wait_ge(vl_done, h + 1)
        passes(pe, bank(6), [(v_hi[:, k, :], v_lo[:, k, :], pt_hi[:, k, :], pt_lo[:, k, :])
                             for k in range(NT)]).then_inc(pv_done, 1)

    def pe_attention_head(pe, h, last):
        t0, tg = PREP + T_HEAD * h, TG_LAST if last else TG
        for j in range(2, NT):
            pe.wait_ge(s_max, NT * h + j - 1)
            pe_scores(pe, j, None)
            if j < 6:
                pe.wait_ge(e_done, NT * h + j - 1)
                pe_turn(pe, j - 2, t0, tg[j - 2])
            if j == 6 and not last:
                pe.wait_ge(q_in, 64 * h + 128)
                pe_turn(pe, "Q0", t0, tg["Q0"])
        if not last:
            pe_turn(pe, "K", t0, tg["K"])
            pe_turn(pe, "Q1", t0, tg["Q1"])
        pe_values(pe, h, 0, t0, tg)
        for j in range(4, NT):
            pe.wait_ge(e_done, NT * h + j + 1)
            pe_turn(pe, j, t0, tg[j])
            if not last and j in (4, 7):
                pe.wait_ge(s_max, NT * h + 7 + j // 7)
                pe_scores(pe, j // 7, t0 + tg["Q1"] + 2 if j == 4 else None)
        pe_values(pe, h, 1, t0, tg)

    def pe_attention(pe):
        pe.wait_ge(a_kv_out, 4 * NT)
        pe.wait_ge(q_in, 64)
        pe_turn(pe, "K", 0, 0)
        pe_turn(pe, "Q0", 0, 4)
        pe_turn(pe, "Q1", 0, 6)
        pe_scores(pe, 0, PREP)
        pe_scores(pe, 1, None)
        with pe.Fori(0, H - 1) as h:
            pe_attention_head(pe, h, False)
        pe_attention_head(pe, H - 1, True)

    def act_exp(act, h, j):
        act.wait_ge(s_max, NT * h + j + 1)
        act.activation(pr[:, j % 4, :], pr[:, j % 4, :], ACT.Exp, bias=cols(BIAS + j), scale=SCALE,
                       accum_out=cols(SUM + j)).then_inc(e_done, 1)

    def act_sums(act, half, base, tg):
        n = tg["S0" if half == 0 else "S1"]
        act.wait_ge(t_done, base + n + 1)
        act.activation(rsb[:, 0:N // 2], bank(t_bank(n))[:, 0:N // 2], ACT.Copy).then_inc(t_hi, 1)

    def act_out(act, h, half):
        act.wait_ge(o_done, 2 * h + half + 1)
        act.activation(h_hi[:, bass.ds(h, 1), N * half:N * half + N].rearrange("p a n -> p (a n)"), osc[:, :],
                       ACT.Copy).then_inc(oh_done, 1)

    def act_attention_head(act, h, last):
        t0, tg = PREP + T_HEAD * h, TG_LAST if last else TG
        for j in range(2, NT):
            if j < 6:
                act_turned(act, j - 2, t0, tg[j - 2])
            if j == 2:
                act.wait_ge(v_in, 16 * h + 16)
                act.activation(v_hi[:, :, :], rv[:, :, :], ACT.Copy).then_inc(vh_done, 1)
            if j == 6 and not last:
                act_turned(act, "Q0", t0, tg["Q0"])
            if j < 6:
                act_exp(act, h, j)
        if last:
            act.wait_ge(s_done, NT * H)
            for i in range(4):
                split_hi(act, O_BASE + i, 0, d_hi[:, i, :])
        else:
            act_turned(act, "K", t0, tg["K"])
            act_turned(act, "Q1", t0, tg["Q1"])
        act_exp(act, h, 6)
        act_exp(act, h, 7)
        act_sums(act, 0, t0, tg)
        for j in range(4, NT):
            act_turned(act, j, t0, tg[j])
            if j == 4:
                act_out(act, h, 0)
        act_sums(act, 1, t0, tg)
        if not last:
            act_exp(act, h + 1, 0)
            act_exp(act, h + 1, 1)
        act_out(act, h, 1)

    def act_attention(act):
        act_turned(act, "K", 0, 0)
        act_turned(act, "Q0", 0, 4)
        act_turned(act, "Q1", 0, 6)
        act_exp(act, 0, 0)
        act_exp(act, 0, 1)
        with act.Fori(0, H - 1) as h:
            act_attention_head(act, h, False)
        act_attention_head(act, H - 1, True)

    def dve_max(dve, h, j, turned):
        i = NT * h + j
        dve.wait_ge(s_done, i + 1)
        if turned is not None:
            dve.wait_ge(t_done, turned)
        dve.memset(cols(40 + j), 0.0).then_inc(b_own, 1)
        dve.tensor_tensor_reduce(out=pr[:, j % 4, :], in0=bank(2 * (j % 2), 2), in1=mask[:, j, :], scale=1.0,
                                 scalar=-3.0e38, op0=ALU.add, op1=ALU.max, accum_out=cols(MAX + j)).then_inc(b_own, 1)
        dve.wait_ge(b_own, 2 * i + 2)
        dve.tensor_scalar(cols(BIAS + j), cols(MAX + j), -SCALE, None, ALU.mult).then_inc(s_max, 1)

    def dve_row_sums(dve, h, half):
        dve.wait_ge(e_done, NT * h + 4 * half + 4)
        dve.reciprocal(cols(INV + 4 * half, 4), cols(SUM + 4 * half, 4)).then_inc(r_inv, 1)

    def dve_sums(dve, half, base, tg):
        n = tg["S0" if half == 0 else "S1"]
        dve.wait_ge(t_hi, base + n + 1)
        dve.tensor_copy(rsb[:, N // 2:], bank(t_bank(n))[:, N // 2:]).then_inc(t_free, 1)

    def dve_out(dve, h, half, base, tg):
        dve.wait_ge(pv_done, 2 * h + half + 1)
        dve.wait_ge(t_free, base + tg["S0" if half == 0 else "S1"] + 1)
        if half == 1:
            dve.wait_ge(ol_done, 2 * h + 1)
        dve.tensor_tensor(osc[:, :], bank(6), rsb[:, :], ALU.mult).then_inc(o_done, 1)

    def dve_out_lo(dve, h, half):
        col = slice(N * half, N * half + N)
        dve.wait_ge(oh_done, 2 * h + half + 1)
        dve.tensor_tensor(h_lo[:, bass.ds(h, 1), col].rearrange("p a n -> p (a n)"), osc[:, :],
                          f32(h_hi[:, bass.ds(h, 1), col].rearrange("p a n -> p (a n)")), ALU.subtract).then_inc(ol_done, 1)

    def dve_attention_head(dve, h, last):
        t0, tg = PREP + T_HEAD * h, TG_LAST if last else TG
        for j in range(2, NT):
            if j == 6 and not last:
                dve_turned(dve, "Q0", t0, tg["Q0"])
            if j < 6:
                dve_max(dve, h, j, t0 if j < 4 else t0 + tg[j - 4] + 2)
                dve_turned(dve, j - 2, t0, tg[j - 2])
            if j == 6:
                dve_row_sums(dve, h, 0)
            if j == 2:
                dve.wait_ge(vh_done, h + 1)
                dve.tensor_tensor(v_lo[:, :, :], rv[:, :, :], f32(v_hi[:, :, :]), ALU.subtract).then_inc(vl_done, 1)
        if last:
            for i in range(4):
                split_lo(dve, O_BASE + i, 0, d_lo[:, i, :], d_hi[:, i, :])
        else:
            dve_turned(dve, "K", t0, tg["K"])
            dve_turned(dve, "Q1", t0, tg["Q1"])
        dve_max(dve, h, 6, t0 + tg[2] + 2)
        dve_max(dve, h, 7, t0 + tg[3] + 2)
        dve_sums(dve, 0, t0, tg)
        dve_out(dve, h, 0, t0, tg)
        for j in range(4, NT):
            dve_turned(dve, j, t0, tg[j])
            if j == 4:
                dve_row_sums(dve, h, 1)
        dve_sums(dve, 1, t0, tg)
        if not last:
            dve_max(dve, h + 1, 0, t0 + tg[4] + 2)
            dve_max(dve, h + 1, 1, t0 + tg[5] + 2)
        dve_out_lo(dve, h, 0)
        dve_out(dve, h, 1, t0, tg)
        dve_out_lo(dve, h, 1)

    def dve_attention(dve):
        dve_turned(dve, "K", 0, 0)
        dve_turned(dve, "Q0", 0, 4)
        dve_turned(dve, "Q1", 0, 6)
        dve_max(dve, 0, 0, None)
        dve_max(dve, 0, 1, None)
        with dve.Fori(0, H - 1) as h:
            dve_attention_head(dve, h, False)
        dve_attention_head(dve, H - 1, True)

    u_done, u_free = sem("u_done"), sem("u_free")
    d_done, d_free = sem("d_done"), sem("d_free")
    square_done = sem("square_done")
    m_hi_done, m_lo_done = sem("m_hi_done"), sem("m_lo_done")
    x_in = [sem(f"x_in{t}") for t in range(NT)]
    gain_in = sem("gain_in")
    n_ss, n_root, n_own, n_xn, n_hi = sem("n_ss"), sem("n_root"), sem("n_own"), sem("n_xn"), sem("n_hi")
    c_own = sem("c_own")
    stored = sem("stored")

    def o_unit(j):
        return ins["attn_w_o"][0, P * j:P * j + P, :]

    def w1_unit(layer, j):
        return ins["mlp_w1"][layer, :, bass.ds(j * P, P)].rearrange("(k p) n -> p k n", p=P)

    def w2_unit(layer, j):
        return ins["mlp_w2"][layer, bass.ds(j * P, P), :]

    PARTS = (1, 2, 0)

    def in_unit(tile, part):
        return ins["conv_w_in"][0, :, bass.ds(PARTS[part] * D + tile * P, P)].rearrange("(k p) n -> p k n", p=P)

    def out_unit(j):
        return ins["conv_w_out"][0, bass.ds(j * P, P), :]

    MLP_CHUNKS = FF // N
    D_O = 0
    D_M1 = D_O + 16 + 32
    D_C = D_M1 + 16 * (MLP_CHUNKS - 1) + 32
    D_M2 = D_C + 16 + 32
    M1 = dict(unit=M1_BASE, down=D_M1, up=0, inner=0, square=0, norm=1, layer=0)
    C = dict(unit=C_BASE, down=D_C, up=64, inner=64, norm=2)
    M2 = dict(unit=M2_BASE, down=D_M2, up=64 + 48, inner=64 + 16, square=64, norm=3, layer=1)

    def order(hook):
        seq = []
        for t in range(NT):
            seq += [("D", t, 0), ("D", t, 1)]
            if hook and t:
                seq += [("T", t - 1, 0), ("T", t - 1, 1)]
        return seq + ([("T", NT - 1, 0), ("T", NT - 1, 1)] if hook else [])

    PLAIN = [("D", t, dh) for t in range(NT) for dh in range(2)]

    def pe_down(pe, base, seq, norm, stationary, moving, ready=None, first_group=0):
        for g, (kind, t, dh) in enumerate(seq, first_group):
            pe.wait_ge(d_free, base + g + 1)
            dst = bank(4 + g % 4)
            if kind == "D":
                if ready is not None and dh == 0 and t in (0, 4):
                    pe.wait_ge(m_lo_done, ready + 7 + t // 4)
                last = passes(pe, dst, [(*stationary(j, slice(P * t, P * t + P)), *moving(j, slice(N * dh, N * dh + N)))
                                        for j in range(4)])
            else:
                pe.wait_ge(n_xn, NT * norm + t + 1)
                for k in range(4):
                    last = pe.transpose(dst[:, k * P:(k + 1) * P], scr[:, t % 2, (4 * dh + k) * P:(4 * dh + k + 1) * P],
                                        ident[:, :])
            last.then_inc(d_done, 1)

    def dve_norm(dve, norm, t):
        i = NT * norm + t
        dve.wait_ge(n_root, i + 1)
        link, _ = linker(dve, n_own, 5 * i)
        dve_rstd(dve, link, cols(R_N), cols(MS_N + t % 2), cols(ROOT_N + t % 2), cols(TMP_N))
        if t == 0:
            dve.wait_ge(gain_in, 16 * norm + 16)
        dve.scalar_tensor_tensor(scr[:, t % 2, :], x[:, t, :], cols(R_N), gain[:, 0:D], ALU.mult, ALU.mult).then_inc(n_xn, 1)

    def dve_down(dve, base, seq, norm):
        for g, (kind, t, dh) in enumerate(seq):
            src = bank(4 + g % 4)
            if kind == "D":
                dst = x[:, t, N * dh:N * dh + N]
                dve.wait_ge(d_done, base + g + 1)
                if norm == 0 and dh == 0:
                    dve.wait_ge(x_in[t], 16)
                dve.tensor_tensor(dst, src, dst, ALU.add).then_inc(d_free, 1)
                if len(seq) > 16 and dh == 0 and t:
                    dve_norm(dve, norm, t - 1)
            else:
                if t == NT - 1 and dh == 0:
                    dve_norm(dve, norm, t)
                i = 2 * (NT * norm + t) + dh
                tok = slice(P * t, P * t + P)
                dve.wait_ge(n_hi, i + 1)
                dve.tensor_tensor(h_lo[:, 4 * dh:4 * dh + 4, tok], src.rearrange("p (k q) -> p k q", k=4),
                                  f32(h_hi[:, 4 * dh:4 * dh + 4, tok]), ALU.subtract).then_inc(d_free, 1)

    def act_down(act, base, seq, norm):
        for g, (kind, t, dh) in enumerate(seq):
            if kind == "D" and dh == 1:
                act.wait_ge(d_free, 4 + base + g + 1)
                act.activation(scr[:, t % 2, :], x[:, t, :], ACT.Square, scale=float(D) ** -0.5,
                               accum_out=cols(MS_N + t % 2)).then_inc(n_ss, 1)
                act.wait_ge(n_ss, NT * norm + t + 1)
                act.activation(cols(ROOT_N + t % 2), cols(MS_N + t % 2), ACT.Sqrt, bias=cols(EPS_C)).then_inc(n_root, 1)
            if kind == "T":
                act.wait_ge(d_done, base + g + 1)
                act.activation(h_hi[:, 4 * dh:4 * dh + 4, P * t:P * t + P],
                               bank(4 + g % 4).rearrange("p (k q) -> p k q", k=4), ACT.Copy).then_inc(n_hi, 1)

    def inner(j, tok):
        return m_hi[:, j, tok], m_lo[:, j, tok]

    def down_weights(j, feat):
        return d_hi[:, j, feat], d_lo[:, j, feat]

    def sp_out_proj(sp):
        sp.wait_ge(vl_done, H)
        for t in range(3):
            sp.dma_start(x[:, t, :], x_rows[:, t, :]).then_inc(x_in[t], 16)
        for j in range(4, 8):
            load_unit(sp, O_BASE + j, 0, o_unit(j))
        sp.wait_ge(ol_done, 2 * H)
        for t in range(3, NT):
            sp.dma_start(x[:, t, :], x_rows[:, t, :]).then_inc(x_in[t], 16)
        for j in range(2):
            load_unit(sp, O_BASE + 8 + j, 0, w1_unit(0, j))

    def pe_out_proj(pe):
        pe.wait_ge(t_free, T_ALL)
        pe.wait_ge(w_lo_done, O_BASE + 4)
        first_heads = lambda j, tok: (h_hi[:, j, tok], h_lo[:, j, tok])
        pe_down(pe, D_O, PLAIN[:2], 0, first_heads, down_weights)
        pe.wait_ge(o_done, 2 * H)
        pe_down(pe, D_O, PLAIN[2:], 0, first_heads, down_weights, first_group=2)
        pe.wait_ge(ol_done, 2 * H)
        pe.wait_ge(w_lo_done, O_BASE + 8)
        pe_down(pe, D_O + 16, order(True), 0, lambda j, tok: (h_hi[:, 4 + j, tok], h_lo[:, 4 + j, tok]),
                lambda j, feat: (o_hi[:, j, feat], o_lo[:, j, feat]))

    def act_out_proj(act):
        act.wait_ge(pv_done, 2 * H)
        for j in range(4):
            split_hi(act, O_BASE + 4 + j, 0, o_hi[:, j, :])
        for j in range(2):
            split_hi(act, O_BASE + 8 + j, 0, u_hi[:, j, :].rearrange("p (k n) -> p k n", k=ND))
        act_down(act, D_O + 16, order(True), 0)

    def dve_out_proj(dve):
        for j in range(4):
            split_lo(dve, O_BASE + 4 + j, 0, o_lo[:, j, :], o_hi[:, j, :])
        dve_down(dve, D_O, PLAIN, 0)
        for j in range(2):
            split_lo(dve, O_BASE + 8 + j, 0, u_lo[:, j, :].rearrange("p (k n) -> p k n", k=ND),
                     u_hi[:, j, :].rearrange("p (k n) -> p k n", k=ND))
        dve_down(dve, D_O + 16, order(True), 0)

    def u_view(ap, slot):
        return ap[:, slot, :].rearrange("p (k n) -> p k n", k=ND)

    def pe_up_unit(pe, slot, up, bank0, ready):
        pe.wait_ge(w_lo_done, ready)
        for half in range(2):
            pe.wait_ge(u_free, up + half + 1)
            tok = slice(N * half, N * half + N)
            passes(pe, bank(bank0 + half), [(u_hi[:, slot, P * k:P * k + P], u_lo[:, slot, P * k:P * k + P],
                                             h_hi[:, k, tok], h_lo[:, k, tok]) for k in range(ND)]).then_inc(u_done, 1)

    def mlp_unit(g, last, final):
        if final and last and g in (5, 7):
            return None
        offset = 5 if final and last and g == 6 else g
        return (offset, "D", g // 2) if g % 2 == 0 else (offset, "U", (g - 1) // 2 + 2)

    def mlp_loop(e, chunk):
        with e.Fori(0, MLP_CHUNKS - 1) as c:
            chunk(c, False)
        chunk(MLP_CHUNKS - 1, True)

    def sp_mlp(sp, st, then):
        def chunk(c, last):
            for g in range(8):
                unit = mlp_unit(g, last, then is None)
                if unit:
                    offset, kind, j = unit
                    src = (w2_unit(st["layer"], 4 * c + j) if kind == "D" else then(j - 4) if last and j > 3
                           else w1_unit(st["layer"], 4 * c + j))
                    load_unit(sp, st["unit"] + offset, 8 * c, src)
        mlp_loop(sp, chunk)

    def pe_mlp(pe, st, final):
        pe.wait_ge(d_free, 4 + st["down"])
        def chunk(c, last):
            for u in range(4):
                ready = st["unit"] + (-1, 0, 2, 4)[u]
                pe_up_unit(pe, u % 2, st["up"] + 8 * c + 2 * u, 2 * u % 4, 8 * c + ready)
            pe.wait_ge(w_lo_done, st["unit"] + 8 * c + (6 if final and last else 7))
            pe_down(pe, st["down"] + 16 * c, order(not final) if last else PLAIN, st["norm"], inner, down_weights,
                    st["inner"] + 8 * c)
        mlp_loop(pe, chunk)

    def act_mlp(act, st, final):
        def chunk(c, last):
            for g in range(8):
                up = st["up"] + 8 * c + g
                r = scr[:, 0, N * (g % 2):N * (g % 2) + N]
                act.wait_ge(u_done, up + 1)
                act.wait_ge(square_done, st["square"] + 8 * c + g + 1)
                act.activation(r, bank(g % 4), ACT.Relu).then_inc(u_free, 1)
                act.wait_ge(u_free, 4 + up + 1)
                act.activation(m_hi[:, g // 2, N * (g % 2):N * (g % 2) + N], r, ACT.Square).then_inc(m_hi_done, 1)
                unit = mlp_unit(g, last, final)
                if unit:
                    offset, kind, j = unit
                    split_hi(act, st["unit"] + offset, 8 * c, d_hi[:, j, :] if kind == "D" else u_view(u_hi, j % 2))
            if last and not final:
                act_down(act, st["down"] + 16 * c, order(True), st["norm"])
        mlp_loop(act, chunk)

    def dve_mlp(dve, st, final):
        def chunk(c, last):
            for g in range(8):
                span = slice(N * (g % 2), N * (g % 2) + N)
                square = scr[:, 1, span]
                dve.wait_ge(u_free, 4 + st["up"] + 8 * c + g + 1)
                dve.tensor_tensor(square, scr[:, 0, span], scr[:, 0, span], ALU.mult).then_inc(square_done, 1)
                dve.wait_ge(square_done, st["square"] + 8 * c + g + 3)
                dve.wait_ge(m_hi_done, st["inner"] + 8 * c + g + 1)
                dve.tensor_tensor(m_lo[:, g // 2, span], square, f32(m_hi[:, g // 2, span]), ALU.subtract).then_inc(m_lo_done, 1)
                unit = mlp_unit(g, last, final)
                if unit:
                    offset, kind, j = unit
                    hi, lo = (d_hi[:, j, :], d_lo[:, j, :]) if kind == "D" else (u_view(u_hi, j % 2), u_view(u_lo, j % 2))
                    split_lo(dve, st["unit"] + offset, 8 * c, lo, hi)
            dve_down(dve, st["down"] + 16 * c, order(not final) if last else PLAIN, st["norm"])
        mlp_loop(dve, chunk)

    def conv_pairs(e, pair, down):
        with e.Fori(0, 2) as r:
            pair(r, r, False)
        down(0)
        pair(2, 0, False)
        pair(3, 1, True)
        down(1)

    def d_slot(ap, r, i):
        return ap[:, bass.ds(2 * r + i // 3, 1), :].rearrange("p a n -> p (a n)")

    def sp_conv(sp, then):
        def pair(pp, r, last):
            for i in range(6):
                tile, part = (i + 2) // 3, (i + 2) % 3
                src = then(i - 4) if last and i > 3 else in_unit(2 * pp + tile, part)
                load_unit(sp, C["unit"] + i + i // 3, 8 * pp, src)
                if i % 3 == 2:
                    load_unit(sp, C["unit"] + i + i // 3 + 1, 8 * pp, out_unit(2 * pp + i // 3))
        for pp in range(4):
            pair(pp, pp % 2, pp == 3)

    def pe_conv(pe):
        pe.wait_ge(d_free, 4 + C["down"])

        def pair(pp, r, last):
            for i in range(6):
                ready = (-2, 0, 1, 2, 3, 5)[i]
                pe_up_unit(pe, i % 2, C["up"] + 12 * pp + 2 * i, 2 * i % 4, C["unit"] + 8 * pp + ready)

        def down(c):
            pe.wait_ge(w_lo_done, C["unit"] + 16 * c + 16)
            pe_down(pe, C["down"] + 16 * c, order(True) if c else PLAIN, C["norm"], inner, down_weights, C["inner"] + 8 * c)
        conv_pairs(pe, pair, down)

    def act_conv(act):
        def pair(pp, r, last):
            for i in range(6):
                if i % 3 == 2:
                    for half in range(2):
                        span = slice(N * half, N * half + N)
                        act.wait_ge(u_free, 4 + C["up"] + 12 * pp + 2 * i + half + 1)
                        act.activation(m_hi[:, bass.ds(2 * r + i // 3, 1), span].rearrange("p a n -> p (a n)"),
                                       scr[:, 1, span], ACT.Copy).then_inc(m_hi_done, 1)
                else:
                    act.wait_ge(u_done, C["up"] + 12 * pp + 2 * i + 2)
                split_hi(act, C["unit"] + i + i // 3, 8 * pp, u_view(u_hi, i % 2))
                if i % 3 == 2:
                    split_hi(act, C["unit"] + i + i // 3 + 1, 8 * pp, d_slot(d_hi, r, i))

        def down(c):
            if c:
                act_down(act, C["down"] + 16 * c, order(True), C["norm"])
        conv_pairs(act, pair, down)

    CONV_OWN = 6

    def dve_conv(dve):
        gate, conv, u = scr[:, 0, :], scr[:, 1, :], gain
        dve.memset(gain[:, 0:2], 0.0).then_inc(c_own, 1)

        def pair(pp, r, last):
            link, count = linker(dve, c_own, 1 + CONV_OWN * pp)
            for i in range(6):
                for half in range(2):
                    span = slice(N * half, N * half + N)
                    up = C["up"] + 12 * pp + 2 * i + half
                    src = bank((2 * i + half) % 4)
                    dve.wait_ge(u_done, up + 1)
                    if i % 3 == 0:
                        dve.tensor_copy(gate[:, span], src).then_inc(u_free, 1)
                    elif i % 3 == 1:
                        dve.wait_ge(u_free, 4 + up - 1)
                        dve.tensor_tensor(u[:, 2 + N * half:2 + N * half + N], src, gate[:, span], ALU.mult).then_inc(u_free, 1)
                    else:
                        dve.tensor_tensor(conv[:, span], src, conv[:, span], ALU.mult).then_inc(u_free, 1)
                        m = C["inner"] + 4 * pp + 2 * (i // 3) + half
                        dve.wait_ge(m_hi_done, m + 1)
                        j = bass.ds(2 * r + i // 3, 1)
                        dve.tensor_tensor(m_lo[:, j, span].rearrange("p a n -> p (a n)"), conv[:, span],
                                          f32(m_hi[:, j, span].rearrange("p a n -> p (a n)")), ALU.subtract).then_inc(m_lo_done, 1)
                if i % 3 == 1:
                    dve.wait_ge(u_free, 4 + C["up"] + 12 * pp + 2 * i + 2)
                    tap = [at(convw, w)[:, bass.ds(2 * pp + i // 3, 1)] for w in range(3)]
                    link(dve.tensor_scalar(conv, u[:, 2:2 + S], tap[2], None, ALU.mult))
                    link(dve.scalar_tensor_tensor(conv, u[:, 1:1 + S], tap[1], conv, ALU.mult, ALU.add))
                    link(dve.scalar_tensor_tensor(conv, u[:, 0:S], tap[0], conv, ALU.mult, ALU.add))
                split_lo(dve, C["unit"] + i + i // 3, 8 * pp, u_view(u_lo, i % 2), u_view(u_hi, i % 2))
                if i % 3 == 2:
                    split_lo(dve, C["unit"] + i + i // 3 + 1, 8 * pp, d_slot(d_lo, r, i), d_slot(d_hi, r, i))

        def down(c):
            dve_down(dve, C["down"] + 16 * c, order(True) if c else PLAIN, C["norm"])
        dve.wait_ge(c_own, 1)
        conv_pairs(dve, pair, down)

    with nc.Block() as block:
        @block.sync
        def _(sp):
            sp_produce_setup(sp)
            a_steps(sp, sp_produce)
            sp_attention(sp)
            sp_out_proj(sp)
            sp_mlp(sp, M1, lambda j: in_unit(0, j))
            sp_conv(sp, lambda j: w1_unit(1, j))
            sp_mlp(sp, M2, None)
            for t in range(NT):
                sp.wait_ge(d_free, 4 + M2["down"] + 16 * (MLP_CHUNKS - 1) + 2 * t + 2)
                sp.dma_start(out_rows[:, t, :], x[:, t, :]).then_inc(stored, 16)
            sp.wait_ge(stored, 16 * NT)

        @block.gpsimd
        def _(pool):
            pool_setup(pool)
            a_steps(pool, pool_produce)
            pool.wait_ge(a_xn, NT)
            pool.dma_start(gain[:, 0:D], spread(ins["g_mlp"][0, :])).then_inc(gain_in, 16)
            pool.wait_ge(n_xn, NT)
            pool.dma_start(gain[:, 0:D], spread(ins["g_mix"][1, :])).then_inc(gain_in, 16)
            pool.wait_ge(m_lo_done, C["inner"] + 16)
            pool.dma_start(gain[:, 0:D], spread(ins["g_mlp"][1, :])).then_inc(gain_in, 16)

        @block.scalar
        def _(act):
            a_steps(act, act_produce)
            act_attention(act)
            act_out_proj(act)
            act_mlp(act, M1, False)
            act_conv(act)
            act_mlp(act, M2, True)

        @block.vector
        def _(dve):
            a_steps(dve, dve_produce)
            dve_attention(dve)
            dve_out_proj(dve)
            dve_mlp(dve, M1, False)
            dve_conv(dve)
            dve_mlp(dve, M2, True)

        @block.tensor
        def _(pe):
            pe.wait_ge(ident_done, 2)
            a_steps(pe, pe_produce)
            pe_attention(pe)
            pe_out_proj(pe)
            pe_mlp(pe, M1, False)
            pe_conv(pe)
            pe_mlp(pe, M2, True)


_INS = ["x", "positions", "g_mix", "g_mlp", "attn_w_down", "attn_g_q_a", "attn_g_kv_a", "attn_w_uq", "attn_w_ukv",
        "attn_g_qnorm", "attn_g_knorm", "attn_w_o", "conv_w_in", "conv_w", "conv_w_out", "mlp_w1", "mlp_w2"]


def kernel(**inputs):
    import concourse.bacc as bacc
    from concourse.bass_utils import run_bass_kernel_spmd

    nc = bacc.Bacc("TRN2", target_bir_lowering=False, num_devices=1)
    arrays = {n: np.ascontiguousarray(inputs[n]) for n in _INS}
    arrays["inv_freq"] = (10000.0 ** (-np.arange(0, ROPE, 2) / ROPE)).astype(np.float32)
    ins = {n: nc.dram_tensor("in_" + n, a.shape, mybir.dt.from_np(a.dtype), kind="ExternalInput").ap()
           for n, a in arrays.items()}
    out = nc.dram_tensor("out", [1, S, D], F32, kind="ExternalOutput").ap()
    build(nc, ins, out)
    result = run_bass_kernel_spmd(nc, [{"in_" + n: a for n, a in arrays.items()}], core_ids=[0])
    return result.results[0]["out"]
```

```python
import numpy as np

import concourse.bass as bass
from concourse import mybir

F32 = mybir.dt.float32
F32R = mybir.dt.float32r
BF16 = mybir.dt.bfloat16
I32 = mybir.dt.int32
ALU = mybir.AluOpType
ACT = mybir.ActivationFunctionType
AX = mybir.AxisListType

P = 128
S = 1024
D = 1024
NT = S // P
ND = D // P
H = 8
NOPE, ROPE, VD = 128, 64, 128
HALF = ROPE // 2
QK = NOPE + ROPE
CQ, CKV = 256, 128
DOWN = CQ + CKV + ROPE
NC = (CQ + CKV) // P
FF = 4 * D
EPS = 1e-6
N = 512
UNIT = 1024
RAW = 4
SCALE = float(QK) ** -0.5
FAR = 1.6e38
PROD_UNITS = 9
KB = 1024


def build(nc, ins, out):
    top = nc.sbuf_base + 31 & ~31
    place = {}

    def sb(name, shape, dtype, offset):
        place[name] = nc.alloc_sbuf_tensor_at(name, shape, dtype, offset=top + offset)
        return place[name]

    X0, DS0, US0, M0, SC0, G0 = 0, 32 * KB, 64 * KB, 80 * KB, 112 * KB, 120 * KB
    HT0 = G0 + 4 * KB + 128
    RAW0 = HT0 + 64 * KB
    SM0 = RAW0 + 16 * KB
    x = sb("x", [P, NT, D], F32, X0)
    d_hi = sb("d_hi", [P, 4, UNIT], F32R, DS0)
    d_lo = sb("d_lo", [P, 4, UNIT], F32R, DS0 + 16 * KB)
    u_hi = sb("u_hi", [P, 2, UNIT], F32R, US0)
    u_lo = sb("u_lo", [P, 2, UNIT], F32R, US0 + 8 * KB)
    m_hi = sb("m_hi", [P, 4, S], F32R, M0)
    m_lo = sb("m_lo", [P, 4, S], F32R, M0 + 16 * KB)
    scr = sb("scr", [P, 2, D], F32, SC0)
    gain = sb("gain", [P, D + 2], F32, G0)
    h_hi = sb("h_hi", [P, ND, S], F32R, HT0)
    h_lo = sb("h_lo", [P, ND, S], F32R, HT0 + 32 * KB)
    raw = sb("raw", [P, RAW, UNIT], F32, RAW0)
    ident = sb("ident", [P, P], F32, SM0)
    stat = sb("stat", [P, 112], F32, SM0 + 1024)
    gain_col = sb("gain_col", [P, 2], F32, SM0 + 896)
    convw = sb("convw", [P, 3, ND], F32, SM0 + 768)
    o_hi = sb("o_hi", [P, 4, UNIT], F32R, M0)
    o_lo = sb("o_lo", [P, 4, UNIT], F32R, M0 + 16 * KB)
    rq = sb("rq", [P, NT, 256], F32, RAW0)
    rk = sb("rk", [P, NT, 256], F32, RAW0 + 8 * KB)
    rv = sb("rv", [P, NT, VD], F32, X0)
    osc = sb("osc", [P, N], F32, X0 + 12 * KB)
    rsb = sb("rsb", [P, N], F32, X0 + 14 * KB)
    pr = sb("pr", [P, 4, S], F32, X0 + 16 * KB)
    q_hi = sb("q_hi", [P, S], F32R, DS0)
    q_lo = sb("q_lo", [P, S], F32R, DS0 + 4 * KB)
    q_rope = sb("q_rope", [P, S], F32R, DS0 + 8 * KB)
    k_hi = sb("k_hi", [P, S], F32R, DS0 + 12 * KB)
    k_lo = sb("k_lo", [P, S], F32R, DS0 + 16 * KB)
    kr_hi = sb("kr_hi", [P, S], F32R, DS0 + 20 * KB)
    kr_lo = sb("kr_lo", [P, S], F32R, DS0 + 24 * KB)
    pt_hi = sb("pt_hi", [P, NT, N], F32R, US0)
    pt_lo = sb("pt_lo", [P, NT, N], F32R, US0 + 16 * KB)
    v_hi = sb("v_hi", [P, NT, VD], F32R, US0 + 32 * KB)
    v_lo = sb("v_lo", [P, NT, VD], F32R, US0 + 36 * KB)
    mask = sb("mask", [P, NT, S], BF16, US0 + 40 * KB)
    xt = sb("xt", [P, D], F32, X0)
    xn = sb("xn", [P, D], F32, X0 + 8 * KB)
    posk_i = sb("posk_i", [P, S], I32, HT0 + 53 * KB)
    cos_1 = sb("cos_1", [P, NT, HALF], F32, X0 + 12 * KB)
    sin_1 = sb("sin_1", [P, NT, HALF], F32, X0 + 13 * KB)
    cos_2 = sb("cos_2", [P, NT, HALF], F32, X0 + 14 * KB)
    sin_2 = sb("sin_2", [P, NT, HALF], F32, X0 + 15 * KB)
    posk = sb("posk", [P, S], F32, X0 + 16 * KB)
    cos = sb("cos", [P, NT, HALF], F32, X0 + 20 * KB)
    sin = sb("sin", [P, NT, HALF], F32, X0 + 21 * KB)
    ang = sb("ang", [P, NT, HALF], F32, X0 + 22 * KB)
    turn = sb("turn", [P, NT, HALF], F32, X0 + 23 * KB)
    g_c = sb("g_c", [P, CQ + CKV], F32, X0 + 24 * KB)
    g_q = sb("g_q", [P, QK], F32, X0 + 24 * KB + 1536)
    g_k = sb("g_k", [P, QK], F32, X0 + 24 * KB + 2304)
    freq = sb("freq", [P, HALF], F32, X0 + 24 * KB + 3072)
    posq_i = sb("posq_i", [P, NT], I32, X0 + 24 * KB + 3200)
    posq = sb("posq", [P, NT], F32, X0 + 24 * KB + 3264)
    c_sb = sb("c_sb", [P, DOWN], F32, X0 + 24 * KB + 3328)
    rotk = sb("rotk", [P, ROPE], F32, X0 + 24 * KB + 5120)
    tmp_r = sb("tmp_r", [P, ROPE], F32, X0 + 24 * KB + 5376)
    wd_hi = sb("wd_hi", [P, ND, DOWN], F32R, DS0)
    wd_lo = sb("wd_lo", [P, ND, DOWN], F32R, DS0 + 14 * KB)
    wq_hi = sb("wq_hi", [P, 2, H * QK], F32R, US0)
    wq_lo = sb("wq_lo", [P, 2, H * QK], F32R, US0 + 12 * KB)
    wk_hi = sb("wk_hi", [P, H * (NOPE + VD)], F32R, US0 + 24 * KB)
    wk_lo = sb("wk_lo", [P, H * (NOPE + VD)], F32R, US0 + 32 * KB)
    hx_hi = sb("hx_hi", [P, ND, P], F32R, HT0)
    hx_lo = sb("hx_lo", [P, ND, P], F32R, HT0 + 4 * KB)
    ct_hi = sb("ct_hi", [P, NC, P], F32R, HT0 + 8 * KB)
    ct_lo = sb("ct_lo", [P, NC, P], F32R, HT0 + 8 * KB + 1536)
    qs, ks, vs = [[sb(f"{name}{i}", [P, H, n], F32, HT0 + (11 + 36 * i + k) * KB) for i in range(2)]
                  for name, n, k in (("qs", QK, 0), ("ks", QK, 6), ("vs", VD, 12))]
    q_sq = sb("q_sq", [P, H, QK], F32, HT0 + 27 * KB)
    k_sq = sb("k_sq", [P, H, NOPE], F32, HT0 + 33 * KB)
    junk = sb("junk", [P, D], F32, HT0 + 37 * KB)
    junk_c = sb("junk_c", [P, DOWN], F32, HT0 + 45 * KB)
    ra = sb("ra", [P, H, HALF], F32, HT0 + 41 * KB)
    rb = sb("rb", [P, H, HALF], F32, HT0 + 42 * KB)
    rc = sb("rc", [P, H, HALF], F32, HT0 + 43 * KB)
    rd = sb("rd", [P, H, HALF], F32, HT0 + 44 * KB)

    psum = nc.alloc_psum_tensor("psum", [P, 8 * N], F32)
    qd = nc.dram_tensor("q_heads", [S, H, QK], F32, kind="Internal").ap()
    kd = nc.dram_tensor("k_heads", [S, H, QK], F32, kind="Internal").ap()
    vd = nc.dram_tensor("v_heads", [S, H, VD], F32, kind="Internal").ap()

    def bank(b, n=1):
        return psum[:, b * N:(b + n) * N]

    def f32(ap):
        return ap.bitcast(F32)


    def sem(name):
        return nc.alloc_semaphore(name)

    def wait(e, s, value):
        if not isinstance(value, int) or value > 0:
            e.wait_ge(s, value)

    def linker(e, s, base):
        count = [0]

        def link(ins):
            count[0] += 1
            ins.then_inc(s, 1)
            e.wait_ge(s, base + count[0])
        return link, count

    def passes(pe, dst, terms):
        for n, (s_hi, s_lo, m_hi_, m_lo_) in enumerate(terms):
            pe.matmul(dst, s_hi, m_hi_, start=n == 0, stop=False)
            pe.matmul(dst, s_hi, m_lo_, start=False, stop=False)
            last = pe.matmul(dst, s_lo, m_hi_, start=False, stop=n == len(terms) - 1)
        return last

    x_rows = ins["x"].rearrange("a (t p) d -> p (a t) d", p=P)
    out_rows = out.rearrange("a (t p) d -> p (a t) d", p=P)

    def spread(src):
        return bass.AP(tensor=src.tensor, offset=src.offset, ap=[[0, P], [1, src.shape[0]]])

    def heads(ap, n):
        return ap.unsqueeze(2).to_broadcast([P, H, n])

    def all_heads(ap, n):
        return ap.unsqueeze(1).to_broadcast([P, H, n])

    raw_in = [sem(f"raw_in{i}") for i in range(RAW)]
    w_hi_done, w_lo_done = sem("w_hi_done"), sem("w_lo_done")
    O_BASE = PROD_UNITS
    M1_BASE = O_BASE + 8 + 2
    C_BASE = M1_BASE + 8 * (FF // N)
    M2_BASE = C_BASE + 16 * 2

    def like(slot, ap):
        shape = list(ap.shape)
        v = raw[:, slot, 0:shape[1] * (shape[2] if len(shape) == 3 else 1)]
        return v.rearrange("p (a b) -> p a b", a=shape[1]) if len(shape) == 3 else v

    def load_unit(sp, s, more, src):
        wait(sp, w_lo_done, s + more - RAW + 1)
        sp.dma_start(like(s % RAW, src), src).then_inc(raw_in[s % RAW], 16)

    def split_hi(act, s, more, dst):
        act.wait_ge(raw_in[s % RAW], 16 * (s // RAW + 1) + more * (16 // RAW))
        act.activation(dst, like(s % RAW, dst), ACT.Copy).then_inc(w_hi_done, 1)

    def split_lo(dve, s, more, dst, hi):
        dve.wait_ge(w_hi_done, s + more + 1)
        dve.tensor_tensor(dst, like(s % RAW, dst), f32(hi), ALU.subtract).then_inc(w_lo_done, 1)

    def dve_rstd(dve, link, dst, mean, root, tmp):
        link(dve.reciprocal(dst, root))
        link(dve.tensor_tensor(tmp, dst, dst, ALU.mult))
        link(dve.scalar_tensor_tensor(tmp, mean, EPS, tmp, ALU.add, ALU.mult))
        link(dve.tensor_scalar(tmp, tmp, -0.5, 1.5, ALU.mult, ALU.add))
        link(dve.tensor_tensor(dst, dst, tmp, ALU.mult))

    def cols(a, n=1):
        return stat[:, a:a + n]

    MS_X, ROOT_X, R_X, MS_C, MS_KR, ROOT_C, R_C, TMP = 0, 1, 2, 3, 5, 6, 8, 10
    MS_Q, ROOT_Q, R_Q, SS_K, MS_K, ROOT_K, R_K = 18, 26, 34, 42, 50, 58, 66
    MS_SHARED, R_Q2 = 74, 92
    MS_N, ROOT_N, R_N, TMP_N, EPS_C = 80, 82, 84, 85, 86
    SPARE = (87, 88, 89, 90, 91, 100, 101, 102, 103, 104)

    gain_x_in, gain_c_in = sem("gain_x_in"), sem("gain_c_in")
    consts = sem("consts")
    pos_in, posk_in = sem("pos_in"), sem("posk_in")
    eps_set, ident_done, tables = sem("eps_set"), sem("ident_done"), sem("tables")
    a_x_in, a_ss, a_root_x, a_xn = sem("a_x_in"), sem("a_ss"), sem("a_root_x"), sem("a_xn")
    a_turned, a_hx_hi, a_hx_lo = sem("a_turned"), sem("a_hx_hi"), sem("a_hx_lo")
    a_latent, a_latent_ss, a_root_c, a_c = sem("a_latent"), sem("a_latent_ss"), sem("a_root_c"), sem("a_c")
    a_c_turned, a_ct_hi, a_ct_lo = sem("a_c_turned"), sem("a_ct_hi"), sem("a_ct_lo")
    a_q, a_q_out, a_q_sq, a_q_summed = sem("a_q"), sem("a_q_out"), sem("a_q_sq"), sem("a_q_summed")
    a_root_q, a_q_factor, a_q_scaled = sem("a_root_q"), sem("a_q_factor"), sem("a_q_scaled")
    a_q_rot, a_stored_q = sem("a_q_rot"), [sem("a_stored_q0"), sem("a_stored_q1")]
    a_kv, a_k_copied, a_kv_out, a_k_sq = sem("a_kv"), sem("a_k_copied"), sem("a_kv_out"), sem("a_k_sq")
    a_k_summed, a_root_k, a_k_norm = sem("a_k_summed"), sem("a_root_k"), sem("a_k_norm")
    a_stored_k, a_stored_v = ([sem(f"a_stored_{n}{i}") for i in range(2)] for n in "kv")
    a_k_shared, a_rope = sem("a_k_shared"), sem("a_rope")
    q_row_own = sem("q_row_own")
    k_row_done, q_row_done = sem("k_row_done"), sem("q_row_done")
    a_own, a_own_c, a_own_q, a_own_k, a_own_r, a_pool_own = (
        sem("a_own"), sem("a_own_c"), sem("a_own_q"), sem("a_own_k"), sem("a_own_r"), sem("a_pool_own"))
    setup_own, ang_done = sem("setup_own"), sem("ang_done")
    CONSTS = 16 * 6

    w_down = ins["attn_w_down"][0, :, :].rearrange("(k p) n -> p k n", p=P)
    w_uq = ins["attn_w_uq"][0, :, :].rearrange("(k p) n -> p k n", p=P)
    w_ukv = ins["attn_w_ukv"][0, :, :]

    def piece(s, down, uq, ukv):
        if s < 4:
            return down[:, 2 * s:2 * s + 2, :]
        if s < 7:
            return uq[:, :, N * (s - 4):N * (s - 3)]
        return ukv[:, UNIT * (s - 7):UNIT * (s - 6)]

    def a_store(ap, t):
        return ap[bass.ds(t * P, P), :, :]

    def sp_produce_setup(sp):
        sp.dma_start(xt[:, :], x_rows[:, 0, :]).then_inc(a_x_in, 16)
        with nc.allow_non_contiguous_dma("one position per partition"):
            sp.dma_start(posq_i[:, :], ins["positions"].rearrange("a (t p) -> p (a t)", p=P)).then_inc(pos_in, 16)
        sp.dma_start(freq[:, :], spread(ins["inv_freq"])).then_inc(pos_in, 16)
        sp.dma_start(gain[:, 0:D], spread(ins["g_mix"][0, :])).then_inc(gain_x_in, 16)
        for s in range(RAW):
            load_unit(sp, s, 0, piece(s, w_down, w_uq, w_ukv))

    def pool_loads(pool):
        pool.dma_start(g_c[:, 0:CQ], spread(ins["attn_g_q_a"][0, :])).then_inc(gain_c_in, 16)
        pool.dma_start(g_c[:, CQ:], spread(ins["attn_g_kv_a"][0, :])).then_inc(gain_c_in, 16)
        pool.dma_start(g_k[:, :], spread(ins["attn_g_knorm"][0, :])).then_inc(gain_c_in, 16)
        pool_angles(pool)
        pool.dma_start(g_q[:, :], spread(ins["attn_g_qnorm"][0, :])).then_inc(consts, 16)
        with nc.allow_non_contiguous_dma("one gain or tap per partition"):
            for i, name in enumerate(("attn_g_qnorm", "attn_g_knorm")):
                pool.dma_start(gain_col[:, i:i + 1], ins[name][0, 0:NOPE].rearrange("(p a) -> p a", a=1)).then_inc(consts, 16)
            for w in range(3):
                pool.dma_start(convw[:, w, :], ins["conv_w"][0, w, :].rearrange("(k p) -> p k", p=P)).then_inc(consts, 16)

    def a_steps(e, step):
        for t in range(-1, 2):
            step(e, t, t % 2)
        with e.Fori(1, NT // 2 - 1) as r:
            step(e, 2 * r, 0)
            step(e, 2 * r + 1, 1)
        for t in range(NT - 2, NT + 2):
            step(e, t, t % 2)

    def has(i):
        return not isinstance(i, int) or 0 <= i < NT

    def is_step(t, n):
        return isinstance(t, int) and t == n

    def all_stored(sp, stored_sems, tiles):
        for i in range(2):
            sp.wait_ge(stored_sems[i], 16 + 16 * ((tiles + 1 - i) // 2))

    def sp_produce(sp, t, odd):
        if is_step(t, -1):
            sp_produce_setup(sp)
        if has(t + 2) and not is_step(t, -2):
            sp.wait_ge(a_xn, t + 2)
            sp.dma_start(xt[:, :], x_rows[:, bass.ds(t + 2, 1), :].rearrange("p a d -> p (a d)")).then_inc(a_x_in, 16)
        if is_step(t, -1):
            for s in range(RAW, PROD_UNITS):
                load_unit(sp, s, 0, piece(s, w_down, w_uq, w_ukv))
                if s == RAW:
                    sp.dma_start(posk_i[:, :], spread(ins["positions"][0, :])).then_inc(posk_in, 16)
        if is_step(t, NT):
            all_stored(sp, a_stored_k, NT - 1)
            sp_rows(sp, rk, kd, 0, 0, NT - 1, q_in)
            sp_rows(sp, rq, qd, 0, 0, 4, q_in)
        if has(t - 1):
            sp.wait_ge(a_kv_out, 4 * t)
            sp.dma_start(a_store(vd, t - 1), vs[1 - odd][:, :, :]).then_inc(a_stored_v[1 - odd], 16)
        if has(t - 2):
            sp.wait_ge(a_q_rot, t - 1)
            sp.dma_start(a_store(qd, t - 2), qs[odd][:, :, :]).then_inc(a_stored_q[odd], 16)
        if has(t - 1):
            sp.wait_ge(a_k_norm, t)
            sp.dma_start(a_store(kd, t - 1), ks[1 - odd][:, :, :]).then_inc(a_stored_k[1 - odd], 16)
        if is_step(t, NT):
            all_stored(sp, a_stored_q, NT - 1)
            sp_rows(sp, rq, qd, 0, 4, NT - 1, late_rows_in)

    def pe_produce(pe, t, odd):
        if has(t):
            wait(pe, a_hx_lo, 2 * t + 2)
            if is_step(t, 0):
                for k in range(ND):
                    if k % 2 == 0:
                        pe.wait_ge(w_lo_done, k // 2 + 1)
                    dst = psum[:, 2 * N:2 * N + DOWN]
                    pe.matmul(dst, hx_hi[:, k, :], wd_hi[:, k, :], start=k == 0, stop=False)
                    pe.matmul(dst, hx_hi[:, k, :], wd_lo[:, k, :], start=False, stop=False)
                    last = pe.matmul(dst, hx_lo[:, k, :], wd_hi[:, k, :], start=False, stop=k == ND - 1)
            else:
                last = passes(pe, psum[:, 2 * N:2 * N + DOWN],
                              [(hx_hi[:, k, :], hx_lo[:, k, :], wd_hi[:, k, :], wd_lo[:, k, :]) for k in range(ND)])
            last.then_inc(a_latent, 1)
        if has(t + 1):
            pe.wait_ge(a_xn, t + 2)
            for b in range(2):
                for k in range(4):
                    last = pe.transpose(psum[:, b * N + k * P:b * N + (k + 1) * P],
                                        xn[:, (4 * b + k) * P:(4 * b + k + 1) * P], ident[:, :])
                last.then_inc(a_turned, 1)
        if has(t - 1):
            pe.wait_ge(a_ct_lo, t)
            if is_step(t, 1):
                pe.wait_ge(w_lo_done, PROD_UNITS)
            for b in range(4):
                wait(pe, a_q_out if b < 3 else a_kv_out, 3 * t - 3 - 2 + b if b < 3 else 4 * t - 4)
                passes(pe, bank(4 + b), [(ct_hi[:, 2, :], ct_lo[:, 2, :], wk_hi[:, b * N:(b + 1) * N],
                                          wk_lo[:, b * N:(b + 1) * N])]).then_inc(a_kv, 1)
            for b in range(3):
                pe.wait_ge(a_kv_out, 4 * t - 4 + b + 1)
                passes(pe, bank(4 + b), [(ct_hi[:, k, :], ct_lo[:, k, :], wq_hi[:, k, b * N:(b + 1) * N],
                                          wq_lo[:, k, b * N:(b + 1) * N]) for k in range(2)]).then_inc(a_q, 1)
        if has(t):
            pe.wait_ge(a_c, t + 1)
            for k in range(NC):
                last = pe.transpose(psum[:, 3 * N + k * P:3 * N + (k + 1) * P], c_sb[:, k * P:(k + 1) * P], ident[:, :])
            last.then_inc(a_c_turned, 1)

    def act_produce_setup(act):
        act.wait_ge(ang_done, 1)
        act.activation(sin[:, :, :], ang[:, :, :], ACT.Sin).then_inc(a_rope, 1)
        act.wait_ge(ang_done, 2)
        act.activation(cos[:, :, :], turn[:, :, :], ACT.Sin).then_inc(a_rope, 1)

    def act_produce_weights(act, units):
        for s in units:
            split_hi(act, s, 0, piece(s, wd_hi, wq_hi, wk_hi))

    def act_mean_square(act, t):
        act.wait_ge(a_x_in, 16 * t + 16)
        act.activation(junk[:, :], xt[:, :], ACT.Square, scale=float(D) ** -0.5, accum_out=cols(MS_X)).then_inc(a_ss, 1)
        act.wait_ge(a_ss, t + 1)
        act.activation(cols(ROOT_X), cols(MS_X), ACT.Sqrt, bias=cols(EPS_C)).then_inc(a_root_x, 1)

    def act_produce(act, t, odd):
        if is_step(t, -1):
            act.wait_ge(eps_set, 1)
            act_mean_square(act, 0)
            act_produce_weights(act, range(0, 2))
        if is_step(t, 0):
            act_produce_weights(act, range(4, 7))
        if has(t - 2):
            act.wait_ge(a_q_summed, t - 1)
            act.activation(cols(ROOT_Q, H), cols(MS_Q, H), ACT.Sqrt, bias=cols(EPS_C)).then_inc(a_root_q, 1)
        if has(t):
            act.wait_ge(a_latent, t + 1)
            wait(act, a_k_shared, t)
            for i, (a, b, n) in enumerate(((0, CQ, CQ), (CQ, CQ + CKV, CKV), (CQ + CKV, DOWN, QK))):
                act.activation(junk_c[:, a:b], psum[:, 2 * N + a:2 * N + b], ACT.Square, scale=float(n) ** -0.5,
                               accum_out=cols(MS_C + i)).then_inc(a_latent_ss, 1)
            act.wait_ge(a_latent_ss, 3 * t + 3)
            act.activation(cols(ROOT_C, 2), cols(MS_C, 2), ACT.Sqrt, bias=cols(EPS_C)).then_inc(a_root_c, 1)
        if has(t + 1):
            for b in range(2):
                act.wait_ge(a_turned, 2 * t + 2 + b + 1)
                act.activation(hx_hi[:, 4 * b:4 * b + 4, :], bank(b).rearrange("p (k q) -> p k q", k=4),
                               ACT.Copy).then_inc(a_hx_hi, 1)
        if is_step(t, -1):
            act_produce_weights(act, range(2, 4))
        if is_step(t, 0):
            act_produce_weights(act, range(7, 9))
        if has(t + 2):
            act_mean_square(act, t + 2)
        if is_step(t, 0):
            act_produce_setup(act)
        if has(t - 1):
            i = 1 - odd
            act.wait_ge(a_stored_k[i], 16 + 8 * (t - 2 + odd))
            act.wait_ge(a_stored_v[i], 16 + 8 * (t - 2 + odd))
            for b in range(4):
                act.wait_ge(a_kv, 4 * t - 4 + b + 1)
                src = bank(4 + b).rearrange("p (h n) -> p h n", h=2)
                act.activation(ks[i][:, 2 * b:2 * b + 2, 0:NOPE], src[:, :, 0:NOPE], ACT.Copy).then_inc(a_k_copied, 1)
                act.activation(vs[i][:, 2 * b:2 * b + 2, :], src[:, :, NOPE:], ACT.Copy).then_inc(a_kv_out, 1)
            act.wait_ge(a_k_copied, 4 * t)
            act.activation(k_sq[:, :, :], ks[i][:, :, 0:NOPE], ACT.Square, scale=float(QK) ** -0.5).then_inc(a_k_sq, 1)
            act.wait_ge(a_stored_q[i], 16 + 8 * (t - 2 + odd))
            flat = qs[i][:, :, :].rearrange("p h n -> p (h n)")
            for b in range(3):
                act.wait_ge(a_q, 3 * t - 3 + b + 1)
                act.activation(flat[:, b * N:(b + 1) * N], bank(4 + b), ACT.Copy).then_inc(a_q_out, 1)
                if b == 1:
                    act.wait_ge(a_k_summed, t)
                    act.activation(cols(ROOT_K, H), cols(MS_K, H), ACT.Sqrt, bias=cols(EPS_C)).then_inc(a_root_k, 1)
        if has(t):
            act.wait_ge(a_c_turned, t + 1)
            act.activation(ct_hi[:, :, :], psum[:, 3 * N:3 * N + NC * P].rearrange("p (k q) -> p k q", k=NC),
                           ACT.Copy).then_inc(a_ct_hi, 1)
        if has(t - 1):
            act.wait_ge(a_q_out, 3 * t)
            act.activation(q_sq[:, :, :], qs[1 - odd][:, :, :], ACT.Square, scale=float(QK) ** -0.5).then_inc(a_q_sq, 1)

    TWO_PI = 2.0 * np.pi
    PI_HI = 6.28125
    PI_MID = float(np.float32(TWO_PI - PI_HI))
    PI_LO = float(np.float32(TWO_PI - PI_HI - PI_MID))
    ROUND = 1.5 * 2.0 ** 23

    def pool_angles(pool):
        link, _ = linker(pool, setup_own, 0)
        pool.wait_ge(pos_in, 32)
        link(pool.tensor_copy(posq[:, :], posq_i[:, :]))
        raw_ang = ra[:, :, :]
        link(pool.tensor_tensor(raw_ang, posq[:, :].unsqueeze(2).to_broadcast([P, NT, HALF]),
                               freq[:, :].unsqueeze(1).to_broadcast([P, NT, HALF]), ALU.mult))
        for dst, quarter in ((ang, 0.0), (turn, 0.25)):
            n, turns = rb[:, :, :], rc[:, :, :]
            link(pool.tensor_scalar(n, raw_ang, 1.0 / TWO_PI, quarter, ALU.mult, ALU.add))
            link(pool.tensor_scalar(n, n, ROUND, None, ALU.add))
            link(pool.tensor_scalar(n, n, ROUND, None, ALU.subtract))
            link(pool.tensor_scalar(turns, n, -PI_HI, None, ALU.mult))
            link(pool.tensor_tensor(dst[:, :, :], turns, raw_ang, ALU.add))
            link(pool.tensor_scalar(turns, n, -PI_MID, None, ALU.mult))
            link(pool.tensor_tensor(dst[:, :, :], turns, dst[:, :, :], ALU.add))
            link(pool.tensor_scalar(turns, n, -PI_LO, None, ALU.mult))
            link(pool.tensor_tensor(dst[:, :, :], turns, dst[:, :, :], ALU.add))
            if quarter:
                link(pool.tensor_scalar(dst[:, :, :], dst[:, :, :], float(np.float32(np.pi / 2)), None, ALU.add))
            pool.tensor_scalar(dst[:, :, :], dst[:, :, :], PI32, -PI32, ALU.min, ALU.max).then_inc(ang_done, 1)

    PI32 = float(np.nextafter(np.float32(np.pi), np.float32(0)))

    def dve_produce_weights(dve, units):
        for s in units:
            split_lo(dve, s, 0, piece(s, wd_lo, wq_lo, wk_lo), piece(s, wd_hi, wq_hi, wk_hi))

    def at(ap, t):
        return ap[:, bass.ds(t, 1), :].rearrange("p a n -> p (a n)")

    def dve_stream_norm(dve, t):
        link, _ = linker(dve, a_own, 5 * t)
        dve.wait_ge(a_root_x, t + 1)
        dve_rstd(dve, link, cols(R_X), cols(MS_X), cols(ROOT_X), cols(TMP))
        dve.scalar_tensor_tensor(xn[:, :], xt[:, :], cols(R_X), gain[:, 0:D], ALU.mult, ALU.mult).then_inc(a_xn, 1)

    def dve_scale_keys(dve, k, link):
        link(dve.tensor_tensor(k[:, :, NOPE:], all_heads(rotk[:, :], ROPE), heads(cols(R_K, H), ROPE), ALU.mult))
        dve.tensor_tensor(k[:, :, 0:NOPE], k[:, :, 0:NOPE], heads(cols(R_K, H), NOPE), ALU.mult).then_inc(a_k_norm, 1)

    def dve_produce(dve, t, odd):
        if is_step(t, -1):
            dve.wait_ge(gain_x_in, 16)
            dve_stream_norm(dve, 0)
            dve_produce_weights(dve, range(0, 2))
        if is_step(t, 0):
            dve_produce_weights(dve, range(4, 7))
        if has(t - 2):
            link, _ = linker(dve, a_own_q, 5 * t - 10)
            dve.wait_ge(a_q_sq, t - 1)
            dve.reduce_sum(cols(MS_Q, H), q_sq[:, :, :], AX.X).then_inc(a_q_summed, 1)
            dve.wait_ge(a_root_q, t - 1)
            wait(dve, a_q_scaled, t - 1)
            dve_rstd(dve, link, cols(R_Q, H), cols(MS_Q, H), cols(ROOT_Q, H), cols(TMP, H))
            dve.tensor_copy(cols(R_Q2, H), cols(R_Q, H)).then_inc(a_q_factor, 1)
        if has(t):
            if is_step(t, 0):
                dve.wait_ge(gain_c_in, 48)
            link, _ = linker(dve, a_own_c, 6 * t)
            dve.wait_ge(a_root_c, t + 1)
            dve_rstd(dve, link, cols(R_C, 2), cols(MS_C, 2), cols(ROOT_C, 2), cols(TMP, 2))
            lat = psum[:, 2 * N:2 * N + DOWN]
            link(dve.tensor_tensor(c_sb[:, CQ + CKV:], lat[:, CQ + CKV:], g_k[:, NOPE:], ALU.mult))
            dve.scalar_tensor_tensor(c_sb[:, 0:CQ], lat[:, 0:CQ], cols(R_C), g_c[:, 0:CQ], ALU.mult, ALU.mult)
            dve.scalar_tensor_tensor(c_sb[:, CQ:CQ + CKV], lat[:, CQ:CQ + CKV], cols(R_C + 1), g_c[:, CQ:],
                                     ALU.mult, ALU.mult).then_inc(a_c, 1)
        if has(t + 1):
            for b in range(2):
                dve.wait_ge(a_hx_hi, 2 * t + 2 + b + 1)
                dve.tensor_tensor(hx_lo[:, 4 * b:4 * b + 4, :], bank(b).rearrange("p (k q) -> p k q", k=4),
                                  f32(hx_hi[:, 4 * b:4 * b + 4, :]), ALU.subtract).then_inc(a_hx_lo, 1)
        if is_step(t, -1):
            dve_produce_weights(dve, range(2, 4))
        if is_step(t, 0):
            dve_produce_weights(dve, range(7, 9))
        if has(t + 2):
            dve_stream_norm(dve, t + 2)
        if is_step(t, 0):
            dve.wait_ge(posk_in, 16)
            dve.tensor_copy(posk[:, :], posk_i[:, :]).then_inc(posk_in, 1)
        if has(t - 1):
            i = 1 - odd
            link, _ = linker(dve, a_own_k, 7 * t - 7)
            dve.wait_ge(a_k_sq, t)
            link(dve.reduce_sum(cols(SS_K, H), k_sq[:, :, :], AX.X))
            dve.tensor_scalar(cols(MS_K, H), cols(SS_K, H), cols(MS_SHARED), None, ALU.add).then_inc(a_k_summed, 1)
            dve.wait_ge(a_root_k, t)
            dve_rstd(dve, link, cols(R_K, H), cols(MS_K, H), cols(ROOT_K, H), cols(TMP, H))
            if is_step(t, NT):
                dve.tensor_scalar(rk[:, NT - 1, 0:NOPE], ks[i][:, 0, 0:NOPE], cols(R_K), None, ALU.mult)
                dve.tensor_scalar(rk[:, NT - 1, NOPE:QK], rotk[:, :], cols(R_K), None, ALU.mult)
                dve.tensor_scalar(rk[:, NT - 1, QK:], rotk[:, :], cols(R_K), None, ALU.mult).then_inc(k_row_done, 1)
                dve.wait_ge(k_row_done, 1)
        if has(t):
            dve.wait_ge(a_ct_hi, t + 1)
            dve.tensor_tensor(ct_lo[:, :, :], psum[:, 3 * N:3 * N + NC * P].rearrange("p (k q) -> p k q", k=NC),
                              f32(ct_hi[:, :, :]), ALU.subtract).then_inc(a_ct_lo, 1)
        if has(t - 1) and not is_step(t, NT):
            dve_scale_keys(dve, ks[1 - odd], link)
        if is_step(t, NT + 1):
            link, _ = linker(dve, a_own_k, 7 * NT - 1)
            dve_scale_keys(dve, ks[odd], link)
        if has(t):
            link, _ = linker(dve, a_own_r, 3 * t)
            one, two = c_sb[:, CQ + CKV:CQ + CKV + HALF], c_sb[:, CQ + CKV + HALF:]
            if is_step(t, 0):
                dve.wait_ge(a_rope, 2)
                dve.wait_ge(posk_in, 17)
            dve.tensor_tensor(tmp_r[:, 0:HALF], two, at(sin, t), ALU.mult)
            dve.tensor_tensor(tmp_r[:, HALF:], one, at(sin, t), ALU.mult)
            dve.tensor_tensor(rotk[:, 0:HALF], one, at(cos, t), ALU.mult)
            link(dve.tensor_tensor(rotk[:, HALF:], two, at(cos, t), ALU.mult))
            dve.tensor_tensor(rotk[:, 0:HALF], rotk[:, 0:HALF], tmp_r[:, 0:HALF], ALU.subtract)
            link(dve.tensor_tensor(rotk[:, HALF:], rotk[:, HALF:], tmp_r[:, HALF:], ALU.add))
            link(dve.tensor_copy(cols(MS_SHARED), cols(MS_KR)))
            dve.tensor_scalar(at(mask, t), posk[:, :], posq[:, bass.ds(t, 1)], -FAR, ALU.is_gt, ALU.mult).then_inc(a_k_shared, 1)

    def pool_setup(pool):
        pool.memset(ident[:, :], 0.0).then_inc(ident_done, 1)
        pool.wait_ge(ident_done, 1)
        pool.affine_select(out=ident[:, :], in_=ident[:, :], compare_op=ALU.not_equal, fill=1.0, base=0,
                           pattern=[[-1, P]], channel_multiplier=1).then_inc(ident_done, 1)
        for i, (s, n) in enumerate(((u_free, 4), (d_free, 4), (square_done, 2), (a_q_scaled, 1),
                                   *((s, 16) for s in (*a_stored_q, *a_stored_k, *a_stored_v)))):
            pool.memset(cols(SPARE[i]), 0.0).then_inc(s, n)
        pool.memset(cols(EPS_C), EPS).then_inc(eps_set, 1)
        pool_loads(pool)

    def pool_tables(pool):
        pool.wait_ge(consts, CONSTS)
        pool.wait_ge(a_rope, 2)
        g = [g_q[:, a:a + HALF].unsqueeze(1).to_broadcast([P, NT, HALF]) for a in (NOPE, NOPE + HALF)]
        pool.tensor_tensor(cos_1[:, :, :], cos[:, :, :], g[0], ALU.mult)
        pool.tensor_tensor(sin_1[:, :, :], sin[:, :, :], g[0], ALU.mult)
        pool.tensor_tensor(cos_2[:, :, :], cos[:, :, :], g[1], ALU.mult)
        pool.tensor_tensor(sin_2[:, :, :], sin[:, :, :], g[1], ALU.mult).then_inc(tables, 1)
        pool.wait_ge(tables, 1)

    def pool_turn_queries(pool, link, tile, q, h0, h1, scaled, count, turned):
        q, n = q[:, h0:h1, :], h1 - h0
        pool.tensor_tensor(q, q, cols(R_Q2 + h0, n).unsqueeze(2).to_broadcast([P, n, QK]), ALU.mult).then_inc(scaled, 1)
        pool.wait_ge(scaled, count)
        pool.wait_ge(tables, 1)
        one, two = q[:, :, NOPE:NOPE + HALF], q[:, :, NOPE + HALF:]

        def table(ap):
            return at(ap, tile).unsqueeze(1).to_broadcast([P, n, HALF])
        pool.tensor_tensor(ra[:, 0:n, :], one, table(cos_1), ALU.mult)
        pool.tensor_tensor(rb[:, 0:n, :], two, table(sin_2), ALU.mult)
        pool.tensor_tensor(rc[:, 0:n, :], two, table(cos_2), ALU.mult)
        link(pool.tensor_tensor(rd[:, 0:n, :], one, table(sin_1), ALU.mult))
        link(pool.tensor_tensor(one, ra[:, 0:n, :], rb[:, 0:n, :], ALU.subtract))
        pool.tensor_tensor(two, rc[:, 0:n, :], rd[:, 0:n, :], ALU.add).then_inc(turned, 1)

    def pool_produce(pool, t, odd):
        if is_step(t, -1):
            pool_tables(pool)
        if not has(t - 2):
            return
        pool.wait_ge(a_q_factor, t - 1)
        if is_step(t, NT + 1):
            link, _ = linker(pool, q_row_own, 1)
            pool_turn_queries(pool, link, t - 2, qs[odd], 0, 1, q_row_own, 1, q_row_own)
            pool.wait_ge(q_row_own, 4)
            pool.tensor_copy(rq[:, NT - 1, 0:QK], qs[odd][:, 0, :])
            pool.tensor_copy(rq[:, NT - 1, QK:], qs[odd][:, 0, NOPE:]).then_inc(q_row_done, 1)
        link, _ = linker(pool, a_pool_own, 2 * t - 4)
        pool_turn_queries(pool, link, t - 2, qs[odd], 1 if is_step(t, NT + 1) else 0, H, a_q_scaled, t, a_q_rot)

    q_in, v_in = sem("q_in"), sem("v_in")
    late_rows_in = sem("late_rows_in")
    s_done, s_max, e_done = sem("s_done"), sem("s_max"), sem("e_done")
    t_done, t_hi, t_free = sem("t_done"), sem("t_hi"), sem("t_free")
    vh_done, vl_done = sem("vh_done"), sem("vl_done")
    r_inv = sem("r_inv")
    pv_done, o_done, oh_done, ol_done = sem("pv_done"), sem("o_done"), sem("oh_done"), sem("ol_done")
    b_own = sem("b_own")
    PREP = 8
    TG = {0: 0, 1: 2, 2: 4, 3: 6, "Q0": 8, "K": 10, "Q1": 14, "S0": 16, 4: 17, 5: 19, 6: 21, 7: 23, "S1": 25}
    TG_LAST = {0: 0, 1: 2, 2: 4, 3: 6, "S0": 8, 4: 9, 5: 11, 6: 13, 7: 15, "S1": 17}
    T_HEAD = 26
    T_ALL = PREP + T_HEAD * (H - 1) + 18

    FIRST_KEYS, LAST_KEYS = (0, 2), (1, 3)
    MAX, BIAS, SUM, INV = 0, 8, 16, 32

    def sp_rows(sp, dst, src, h, t0, t1, into):
        rows = src[:, bass.ds(h, 1), :].rearrange("(t p) a n -> p t (a n)", p=P)[:, t0:t1, :]
        sp.dma_start(dst[:, t0:t1, 0:QK], rows).then_inc(into, 16)
        sp.dma_start(dst[:, t0:t1, QK:], rows[:, :, NOPE:]).then_inc(into, 16)

    def sp_head_qk(sp, h):
        sp_rows(sp, rq, qd, h, 0, NT, q_in)
        sp_rows(sp, rk, kd, h, 0, NT, q_in)

    def sp_head_v(sp, h):
        sp.dma_start(rv[:, :, :], vd[:, bass.ds(h, 1), :].rearrange("(t p) a n -> p t (a n)", p=P)).then_inc(v_in, 16)

    def sp_attention(sp):
        all_stored(sp, a_stored_v, NT)
        sp.wait_ge(a_xn, NT)
        sp_head_v(sp, 0)
        all_stored(sp, a_stored_k, NT)
        all_stored(sp, a_stored_q, NT)
        sp.wait_ge(t_done, PREP)
        sp_head_qk(sp, 1)
        with sp.Fori(2, H) as h:
            sp.wait_ge(vl_done, h - 1)
            sp_head_v(sp, h - 1)
            sp.wait_ge(t_done, (h - 2) * T_HEAD + PREP + TG["Q1"] + 2)
            sp_head_qk(sp, h)
        sp.wait_ge(vl_done, H - 1)
        sp_head_v(sp, H - 1)
        sp.wait_ge(t_done, PREP + T_HEAD * (H - 2) + TG["Q1"] + 2)
        for j in range(RAW):
            load_unit(sp, O_BASE + j, 0, o_unit(j))

    def blocks(group, j):
        if group == "K":
            a, b = (0, NOPE) if j < 2 else (NOPE, 256)
            return [rk[:, 4 * (j % 2) + i, a:b] for i in range(4)]
        if group in ("Q0", "Q1"):
            half = int(group[1])
            a, b = (0, NOPE) if j == 0 else (NOPE, 256)
            return [rq[:, 4 * half + i, a:b] for i in range(4)]
        return [pr[:, group % 4, (4 * j + i) * P:(4 * j + i + 1) * P] for i in range(4)]

    def dests(group, j):
        if group == "K":
            c = slice(N * (j % 2), N * (j % 2) + N)
            return (k_hi[:, c], k_lo[:, c]) if j < 2 else (kr_hi[:, c], kr_lo[:, c])
        if group in ("Q0", "Q1"):
            c = slice(N * int(group[1]), N * int(group[1]) + N)
            return (q_hi[:, c], q_lo[:, c]) if j == 0 else (q_rope[:, c], None)
        c = slice(P * (group % 4), P * (group % 4) + P)
        return pt_hi[:, 4 * j:4 * j + 4, c], pt_lo[:, 4 * j:4 * j + 4, c]

    def groups_of(group):
        return 4 if group == "K" else 2

    def t_view(b, dst):
        return bank(b).rearrange("p (k q) -> p k q", k=4) if len(dst.shape) == 3 else bank(b)

    def gain_of(group, j):
        if group == "K" and j < 2:
            return gain_col[:, 1:2]
        return gain_col[:, 0:1] if group in ("Q0", "Q1") and j == 0 else None

    def t_bank(n):
        return (4, 5, 7)[n % 3]

    def t_wait(pe, base, n):
        wait(pe, t_free, base + n - (1 if n < 2 else 2))

    def pe_turn(pe, group, base, at0, js=None):
        for n, j in enumerate(js or range(groups_of(group))):
            t_wait(pe, base, at0 + n)
            b = t_bank(at0 + n)
            for i, src in enumerate(blocks(group, j)):
                last = pe.transpose(psum[:, b * N + i * P:b * N + (i + 1) * P], src, ident[:, :])
            last.then_inc(t_done, 1)

    def act_turned(act, group, base, at0, js=None):
        for n, j in enumerate(js or range(groups_of(group))):
            hi, _ = dests(group, j)
            g = gain_of(group, j)
            act.wait_ge(t_done, base + at0 + n + 1)
            act.activation(hi, t_view(t_bank(at0 + n), hi), ACT.Copy, scale=1.0 if g is None else g).then_inc(t_hi, 1)

    def dve_turned(dve, group, base, at0, js=None):
        for n, j in enumerate(js or range(groups_of(group))):
            hi, lo = dests(group, j)
            g = gain_of(group, j)
            src = t_bank(at0 + n)
            dve.wait_ge(t_hi, base + at0 + n + 1)
            if lo is None:
                rows = slice(ROPE, P)
                dve.tensor_tensor(hi[rows, :], bank(src)[rows, :], f32(hi[rows, :]), ALU.subtract).then_inc(t_free, 1)
            elif g is None:
                dve.tensor_tensor(lo, t_view(src, hi), f32(hi), ALU.subtract).then_inc(t_free, 1)
            else:
                dve.scalar_tensor_tensor(lo, bank(src), g, f32(hi), ALU.mult, ALU.subtract).then_inc(t_free, 1)

    def pe_scores(pe, j, ready):
        if ready is not None:
            pe.wait_ge(t_free, ready)
        c = slice(P * j, P * j + P)
        for half in range(2):
            m = slice(N * half, N * half + N)
            dst = bank(2 * (j % 2) + half)
            pe.matmul(dst, q_hi[:, c], k_hi[:, m], start=True, stop=False)
            pe.matmul(dst, q_hi[:, c], k_lo[:, m], start=False, stop=False)
            pe.matmul(dst, q_lo[:, c], k_hi[:, m], start=False, stop=False)
            pe.matmul(dst, q_rope[:, c], kr_hi[:, m], start=False, stop=False)
            last = pe.matmul(dst, q_rope[:, c], kr_lo[:, m], start=False, stop=True)
        last.then_inc(s_done, 1)

    def pe_values(pe, h, half, base, tg):
        n = tg["S0" if half == 0 else "S1"]
        t_wait(pe, base, n)
        pe.wait_ge(r_inv, 2 * h + half + 1)
        for i in range(4):
            b = t_bank(n) * N + i * P
            last = pe.transpose(psum[:, b:b + P], cols(INV + 4 * half + i).to_broadcast([P, P]), ident[:, :])
        last.then_inc(t_done, 1)
        pe.wait_ge(t_free, base + tg[4 * half + 3] + 2)
        if half == 0:
            pe.wait_ge(vl_done, h + 1)
        passes(pe, bank(6), [(v_hi[:, k, :], v_lo[:, k, :], pt_hi[:, k, :], pt_lo[:, k, :])
                             for k in range(NT)]).then_inc(pv_done, 1)

    def pe_attention_head(pe, h, last):
        t0, tg = PREP + T_HEAD * h, TG_LAST if last else TG
        for j in range(2, NT):
            pe.wait_ge(s_max, NT * h + j - 1)
            pe_scores(pe, j, None)
            if j < 6:
                pe.wait_ge(e_done, NT * h + j - 1)
                pe_turn(pe, j - 2, t0, tg[j - 2])
            if j == 6 and not last:
                pe.wait_ge(q_in, 64 * h + 128)
                pe_turn(pe, "Q0", t0, tg["Q0"])
        if not last:
            pe_turn(pe, "K", t0, tg["K"])
            pe_turn(pe, "Q1", t0, tg["Q1"])
        pe_values(pe, h, 0, t0, tg)
        for j in range(4, NT):
            pe.wait_ge(e_done, NT * h + j + 1)
            pe_turn(pe, j, t0, tg[j])
            if not last and j in (4, 7):
                pe.wait_ge(s_max, NT * h + 7 + j // 7)
                pe_scores(pe, j // 7, t0 + tg["Q1"] + 2 if j == 4 else None)
        pe_values(pe, h, 1, t0, tg)

    def pe_attention(pe):
        pe.wait_ge(a_kv_out, 4 * NT)
        pe.wait_ge(a_q_out, 3 * NT)
        pe.wait_ge(q_in, 64)
        pe_turn(pe, "K", 0, 0, FIRST_KEYS)
        pe_turn(pe, "Q0", 0, 2)
        pe.wait_ge(k_row_done, 1)
        pe_turn(pe, "K", 0, 4, LAST_KEYS)
        pe_scores(pe, 0, 6)
        pe_scores(pe, 1, None)
        pe.wait_ge(late_rows_in, 32)
        pe.wait_ge(q_row_done, 1)
        pe_turn(pe, "Q1", 0, 6)
        with pe.Fori(0, H - 1) as h:
            pe_attention_head(pe, h, False)
        pe_attention_head(pe, H - 1, True)

    def act_exp(act, h, j):
        act.wait_ge(s_max, NT * h + j + 1)
        act.activation(pr[:, j % 4, :], pr[:, j % 4, :], ACT.Exp, bias=cols(BIAS + j), scale=SCALE,
                       accum_out=cols(SUM + j)).then_inc(e_done, 1)

    def act_sums(act, half, base, tg):
        n = tg["S0" if half == 0 else "S1"]
        act.wait_ge(t_done, base + n + 1)
        act.activation(rsb[:, 0:N // 2], bank(t_bank(n))[:, 0:N // 2], ACT.Copy).then_inc(t_hi, 1)

    def act_out(act, h, half):
        act.wait_ge(o_done, 2 * h + half + 1)
        act.activation(h_hi[:, bass.ds(h, 1), N * half:N * half + N].rearrange("p a n -> p (a n)"), osc[:, :],
                       ACT.Copy).then_inc(oh_done, 1)

    def act_attention_head(act, h, last):
        t0, tg = PREP + T_HEAD * h, TG_LAST if last else TG
        for j in range(2, NT):
            if j < 6:
                act_turned(act, j - 2, t0, tg[j - 2])
            if j == 2:
                act.wait_ge(v_in, 16 * h + 16)
                act.activation(v_hi[:, :, :], rv[:, :, :], ACT.Copy).then_inc(vh_done, 1)
            if j == 6 and not last:
                act_turned(act, "Q0", t0, tg["Q0"])
            if j < 6:
                act_exp(act, h, j)
        if not last:
            act_turned(act, "K", t0, tg["K"])
            act_turned(act, "Q1", t0, tg["Q1"])
        act_exp(act, h, 6)
        act_exp(act, h, 7)
        act_sums(act, 0, t0, tg)
        if last:
            act.wait_ge(s_done, NT * H)
            for i in range(4):
                split_hi(act, O_BASE + i, 0, d_hi[:, i, :])
        for j in range(4, NT):
            act_turned(act, j, t0, tg[j])
            if j == 4:
                act_out(act, h, 0)
        act_sums(act, 1, t0, tg)
        if not last:
            act_exp(act, h + 1, 0)
            act_exp(act, h + 1, 1)
        act_out(act, h, 1)

    def act_attention(act):
        act_turned(act, "K", 0, 0, FIRST_KEYS)
        act_turned(act, "Q0", 0, 2)
        act_turned(act, "K", 0, 4, LAST_KEYS)
        act_exp(act, 0, 0)
        act_exp(act, 0, 1)
        act_turned(act, "Q1", 0, 6)
        with act.Fori(0, H - 1) as h:
            act_attention_head(act, h, False)
        act_attention_head(act, H - 1, True)

    def dve_max(dve, h, j, turned):
        i = NT * h + j
        dve.wait_ge(s_done, i + 1)
        if turned is not None:
            dve.wait_ge(t_done, turned)
        dve.memset(cols(40 + j), 0.0).then_inc(b_own, 1)
        dve.tensor_tensor_reduce(out=pr[:, j % 4, :], in0=bank(2 * (j % 2), 2), in1=mask[:, j, :], scale=1.0,
                                 scalar=-3.0e38, op0=ALU.add, op1=ALU.max, accum_out=cols(MAX + j)).then_inc(b_own, 1)
        dve.wait_ge(b_own, 2 * i + 2)
        dve.tensor_scalar(cols(BIAS + j), cols(MAX + j), -SCALE, None, ALU.mult).then_inc(s_max, 1)

    def dve_row_sums(dve, h, half):
        dve.wait_ge(e_done, NT * h + 4 * half + 4)
        dve.reciprocal(cols(INV + 4 * half, 4), cols(SUM + 4 * half, 4)).then_inc(r_inv, 1)

    def dve_sums(dve, half, base, tg):
        n = tg["S0" if half == 0 else "S1"]
        dve.wait_ge(t_hi, base + n + 1)
        dve.tensor_copy(rsb[:, N // 2:], bank(t_bank(n))[:, N // 2:]).then_inc(t_free, 1)

    def dve_out(dve, h, half, base, tg):
        dve.wait_ge(pv_done, 2 * h + half + 1)
        dve.wait_ge(t_free, base + tg["S0" if half == 0 else "S1"] + 1)
        if half == 1:
            dve.wait_ge(ol_done, 2 * h + 1)
        dve.tensor_tensor(osc[:, :], bank(6), rsb[:, :], ALU.mult).then_inc(o_done, 1)

    def dve_out_lo(dve, h, half):
        col = slice(N * half, N * half + N)
        dve.wait_ge(oh_done, 2 * h + half + 1)
        dve.tensor_tensor(h_lo[:, bass.ds(h, 1), col].rearrange("p a n -> p (a n)"), osc[:, :],
                          f32(h_hi[:, bass.ds(h, 1), col].rearrange("p a n -> p (a n)")), ALU.subtract).then_inc(ol_done, 1)

    def dve_attention_head(dve, h, last):
        t0, tg = PREP + T_HEAD * h, TG_LAST if last else TG
        for j in range(2, NT):
            if j == 6 and not last:
                dve_turned(dve, "Q0", t0, tg["Q0"])
            if j < 6:
                dve_max(dve, h, j, t0 if j < 4 else t0 + tg[j - 4] + 2)
                dve_turned(dve, j - 2, t0, tg[j - 2])
            if j == 6:
                dve_row_sums(dve, h, 0)
            if j == 2:
                dve.wait_ge(vh_done, h + 1)
                dve.tensor_tensor(v_lo[:, :, :], rv[:, :, :], f32(v_hi[:, :, :]), ALU.subtract).then_inc(vl_done, 1)
        if not last:
            dve_turned(dve, "K", t0, tg["K"])
            dve_turned(dve, "Q1", t0, tg["Q1"])
        dve_max(dve, h, 6, t0 + tg[2] + 2)
        dve_max(dve, h, 7, t0 + tg[3] + 2)
        dve_sums(dve, 0, t0, tg)
        if last:
            for i in range(4):
                split_lo(dve, O_BASE + i, 0, d_lo[:, i, :], d_hi[:, i, :])
        dve_out(dve, h, 0, t0, tg)
        for j in range(4, NT):
            dve_turned(dve, j, t0, tg[j])
            if j == 4:
                dve_row_sums(dve, h, 1)
        dve_sums(dve, 1, t0, tg)
        if not last:
            dve_max(dve, h + 1, 0, t0 + tg[4] + 2)
            dve_max(dve, h + 1, 1, t0 + tg[5] + 2)
        dve_out_lo(dve, h, 0)
        dve_out(dve, h, 1, t0, tg)
        dve_out_lo(dve, h, 1)

    def dve_attention(dve):
        dve_turned(dve, "K", 0, 0, FIRST_KEYS)
        dve_turned(dve, "Q0", 0, 2)
        dve_turned(dve, "K", 0, 4, LAST_KEYS)
        dve_max(dve, 0, 0, None)
        dve_max(dve, 0, 1, None)
        dve_turned(dve, "Q1", 0, 6)
        with dve.Fori(0, H - 1) as h:
            dve_attention_head(dve, h, False)
        dve_attention_head(dve, H - 1, True)

    u_done, u_free = sem("u_done"), sem("u_free")
    d_done, d_free = sem("d_done"), sem("d_free")
    square_done = sem("square_done")
    m_hi_done, m_lo_done = sem("m_hi_done"), sem("m_lo_done")
    x_in = [sem(f"x_in{t}") for t in range(NT)]
    gain_in = sem("gain_in")
    n_ss, n_root, n_own, n_xn, n_hi = sem("n_ss"), sem("n_root"), sem("n_own"), sem("n_xn"), sem("n_hi")
    c_own = sem("c_own")
    stored = sem("stored")

    def o_unit(j):
        return ins["attn_w_o"][0, P * j:P * j + P, :]

    def w1_unit(layer, j):
        return ins["mlp_w1"][layer, :, bass.ds(j * P, P)].rearrange("(k p) n -> p k n", p=P)

    def w2_unit(layer, j):
        return ins["mlp_w2"][layer, bass.ds(j * P, P), :]

    PARTS = (1, 2, 0)

    def in_unit(tile, part):
        return ins["conv_w_in"][0, :, bass.ds(PARTS[part] * D + tile * P, P)].rearrange("(k p) n -> p k n", p=P)

    def out_unit(j):
        return ins["conv_w_out"][0, bass.ds(j * P, P), :]

    MLP_CHUNKS = FF // N
    D_O = 0
    D_M1 = D_O + 16 + 32
    D_C = D_M1 + 16 * (MLP_CHUNKS - 1) + 32
    D_M2 = D_C + 16 + 32
    M1 = dict(unit=M1_BASE, down=D_M1, up=0, inner=0, square=0, norm=1, layer=0, first_ready=-1)
    C = dict(unit=C_BASE, down=D_C, up=64, inner=64, norm=2, first_ready=-2)
    M2 = dict(unit=M2_BASE, down=D_M2, up=64 + 48, inner=64 + 16, square=64, norm=3, layer=1, first_ready=-1)

    def order(hook):
        seq = []
        for t in range(NT):
            seq += [("D", t, 0), ("D", t, 1)]
            if hook and t:
                seq += [("T", t - 1, 0), ("T", t - 1, 1)]
        return seq + ([("T", NT - 1, 0), ("T", NT - 1, 1)] if hook else [])

    PLAIN = [("D", t, dh) for t in range(NT) for dh in range(2)]

    def pe_down(pe, base, seq, norm, stationary, moving, ready=None, first_group=0, then=None):
        for g, (kind, t, dh) in enumerate(seq, first_group):
            pe.wait_ge(d_free, base + g + 1)
            dst = bank(4 + g % 4)
            if kind == "D":
                if ready is not None and dh == 0 and t in (0, 4):
                    pe.wait_ge(m_lo_done, ready + 7 + t // 4)
                last = passes(pe, dst, [(*stationary(j, slice(P * t, P * t + P)), *moving(j, slice(N * dh, N * dh + N)))
                                        for j in range(4)])
            else:
                if then is not None and t == NT - 1 and dh == 0:
                    pe_up_first(pe, then)
                pe.wait_ge(n_xn, NT * norm + t + 1)
                for k in range(4):
                    last = pe.transpose(dst[:, k * P:(k + 1) * P], scr[:, t % 2, (4 * dh + k) * P:(4 * dh + k + 1) * P],
                                        ident[:, :])
            last.then_inc(d_done, 1)

    def dve_norm(dve, norm, t):
        i = NT * norm + t
        dve.wait_ge(n_root, i + 1)
        link, _ = linker(dve, n_own, 5 * i)
        dve_rstd(dve, link, cols(R_N), cols(MS_N + t % 2), cols(ROOT_N + t % 2), cols(TMP_N))
        if t == 0:
            dve.wait_ge(gain_in, 16 * norm + 16)
        dve.scalar_tensor_tensor(scr[:, t % 2, :], x[:, t, :], cols(R_N), gain[:, 0:D], ALU.mult, ALU.mult).then_inc(n_xn, 1)

    def dve_down(dve, base, seq, norm):
        for g, (kind, t, dh) in enumerate(seq):
            src = bank(4 + g % 4)
            if kind == "D":
                dst = x[:, t, N * dh:N * dh + N]
                dve.wait_ge(d_done, base + g + 1)
                if norm == 0 and dh == 0:
                    dve.wait_ge(x_in[t], 16)
                dve.tensor_tensor(dst, src, dst, ALU.add).then_inc(d_free, 1)
                if len(seq) > 16 and dh == 0 and t:
                    dve_norm(dve, norm, t - 1)
            else:
                if t == NT - 1 and dh == 0:
                    dve_norm(dve, norm, t)
                i = 2 * (NT * norm + t) + dh
                tok = slice(P * t, P * t + P)
                dve.wait_ge(n_hi, i + 1)
                dve.tensor_tensor(h_lo[:, 4 * dh:4 * dh + 4, tok], src.rearrange("p (k q) -> p k q", k=4),
                                  f32(h_hi[:, 4 * dh:4 * dh + 4, tok]), ALU.subtract).then_inc(d_free, 1)

    def act_down(act, base, seq, norm):
        for g, (kind, t, dh) in enumerate(seq):
            if kind == "D" and dh == 1:
                act.wait_ge(d_free, 4 + base + g + 1)
                act.activation(scr[:, t % 2, :], x[:, t, :], ACT.Square, scale=float(D) ** -0.5,
                               accum_out=cols(MS_N + t % 2)).then_inc(n_ss, 1)
                act.wait_ge(n_ss, NT * norm + t + 1)
                act.activation(cols(ROOT_N + t % 2), cols(MS_N + t % 2), ACT.Sqrt, bias=cols(EPS_C)).then_inc(n_root, 1)
            if kind == "T":
                act.wait_ge(d_done, base + g + 1)
                act.activation(h_hi[:, 4 * dh:4 * dh + 4, P * t:P * t + P],
                               bank(4 + g % 4).rearrange("p (k q) -> p k q", k=4), ACT.Copy).then_inc(n_hi, 1)

    def inner(j, tok):
        return m_hi[:, j, tok], m_lo[:, j, tok]

    def down_weights(j, feat):
        return d_hi[:, j, feat], d_lo[:, j, feat]

    def sp_out_proj(sp):
        sp.wait_ge(vl_done, H)
        for t in range(3):
            sp.dma_start(x[:, t, :], x_rows[:, t, :]).then_inc(x_in[t], 16)
        for j in range(4, 8):
            load_unit(sp, O_BASE + j, 0, o_unit(j))
        sp.wait_ge(ol_done, 2 * H)
        for t in range(3, NT):
            sp.dma_start(x[:, t, :], x_rows[:, t, :]).then_inc(x_in[t], 16)
        for j in range(2):
            load_unit(sp, O_BASE + 8 + j, 0, w1_unit(0, j))

    def pe_out_proj(pe):
        pe.wait_ge(t_free, T_ALL)
        pe.wait_ge(w_lo_done, O_BASE + 4)
        first_heads = lambda j, tok: (h_hi[:, j, tok], h_lo[:, j, tok])
        pe_down(pe, D_O, PLAIN[:2], 0, first_heads, down_weights)
        pe.wait_ge(o_done, 2 * H)
        pe_down(pe, D_O, PLAIN[2:], 0, first_heads, down_weights, first_group=2)
        pe.wait_ge(ol_done, 2 * H)
        pe.wait_ge(w_lo_done, O_BASE + 8)
        pe_down(pe, D_O + 16, order(True), 0, lambda j, tok: (h_hi[:, 4 + j, tok], h_lo[:, 4 + j, tok]),
                lambda j, feat: (o_hi[:, j, feat], o_lo[:, j, feat]), then=M1)

    def act_out_proj(act):
        act.wait_ge(pv_done, 2 * H)
        for j in range(4):
            split_hi(act, O_BASE + 4 + j, 0, o_hi[:, j, :])
        for j in range(2):
            split_hi(act, O_BASE + 8 + j, 0, u_hi[:, j, :].rearrange("p (k n) -> p k n", k=ND))
        act_down(act, D_O + 16, order(True), 0)

    def dve_out_proj(dve):
        for j in range(4):
            split_lo(dve, O_BASE + 4 + j, 0, o_lo[:, j, :], o_hi[:, j, :])
        dve_down(dve, D_O, PLAIN, 0)
        for j in range(2):
            split_lo(dve, O_BASE + 8 + j, 0, u_lo[:, j, :].rearrange("p (k n) -> p k n", k=ND),
                     u_hi[:, j, :].rearrange("p (k n) -> p k n", k=ND))
        dve_down(dve, D_O + 16, order(True), 0)

    def u_view(ap, slot):
        return ap[:, slot, :].rearrange("p (k n) -> p k n", k=ND)

    def pe_up_half(pe, slot, up, bank0, ready, half):
        pe.wait_ge(w_lo_done, ready)
        pe.wait_ge(u_free, up + half + 1)
        tok = slice(N * half, N * half + N)
        passes(pe, bank(bank0 + half), [(u_hi[:, slot, P * k:P * k + P], u_lo[:, slot, P * k:P * k + P],
                                         h_hi[:, k, tok], h_lo[:, k, tok]) for k in range(ND)]).then_inc(u_done, 1)

    def pe_up_unit(pe, *unit):
        for half in range(2):
            pe_up_half(pe, *unit, half)

    def pe_up_first(pe, st, more_up=0, more_units=0):
        pe_up_half(pe, 0, st["up"] + more_up, 0, st["unit"] + more_units + st["first_ready"], 0)

    def mlp_unit(g, last, final):
        if final and last and g in (5, 7):
            return None
        offset = 5 if final and last and g == 6 else g
        return (offset, "D", g // 2) if g % 2 == 0 else (offset, "U", (g - 1) // 2 + 2)

    def mlp_loop(e, chunk):
        with e.Fori(0, MLP_CHUNKS - 1) as c:
            chunk(c, False)
        chunk(MLP_CHUNKS - 1, True)

    def sp_mlp(sp, st, then):
        def chunk(c, last):
            for g in range(8):
                unit = mlp_unit(g, last, then is None)
                if unit:
                    offset, kind, j = unit
                    src = (w2_unit(st["layer"], 4 * c + j) if kind == "D" else then(j - 4) if last and j > 3
                           else w1_unit(st["layer"], 4 * c + j))
                    load_unit(sp, st["unit"] + offset, 8 * c, src)
        mlp_loop(sp, chunk)

    def pe_mlp(pe, st, final, then=None):
        pe.wait_ge(d_free, 4 + st["down"])
        def chunk(c, last):
            for u in range(4):
                unit = (u % 2, st["up"] + 8 * c + 2 * u, 2 * u % 4, st["unit"] + 8 * c + (-1, 0, 2, 4)[u])
                if u == 0:
                    pe_up_half(pe, *unit, 1)
                else:
                    pe_up_unit(pe, *unit)
            pe.wait_ge(w_lo_done, st["unit"] + 8 * c + (6 if final and last else 7))
            pe_down(pe, st["down"] + 16 * c, order(not final) if last else PLAIN, st["norm"], inner, down_weights,
                    st["inner"] + 8 * c, then=then if last else None)
            if not last:
                pe_up_first(pe, st, 8 * c + 8, 8 * c + 8)
        mlp_loop(pe, chunk)

    def act_mlp(act, st, final):
        def chunk(c, last):
            for g in range(8):
                up = st["up"] + 8 * c + g
                r = scr[:, 0, N * (g % 2):N * (g % 2) + N]
                act.wait_ge(u_done, up + 1)
                act.wait_ge(square_done, st["square"] + 8 * c + g + 1)
                act.activation(r, bank(g % 4), ACT.Relu).then_inc(u_free, 1)
                act.wait_ge(u_free, 4 + up + 1)
                act.activation(m_hi[:, g // 2, N * (g % 2):N * (g % 2) + N], r, ACT.Square).then_inc(m_hi_done, 1)
                unit = mlp_unit(g, last, final)
                if unit:
                    offset, kind, j = unit
                    split_hi(act, st["unit"] + offset, 8 * c, d_hi[:, j, :] if kind == "D" else u_view(u_hi, j % 2))
            if last and not final:
                act_down(act, st["down"] + 16 * c, order(True), st["norm"])
        mlp_loop(act, chunk)

    def dve_mlp(dve, st, final):
        def chunk(c, last):
            for g in range(8):
                span = slice(N * (g % 2), N * (g % 2) + N)
                square = scr[:, 1, span]
                dve.wait_ge(u_free, 4 + st["up"] + 8 * c + g + 1)
                dve.tensor_tensor(square, scr[:, 0, span], scr[:, 0, span], ALU.mult).then_inc(square_done, 1)
                dve.wait_ge(square_done, st["square"] + 8 * c + g + 3)
                dve.wait_ge(m_hi_done, st["inner"] + 8 * c + g + 1)
                dve.tensor_tensor(m_lo[:, g // 2, span], square, f32(m_hi[:, g // 2, span]), ALU.subtract).then_inc(m_lo_done, 1)
                unit = mlp_unit(g, last, final)
                if unit:
                    offset, kind, j = unit
                    hi, lo = (d_hi[:, j, :], d_lo[:, j, :]) if kind == "D" else (u_view(u_hi, j % 2), u_view(u_lo, j % 2))
                    split_lo(dve, st["unit"] + offset, 8 * c, lo, hi)
            dve_down(dve, st["down"] + 16 * c, order(not final) if last else PLAIN, st["norm"])
        mlp_loop(dve, chunk)

    def conv_pairs(e, pair, down):
        with e.Fori(0, 2) as r:
            pair(r, r, False)
        down(0)
        pair(2, 0, False)
        pair(3, 1, True)
        down(1)

    def d_slot(ap, r, i):
        return ap[:, bass.ds(2 * r + i // 3, 1), :].rearrange("p a n -> p (a n)")

    def sp_conv(sp, then):
        def pair(pp, r, last):
            for i in range(6):
                tile, part = (i + 2) // 3, (i + 2) % 3
                src = then(i - 4) if last and i > 3 else in_unit(2 * pp + tile, part)
                load_unit(sp, C["unit"] + i + i // 3, 8 * pp, src)
                if i % 3 == 2:
                    load_unit(sp, C["unit"] + i + i // 3 + 1, 8 * pp, out_unit(2 * pp + i // 3))
        for pp in range(4):
            pair(pp, pp % 2, pp == 3)

    def pe_conv(pe, then):
        pe.wait_ge(d_free, 4 + C["down"])

        def pair(pp, r, last):
            for i in range(6):
                ready = (-2, 0, 1, 2, 3, 5)[i]
                unit = (i % 2, C["up"] + 12 * pp + 2 * i, 2 * i % 4, C["unit"] + 8 * pp + ready)
                if i == 0:
                    pe_up_half(pe, *unit, 1)
                else:
                    pe_up_unit(pe, *unit)
            if not last:
                pe_up_first(pe, C, 12 * pp + 12, 8 * pp + 8)

        def down(c):
            pe.wait_ge(w_lo_done, C["unit"] + 16 * c + 16)
            pe_down(pe, C["down"] + 16 * c, order(True) if c else PLAIN, C["norm"], inner, down_weights,
                    C["inner"] + 8 * c, then=then if c else None)
        conv_pairs(pe, pair, down)

    def act_conv(act):
        def pair(pp, r, last):
            for i in range(6):
                if i % 3 == 2:
                    for half in range(2):
                        span = slice(N * half, N * half + N)
                        act.wait_ge(u_free, 4 + C["up"] + 12 * pp + 2 * i + half + 1)
                        act.activation(m_hi[:, bass.ds(2 * r + i // 3, 1), span].rearrange("p a n -> p (a n)"),
                                       scr[:, 1, span], ACT.Copy).then_inc(m_hi_done, 1)
                else:
                    act.wait_ge(u_done, C["up"] + 12 * pp + 2 * i + 2)
                split_hi(act, C["unit"] + i + i // 3, 8 * pp, u_view(u_hi, i % 2))
                if i % 3 == 2:
                    split_hi(act, C["unit"] + i + i // 3 + 1, 8 * pp, d_slot(d_hi, r, i))

        def down(c):
            if c:
                act_down(act, C["down"] + 16 * c, order(True), C["norm"])
        conv_pairs(act, pair, down)

    CONV_OWN = 6

    def dve_conv(dve):
        gate, conv, u = scr[:, 0, :], scr[:, 1, :], gain
        dve.memset(gain[:, 0:2], 0.0).then_inc(c_own, 1)

        def pair(pp, r, last):
            link, count = linker(dve, c_own, 1 + CONV_OWN * pp)
            for i in range(6):
                for half in range(2):
                    span = slice(N * half, N * half + N)
                    up = C["up"] + 12 * pp + 2 * i + half
                    src = bank((2 * i + half) % 4)
                    dve.wait_ge(u_done, up + 1)
                    if i % 3 == 0:
                        dve.tensor_copy(gate[:, span], src).then_inc(u_free, 1)
                    elif i % 3 == 1:
                        dve.wait_ge(u_free, 4 + up - 1)
                        dve.tensor_tensor(u[:, 2 + N * half:2 + N * half + N], src, gate[:, span], ALU.mult).then_inc(u_free, 1)
                    else:
                        dve.tensor_tensor(conv[:, span], src, conv[:, span], ALU.mult).then_inc(u_free, 1)
                        m = C["inner"] + 4 * pp + 2 * (i // 3) + half
                        dve.wait_ge(m_hi_done, m + 1)
                        j = bass.ds(2 * r + i // 3, 1)
                        dve.tensor_tensor(m_lo[:, j, span].rearrange("p a n -> p (a n)"), conv[:, span],
                                          f32(m_hi[:, j, span].rearrange("p a n -> p (a n)")), ALU.subtract).then_inc(m_lo_done, 1)
                if i % 3 == 1:
                    dve.wait_ge(u_free, 4 + C["up"] + 12 * pp + 2 * i + 2)
                    tap = [at(convw, w)[:, bass.ds(2 * pp + i // 3, 1)] for w in range(3)]
                    link(dve.tensor_scalar(conv, u[:, 2:2 + S], tap[2], None, ALU.mult))
                    link(dve.scalar_tensor_tensor(conv, u[:, 1:1 + S], tap[1], conv, ALU.mult, ALU.add))
                    link(dve.scalar_tensor_tensor(conv, u[:, 0:S], tap[0], conv, ALU.mult, ALU.add))
                split_lo(dve, C["unit"] + i + i // 3, 8 * pp, u_view(u_lo, i % 2), u_view(u_hi, i % 2))
                if i % 3 == 2:
                    split_lo(dve, C["unit"] + i + i // 3 + 1, 8 * pp, d_slot(d_lo, r, i), d_slot(d_hi, r, i))

        def down(c):
            dve_down(dve, C["down"] + 16 * c, order(True) if c else PLAIN, C["norm"])
        dve.wait_ge(c_own, 1)
        conv_pairs(dve, pair, down)

    with nc.Block() as block:
        @block.sync
        def _(sp):
            a_steps(sp, sp_produce)
            sp_attention(sp)
            sp_out_proj(sp)
            sp_mlp(sp, M1, lambda j: in_unit(0, j))
            sp_conv(sp, lambda j: w1_unit(1, j))
            sp_mlp(sp, M2, None)
            for t in range(NT):
                sp.wait_ge(d_free, 4 + M2["down"] + 16 * (MLP_CHUNKS - 1) + 2 * t + 2)
                sp.dma_start(out_rows[:, t, :], x[:, t, :]).then_inc(stored, 16)
            sp.wait_ge(stored, 16 * NT)

        @block.gpsimd
        def _(pool):
            pool_setup(pool)
            a_steps(pool, pool_produce)
            pool.wait_ge(a_xn, NT)
            pool.dma_start(gain[:, 0:D], spread(ins["g_mlp"][0, :])).then_inc(gain_in, 16)
            pool.wait_ge(n_xn, NT)
            pool.dma_start(gain[:, 0:D], spread(ins["g_mix"][1, :])).then_inc(gain_in, 16)
            pool.wait_ge(m_lo_done, C["inner"] + 16)
            pool.dma_start(gain[:, 0:D], spread(ins["g_mlp"][1, :])).then_inc(gain_in, 16)

        @block.scalar
        def _(act):
            a_steps(act, act_produce)
            act_attention(act)
            act_out_proj(act)
            act_mlp(act, M1, False)
            act_conv(act)
            act_mlp(act, M2, True)

        @block.vector
        def _(dve):
            a_steps(dve, dve_produce)
            dve_attention(dve)
            dve_out_proj(dve)
            dve_mlp(dve, M1, False)
            dve_conv(dve)
            dve_mlp(dve, M2, True)

        @block.tensor
        def _(pe):
            pe.wait_ge(ident_done, 2)
            a_steps(pe, pe_produce)
            pe_attention(pe)
            pe_out_proj(pe)
            pe_mlp(pe, M1, False, C)
            pe_conv(pe, M2)
            pe_mlp(pe, M2, True)


_INS = ["x", "positions", "g_mix", "g_mlp", "attn_w_down", "attn_g_q_a", "attn_g_kv_a", "attn_w_uq", "attn_w_ukv",
        "attn_g_qnorm", "attn_g_knorm", "attn_w_o", "conv_w_in", "conv_w", "conv_w_out", "mlp_w1", "mlp_w2"]


def kernel(**inputs):
    import concourse.bacc as bacc
    from concourse.bass_utils import run_bass_kernel_spmd

    nc = bacc.Bacc("TRN2", target_bir_lowering=False, num_devices=1)
    arrays = {n: np.ascontiguousarray(inputs[n]) for n in _INS}
    arrays["inv_freq"] = (10000.0 ** (-np.arange(0, ROPE, 2) / ROPE)).astype(np.float32)
    ins = {n: nc.dram_tensor("in_" + n, a.shape, mybir.dt.from_np(a.dtype), kind="ExternalInput").ap()
           for n, a in arrays.items()}
    out = nc.dram_tensor("out", [1, S, D], F32, kind="ExternalOutput").ap()
    build(nc, ins, out)
    result = run_bass_kernel_spmd(nc, [{"in_" + n: a for n, a in arrays.items()}], core_ids=[0])
    return result.results[0]["out"]
```
